# Optimizing a Trainium2 kernel written in Bass

```python
import jax, jax.numpy as jnp
from jax import lax
import numpy as np

D_MODEL = 1024
BATCH = 1
SEQ = 512
DEPTH = 2
DEC_BATCH = 8
DEC_SEQ = 8
PAST_LEN = 2048
PAGE_SIZE = 128

N_A = DEPTH // 2
N_B = DEPTH - N_A
CONV_WIDTH = 31
D_FF = 4 * D_MODEL
PLE_DIM = 256
N_HEADS = 8
QK_NOPE = 128
QK_ROPE = 64
V_HEAD = 128
KV_LORA = 512
Q_LORA = 768
ROPE_THETA = 10000.0
Q_BLOCK = 128
EPS = 1e-6
SM_SCALE = (QK_NOPE + QK_ROPE) ** -0.5

kernel_name = 'yoco_conformer_mla_decoder_step'

def rms_norm(x, g):
    xf = x.astype(jnp.float32)
    y = xf * lax.rsqrt(jnp.mean(xf * xf, axis=-1, keepdims=True) + EPS)
    return (y * g.astype(jnp.float32)).astype(x.dtype)

def layer_norm(x, g, b):
    xf = x.astype(jnp.float32)
    mu = jnp.mean(xf, axis=-1, keepdims=True)
    var = jnp.mean(jnp.square(xf - mu), axis=-1, keepdims=True)
    y = (xf - mu) * lax.rsqrt(var + EPS)
    return (y * g.astype(jnp.float32) + b.astype(jnp.float32)).astype(x.dtype)

def rope(x, pos):
    half = x.shape[-1] // 2
    freqs = 1.0 / (ROPE_THETA ** (jnp.arange(half, dtype=jnp.float32) / half))
    ang = pos.astype(jnp.float32)[:, None] * freqs[None, :]
    ang = ang.reshape(ang.shape[:1] + (1,) * (x.ndim - 3) + ang.shape[1:])
    cos, sin = jnp.cos(ang), jnp.sin(ang)
    xf = x.astype(jnp.float32)
    x1, x2 = xf[..., :half], xf[..., half:]
    return jnp.concatenate([x1 * cos - x2 * sin, x1 * sin + x2 * cos], axis=-1).astype(x.dtype)

def conformer_conv(h, conv_prev, w_pw1, w_dw, b_dw, ln_g, ln_b, w_pw2):
    a, gate = jnp.split(h @ w_pw1, 2, axis=-1)
    v = a * jax.nn.sigmoid(gate)
    full = jnp.concatenate([conv_prev.astype(v.dtype), v], axis=1)
    y = lax.conv_general_dilated(full, w_dw[:, None, :], window_strides=(1,), padding='VALID',
                                 dimension_numbers=('NWC', 'WIO', 'NWC'),
                                 feature_group_count=D_MODEL) + b_dw
    y = jax.nn.silu(layer_norm(y, ln_g, ln_b))
    return y @ w_pw2, full[:, -(CONV_WIDTH - 1):]

def sq_relu_mlp(h, w_up, w_down):
    return jnp.square(jax.nn.relu(h @ w_up)) @ w_down

def shared_kv(x, pos, kv_in_g, w_dkv, kv_norm_g):
    h = rms_norm(x, kv_in_g)
    ckr = h @ w_dkv
    c_kv = rms_norm(ckr[..., :KV_LORA], kv_norm_g)
    k_rope = rope(ckr[..., KV_LORA:], pos)
    return c_kv, k_rope

def mla_query(h, pos, w_dq, q_norm_g, w_uq, w_uk):
    B, T = h.shape[:2]
    cq = rms_norm(h @ w_dq, q_norm_g)
    q = (cq @ w_uq).reshape(B, T, N_HEADS, QK_NOPE + QK_ROPE)
    q_rope = rope(q[..., QK_NOPE:], pos)
    q_lat = jnp.einsum('bthn,chn->bthc', q[..., :QK_NOPE], w_uk)
    return q_lat, q_rope

def latent_scores(q_lat, q_rope, c, kr):
    s = jnp.einsum('bqhc,bkc->bhqk', q_lat, c, preferred_element_type=jnp.float32)
    s = s + jnp.einsum('bqhr,bkr->bhqk', q_rope, kr, preferred_element_type=jnp.float32)
    return s * SM_SCALE

def prompt_attention(q_lat, q_rope, c, kr, pos):
    B, T = q_lat.shape[:2]
    nb = T // Q_BLOCK

    def block(args):
        ql, qr, qp = args
        s = latent_scores(ql, qr, c, kr)
        s = jnp.where(pos[None, :] <= qp[:, None], s, -jnp.inf)
        p = jax.nn.softmax(s, axis=-1).astype(c.dtype)
        return jnp.einsum('bhqk,bkc->bqhc', p, c)

    ql = q_lat.reshape(B, nb, Q_BLOCK, N_HEADS, KV_LORA).swapaxes(0, 1)
    qr = q_rope.reshape(B, nb, Q_BLOCK, N_HEADS, QK_ROPE).swapaxes(0, 1)
    qp = pos.reshape(nb, Q_BLOCK)
    o = lax.map(block, (ql, qr, qp))
    return o.swapaxes(0, 1).reshape(B, T, N_HEADS, KV_LORA)

def sample_attention(q_lat, q_rope, past_c, past_kr, c, kr):
    T = q_lat.shape[1]
    P = past_c.shape[1]
    s_past = latent_scores(q_lat, q_rope, past_c, past_kr)
    s_new = latent_scores(q_lat, q_rope, c, kr)
    s_new = jnp.where(jnp.tril(jnp.ones((T, T), dtype=bool)), s_new, -jnp.inf)
    p = jax.nn.softmax(jnp.concatenate([s_past, s_new], axis=-1), axis=-1).astype(c.dtype)
    return (jnp.einsum('bhqk,bkc->bqhc', p[..., :P], past_c)
            + jnp.einsum('bhqk,bkc->bqhc', p[..., P:], c))

def mla_output(o_lat, w_uv, w_o):
    B, T = o_lat.shape[:2]
    o = jnp.einsum('bthc,chv->bthv', o_lat, w_uv).reshape(B, T, N_HEADS * V_HEAD)
    return o @ w_o

def run_group(x, ple, pos, conv_prev, past_c, past_kr, W):
    new_conv = []
    c_kv = None
    k_rope = None
    for i in range(DEPTH):
        h = rms_norm(x, W['norm_mix_pre'][i])
        if i < N_A:
            m, st = conformer_conv(h, conv_prev[i], W['conv_pw1'][i], W['conv_dw'][i], W['conv_dw_bias'][i],
                                   W['conv_ln_g'][i], W['conv_ln_b'][i], W['conv_pw2'][i])
            new_conv.append(st)
        else:
            j = i - N_A
            if j == 0:
                c_kv, k_rope = shared_kv(x, pos, W['kv_in_norm'], W['w_dkv'], W['kv_norm'])
            q_lat, q_rope = mla_query(h, pos, W['w_dq'][j], W['q_norm'][j], W['w_uq'][j], W['w_uk'])
            if past_c is None:
                o_lat = prompt_attention(q_lat, q_rope, c_kv, k_rope, pos)
            else:
                o_lat = sample_attention(q_lat, q_rope, past_c, past_kr, c_kv, k_rope)
            m = mla_output(o_lat, W['w_uv'], W['w_o'][j])
        x = x + rms_norm(m, W['norm_mix_post'][i])
        h = rms_norm(x, W['norm_ff_pre'][i])
        x = x + rms_norm(sq_relu_mlp(h, W['w_up'][i], W['w_down'][i]), W['norm_ff_post'][i])
        x = x + jax.nn.sigmoid(x @ W['ple_gate'][i]) * (ple[i] @ W['ple_proj'][i])
    return x, jnp.stack(new_conv), c_kv, k_rope

def setup_inputs(seed: int = 0) -> dict:
    key = jax.random.key(seed)
    ks = iter(jax.random.split(key, 48))

    def nrm(shape, scale):
        return jax.random.normal(next(ks), shape, jnp.float32) * scale

    def gain(shape):
        return 1.0 + nrm(shape, 0.05)

    n_pages = PAST_LEN // PAGE_SIZE
    n_used = DEC_BATCH * n_pages
    n_phys = n_used + n_used // 4
    page_table = jax.random.permutation(next(ks), n_phys)[:n_used].reshape(DEC_BATCH, n_pages).astype(jnp.int32)

    return {
        'x_prompt': nrm((BATCH, SEQ, D_MODEL), 1.0),
        'x_sample': nrm((DEC_BATCH, DEC_SEQ, D_MODEL), 1.0),
        'state_conv': nrm((N_A, DEC_BATCH, CONV_WIDTH - 1, D_MODEL), 1.0),
        'cache_kv_latent': nrm((n_phys, PAGE_SIZE, KV_LORA), 1.0),
        'cache_k_rope': nrm((n_phys, PAGE_SIZE, QK_ROPE), 1.0),
        'page_table': page_table,
        'p_prompt': nrm((DEPTH, BATCH, SEQ, PLE_DIM), 1.0),
        'p_sample': nrm((DEPTH, DEC_BATCH, DEC_SEQ, PLE_DIM), 1.0),
        'norm_mix_pre': gain((DEPTH, D_MODEL)),
        'norm_mix_post': gain((DEPTH, D_MODEL)),
        'norm_ff_pre': gain((DEPTH, D_MODEL)),
        'norm_ff_post': gain((DEPTH, D_MODEL)),
        'conv_pw1': nrm((N_A, D_MODEL, 2 * D_MODEL), D_MODEL ** -0.5),
        'conv_dw': nrm((N_A, CONV_WIDTH, D_MODEL), CONV_WIDTH ** -0.5),
        'conv_dw_bias': nrm((N_A, D_MODEL), 0.01),
        'conv_ln_g': gain((N_A, D_MODEL)),
        'conv_ln_b': nrm((N_A, D_MODEL), 0.01),
        'conv_pw2': nrm((N_A, D_MODEL, D_MODEL), D_MODEL ** -0.5),
        'kv_in_norm': gain((D_MODEL,)),
        'w_dkv': nrm((D_MODEL, KV_LORA + QK_ROPE), D_MODEL ** -0.5),
        'kv_norm': gain((KV_LORA,)),
        'w_uk': nrm((KV_LORA, N_HEADS, QK_NOPE), KV_LORA ** -0.5),
        'w_uv': nrm((KV_LORA, N_HEADS, V_HEAD), KV_LORA ** -0.5),
        'w_dq': nrm((N_B, D_MODEL, Q_LORA), D_MODEL ** -0.5),
        'q_norm': gain((N_B, Q_LORA)),
        'w_uq': nrm((N_B, Q_LORA, N_HEADS * (QK_NOPE + QK_ROPE)), Q_LORA ** -0.5),
        'w_o': nrm((N_B, N_HEADS * V_HEAD, D_MODEL), (N_HEADS * V_HEAD) ** -0.5),
        'w_up': nrm((DEPTH, D_MODEL, D_FF), D_MODEL ** -0.5),
        'w_down': nrm((DEPTH, D_FF, D_MODEL), D_FF ** -0.5),
        'ple_proj': nrm((DEPTH, PLE_DIM, D_MODEL), PLE_DIM ** -0.5),
        'ple_gate': nrm((DEPTH, D_MODEL, D_MODEL), D_MODEL ** -0.5),
    }

def reference(x_prompt, x_sample, state_conv, cache_kv_latent, cache_k_rope, page_table, p_prompt, p_sample,
              norm_mix_pre, norm_mix_post, norm_ff_pre, norm_ff_post,
              conv_pw1, conv_dw, conv_dw_bias, conv_ln_g, conv_ln_b, conv_pw2,
              kv_in_norm, w_dkv, kv_norm, w_uk, w_uv,
              w_dq, q_norm, w_uq, w_o,
              w_up, w_down, ple_proj, ple_gate):
    W = {
        'norm_mix_pre': norm_mix_pre, 'norm_mix_post': norm_mix_post,
        'norm_ff_pre': norm_ff_pre, 'norm_ff_post': norm_ff_post,
        'conv_pw1': conv_pw1, 'conv_dw': conv_dw, 'conv_dw_bias': conv_dw_bias,
        'conv_ln_g': conv_ln_g, 'conv_ln_b': conv_ln_b, 'conv_pw2': conv_pw2,
        'kv_in_norm': kv_in_norm, 'w_dkv': w_dkv, 'kv_norm': kv_norm, 'w_uk': w_uk, 'w_uv': w_uv,
        'w_dq': w_dq, 'q_norm': q_norm, 'w_uq': w_uq, 'w_o': w_o,
        'w_up': w_up, 'w_down': w_down, 'ple_proj': ple_proj, 'ple_gate': ple_gate,
    }
    B, T = x_prompt.shape[:2]
    conv0 = jnp.zeros((N_A, B, CONV_WIDTH - 1, D_MODEL), x_prompt.dtype)
    y_prompt, conv_p, c_p, kr_p = run_group(x_prompt, p_prompt, jnp.arange(T), conv0, None, None, W)

    DB, TS = x_sample.shape[:2]
    past_len = page_table.shape[1] * PAGE_SIZE
    past_c = cache_kv_latent[page_table].reshape(DB, past_len, KV_LORA)
    past_kr = cache_k_rope[page_table].reshape(DB, past_len, QK_ROPE)
    y_sample, conv_s, c_s, kr_s = run_group(x_sample, p_sample, past_len + jnp.arange(TS), state_conv,
                                            past_c, past_kr, W)
    return (y_prompt, y_sample, conv_p, conv_s, c_p, kr_p, c_s, kr_s)


_drawn_inputs = setup_inputs


def setup_inputs(seed=0):
    import zlib

    import numpy as np

    out = dict(_drawn_inputs(seed))
    spreads = {}
    factors = {'conv_dw_bias': 2.947, 'conv_ln_b': 6.042}
    for name, (base, spread) in spreads.items():
        noise = np.random.default_rng([zlib.crc32(name.encode()), seed]).standard_normal(out[name].shape)
        drawn = base * np.exp(spread * noise) if base else spread * noise
        out[name] = __import__('jax').numpy.asarray(drawn.astype(out[name].dtype))
    for name, factor in factors.items():
        out[name] = (out[name] * factor).astype(out[name].dtype)
    return out
```

```python
from contextlib import ExitStack

import numpy as np

import concourse.bass as bass
from concourse import mybir

F32 = mybir.dt.float32
F32R = mybir.dt.float32r
I32 = mybir.dt.int32
ACT = mybir.ActivationFunctionType
ALU = mybir.AluOpType
AX = mybir.AxisListType

P = 128
D = 1024
KT = D // P
TP, TS = 512, 64
T = TP + TS
H = T // 2
NS, TQ = 8, 8
CW = 31
FF = 4 * D
FC = 4
NCH = FF // P // FC
PLE = 256
NH, DN, DR, DV = 8, 128, 64, 128
CL, QL = 512, 768
PAGES, PAGE = 16, 128
EPS = 1e-6
SCALE = (DN + DR) ** -0.5
NEG = -1e30
RING, WRING = 4, 2
SLOT = 4 * (CL + DR)
WSLOT = 2048
VP = TP + CW - 1
VSQ = TQ + CW - 1
VW = VP + NS * VSQ


class Order:

    def __init__(self, keys):
        self.at = {k: n + 1 for n, k in enumerate(keys)}

    def __call__(self, *key):
        return self.at[key]


PHASES = [("pw1", 8, KT, 2, 2), ("pw2", 4, KT, 2, 1), ("mlp0", 4 * NCH, 0, 0, 1), ("ple0", 1, 2, 8, 1),
          ("gate0", 4, KT, 2, 1), ("dkv", 3, KT, 2, (1, 1, 2)), ("dq", 3, KT, 2, 1),
          ("uq", 6, QL // P, 2, (2, 2, 2, 2, 4, 4)), ("kvh", 4, CL // P, 0, 2), ("cache", 32, 0, 0, 8), ("uv", 2, CL // P, 0, 1), ("wo", 4, KT, 2, 1),
          ("mlp1", 4 * NCH, 0, 0, 1), ("ple1", 1, 2, 8, 1), ("gate1", 4, KT, 2, 1)]
RAW0, DENSE0, UNIT0, UNITS = {}, {}, {}, {}
PARTS, KIND = [], []
_d = _u = 0
for _n, _s, _k, _t, _parts in PHASES:
    RAW0[_n], DENSE0[_n], UNIT0[_n] = len(PARTS), _d, _u
    PARTS += list(_parts) if isinstance(_parts, tuple) else [_parts] * _s
    KIND += [(_n, _j) for _j in range(_s)]
    _d += 0 if _n == "cache" else _s
    UNITS[_n] = {"mlp0": 24 * NCH, "mlp1": 24 * NCH, "dkv": 10}.get(_n, 2 * _t * _s)
    _u += UNITS[_n]
LANDED = [16 * sum(PARTS[g % RING:g + 1:RING]) for g in range(len(PARTS))]

STATS = [("x0", KT), ("lm", KT), ("lv", KT), ("y0", KT), ("x1", KT), ("m0", KT), ("x2", KT), ("ck", CL // P),
         ("cq", QL // P), ("y1", KT), ("x3", KT), ("m1", KT)]
NT = dict(STATS)
BLOCKS = [("x0", 0), ("x0", 1), ("lm", 0), ("lm", 1), ("lv", 0), ("lv", 1), ("y0", 0), ("x1", 0), ("y0", 1), ("x1", 1),
          ("m0", 0), ("m0", 1), ("x2", 0), ("x2", 1), ("ck", 0), ("ck", 1), ("cq", 0), ("cq", 1),
          ("y1", 0), ("x3", 0), ("y1", 1), ("x3", 1), ("m1", 0), ("m1", 1)]
SUMS = [("x0", 0), ("x0", 1), ("lm", 0), ("lm", 1), ("lv", 0), ("lv", 1), ("y0", 0), ("y0", 1), ("x1", 0), ("x1", 1),
        ("m0", 0), ("m0", 1), ("x2", 0), ("x2", 1), ("ck", 0), ("ck", 1), ("cq", 0), ("cq", 1),
        ("y1", 0), ("y1", 1), ("x3", 0), ("x3", 1), ("m1", 0), ("m1", 1)]
SQ = Order([(s, h, m) for s, h in BLOCKS if s != "lm" for m in range(NT[s])])
ACC = Order([(s, h, m) for s, h in BLOCKS for m in range(NT[s])])
SUM = Order(SUMS)
ROOT = Order([(s, h) for s, h in SUMS if s != "lm"])
SCALED_BY_INPUT = ("m0", "m1", "ck", "cq")
ROW = Order([(s, h) for s, h in SUMS if s in SCALED_BY_INPUT])
RSTD = SUM
SPLITS = [("x0", KT), ("sw", KT), ("ff0", KT), ("g0", KT), ("kv", KT), ("mx", KT), ("cq", QL // P), ("o", NH),
          ("ff1", KT), ("g1", KT)]
A = Order([(v, h, m) for v, n in SPLITS for h in range(2) for m in range(n)])
XS = ["y0", "m0", "y1", "m1"]
XU = Order([(s, h, m) for s in XS for h in range(2) for m in range(KT)])
GATE_ORDER = [(h, 2 * s + t) for s in range(4) for h in range(2) for t in range(2)]
XG = Order([(g, h, m) for g in range(2) for h, m in GATE_ORDER])
SC = Order([(s, h, m) for s in ("sw", "y0", "m0", "ck", "cq", "y1", "m1")
            for h in range(2) for m in range(NT.get(s, KT))])

GAINS = [("mix_pre0", KT), ("mix_pre1", KT), ("mix_post0", KT), ("mix_post1", KT), ("ff_pre0", KT), ("ff_pre1", KT),
         ("ff_post0", KT), ("ff_post1", KT), ("dw_bias", KT), ("ln_g", KT), ("ln_b", KT), ("kv_in", KT),
         ("kv_norm", CL // P), ("q_norm", QL // P)]
GCOL, _c = {}, 0
for _n, _t in GAINS:
    GCOL[_n] = _c
    _c += _t
NG = _c


EVACUATED = {"y0": "pw2", "y1": "wo", "m0": "mlp0", "m1": "mlp1", "ck": "dkv", "cq": "dq"}
BANKS = 4
UP = 8
CHUNK = 24


def unit_of(st, h, m):
    u0 = UNIT0[EVACUATED[st]]
    if st in ("m0", "m1"):
        return u0 + CHUNK * (NCH - 1) + UP + 8 * (m // 4) + 4 * h + m % 4
    return u0 + 4 * (m // 2) + 2 * h + m % 2


def freed(u):
    return BANKS + u + 1


def decoder_step(nc, io):
    with ExitStack() as ctx:
        def sb(name, shape, dt=F32):
            return ctx.enter_context(nc.sbuf_tensor(name, shape, dt))

        def sem(name):
            return ctx.enter_context(nc.semaphore(name))

        bank = [ctx.enter_context(nc.psum_tensor(f"bank{i}", [P, 512], F32)) for i in range(8)]
        X = sb("X", [P, KT, T])
        AH, AL = sb("AH", [P, KT, T], F32R), sb("AL", [P, KT, T], F32R)
        BH, BL = sb("BH", [P, FC, T], F32R), sb("BL", [P, FC, T], F32R)
        Y = sb("Y", [P, KT, T])
        RAW = sb("RAW", [P, RING, SLOT])
        WH, WL = sb("WH", [P, WRING, WSLOT], F32R), sb("WL", [P, WRING, WSLOT], F32R)
        R1, R2 = sb("R1", [P, 2, H]), sb("R2", [P, 2, H])
        acc, sq = sb("acc", [P, 2, H]), sb("sq", [P, 2, H])
        scaled, prod = sb("scaled", [P, 2, H]), sb("prod", [P, 2, H])
        root = sb("root", [P, 2, H])
        ident, ones = sb("ident", [P, P]), sb("ones", [P, P])
        gains = sb("gains", [P, NG])
        taps = sb("taps", [P, KT, CW])
        eps = sb("eps", [P, 1])
        tiny = sb("tiny", [P, 8])
        S = sb("S", [P, 8064])

        V = S[:, 0:KT * VW].rearrange("p (m c) -> p m c", m=KT)
        v0 = KT * VW
        state_out = S[:, v0:v0 + 1024].rearrange("p (b c) -> p b c", b=2)
        x_stage = S[:, v0:v0 + D]
        taps_stage = RAW[:, 2, 0:D]
        state_stage = RAW[:, 3, 0:2 * D].rearrange("p (g n) -> p g n", g=2)
        yflat = Y[:, :, :].rearrange("p m t -> p (m t)")
        p_stage = S[:, 0:5 * PLE].rearrange("p (b c) -> p b c", b=5)
        QR = S[:, 0:2304].rearrange("p (j t) -> p j t", j=4)
        KR = S[:, 2304:2880]
        QLAT = S[:, 2880:4928].rearrange("p (c q) -> p c q", c=4)
        CS = S[:, 4928:5184].rearrange("p (c t) -> p c t", c=4)
        QRS = S[0:DR, 5184:5696]
        CK = S[:, 5696:8000].rearrange("p (c t) -> p c t", c=4)
        PT = S[:, 5696:7744].rearrange("p (k q) -> p k q", k=4)
        KTS = S[:, 5696:6976].rearrange("p (b c) -> p b c", b=2)
        PS = S[:, 6976:8064].rearrange("p (k q) -> p k q", k=17)
        COS, SIN, ROT = S[:, 2880:3456], S[:, 3456:4032], S[:, 4032:4160]
        kv_stage = S[:, 4160:4736]
        kT = sq[:, :, :].rearrange("p a b -> p (a b)")[:, 0:TP]
        vn = root[:, :, :].rearrange("p a b -> p (a b)")[:, 0:TP]
        ukT = acc[:, :, :].rearrange("p a b -> p (a b)")[:, 0:TP]
        PB = [prod[:, :, :].rearrange("p a b -> p (a b)")[:, 0:TP],
              scaled[:, :, :].rearrange("p a b -> p (a b)")[:, 0:TP]]
        flat = {n: t[:, :, :].rearrange("p a b -> p (a b)") for n, t in
                (("prod", prod), ("scaled", scaled), ("sq", sq), ("root", root), ("acc", acc))}
        cmask = R2[:, :, :].rearrange("p a b -> p (a b)")[:, 0:P]
        nmask = R2[:, :, :].rearrange("p a b -> p (a b)")[0:TQ, P:P + 64]

        landed = [sem(f"landed{i}") for i in range(RING)]
        hi_done, lo_done, w_used, pe_read_raw = sem("hi_done"), sem("lo_done"), sem("w_used"), sem("pe_read_raw")
        unit_done, bank_free = sem("unit_done"), sem("bank_free")
        consts, ones_set, vecs, x_in, x_stage_in = sem("consts"), sem("ones_set"), sem("vecs"), sem("x_in"), sem("x_stage_in")
        turned, unturned = sem("turned"), sem("unturned")
        sq_done, acc_done, sum_done, root_done, rstd_done = (sem("sq_done"), sem("acc_done"), sem("sum_done"),
                                                             sem("root_done"), sem("rstd_done"))
        row_step = sem("row_step")
        a_hi, a_lo, x_done, sc_done = sem("a_hi"), sem("a_lo"), sem("x_done"), sem("sc_done")
        xg_done, y_out = sem("xg_done"), [sem("y_out0"), sem("y_out1")]
        out_sem = sem("out_sem")

        SG = NS // 2 * (CW - 1)

        def half(t, m, h):
            return t[:, m, h * H:(h + 1) * H]

        def gain(name, m):
            return gains[:, GCOL[name] + m:GCOL[name] + m + 1]

        consts_sem = consts
        conv_step, v_done, gate_sig = sem("conv_step"), sem("v_done"), sem("gate_sig")
        state_done, state_copied = sem("state_done"), sem("state_copied")
        state_out_sem = [sem("state_out0"), sem("state_out1")]
        unturned_v, unturned_a = sem("unturned_v"), sem("unturned_a")
        sw_sig, sw_lin, sw_val = sem("sw_sig"), sem("sw_lin"), sem("sw_val")
        ck_val, b_hi, b_lo = sem("ck_val"), sem("b_hi"), sem("b_lo")
        relu_done, sq_relu, u_hi, u_lo = sem("relu_done"), sem("sq_relu"), sem("u_hi"), sem("u_lo")
        y_zero, p_in, p_turned, p_hi, p_lo = sem("y_zero"), sem("p_in"), sem("p_turned"), sem("p_hi"), sem("p_lo")
        sig_done, gated = sem("sig_done"), sem("gated")
        rope_in, rot_done, rope_step = sem("rope_in"), sem("rot_done"), sem("rope_step")
        kv_turned, kv_staged, kv_out, cs_done = sem("kv_turned"), sem("kv_staged"), sem("kv_out"), sem("cs_done")
        centred = sem("centred")

        def w_at(d):
            return d % WRING

        def unit_end(phase, h):
            last = {"pw1": 2, "pw2": 2, "dkv": 1, "dq": 2, "uq": 2, "wo": 2, "gate0": 2, "gate1": 2,
                    "ple0": 8, "ple1": 8}[phase]
            return UNIT0[phase] + UNITS[phase] - (last if h == 0 else 0)

        def up_n(h, m):
            return 4 * (m // 2) + 2 * h + m % 2

        read_before = {"sw": "pw1", "ff0": "pw2", "kv": "gate0", "mx": "dkv", "cq": "dq", "ff1": "wo"}
        gain_of = {"x0": "mix_pre0", "ff0": "ff_pre0", "g0": None, "kv": "kv_in", "mx": "mix_pre1",
                   "cq": "q_norm", "ff1": "ff_pre1", "g1": None, "sw": None}
        tokens = [(b * P, P) for b in range(4)] + [(TP, TS)]
        SLABS = {n: s for n, s, *_ in PHASES}
        KR_STEP = 7
        STATES = [(m, g) for m in range(KT) for g in range(2)] + [(None, 0), (None, 1)]
        NORM_OF = {"sw": "lv"}
        SM = 13

        def scaled_read(key):
            st, h, m = key
            if st in ("y0", "m0", "y1", "m1"):
                return x_done, XU(*key)
            if st == "sw":
                return sw_val, KT * h + m + 1
            return (ck_val, 4 * h + m + 1) if st == "ck" else (a_lo, A(*key))

        kvt_done, kvt_used = sem("kvt_done"), sem("kvt_used")
        v_mm, v_used, uk_mm, uk_used, ql_mm, ql_used = (sem("v_mm"), sem("v_used"), sem("uk_mm"), sem("uk_used"),
                                                        sem("ql_mm"), sem("ql_used"))
        s_mm, s_masked, s_max, s_exp, s_rec, p_ready = (sem("s_mm"), sem("s_masked"), sem("s_max"), sem("s_exp"),
                                                        sem("s_rec"), sem("p_ready"))
        pt_mm, pt_used, pv_mm = sem("pt_mm"), sem("pt_used"), sem("pv_mm")
        table_in, page_mm, page_c, page_r, qk_mm, new_in, new_nat, new_nat_c = (
            sem("table_in"), sem("page_mm"), sem("page_c"), sem("page_r"), sem("qk_mm"), sem("new_in"),
            sem("new_nat"), sem("new_nat_c"))
        sm_step, max_t, max_b, den_b, prob, out_mm, lat_out = (sem("sm_step"), sem("max_t"), sem("max_b"),
                                                               sem("den_b"), sem("prob"), sem("out_mm"), sem("lat_out"))
        new_mm, dve_step = sem("new_mm"), sem("dve_step")
        qrs_mm, qrs_c, uv_mm, y_turned, y_copied_v, y_copied_a = (sem("qrs_mm"), sem("qrs_c"), sem("uv_mm"),
                                                                  sem("y_turned"), sem("y_copied_v"), sem("y_copied_a"))
        table = sb("table", [1, PAGES], I32)

        block = ctx.enter_context(nc.Block())

        def cache_loads(sp):
            g0 = RAW0["cache"]
            with sp.Fori(0, NS) as i:
                sp.dma_start(table[:], io["page_table"][bass.ds(i, 1), :]).then_inc(table_in, 16)
                sp.wait_ge(table_in, 16)
                sp.sem_clear(table_in)
                for j in range(RING):
                    pages = [sp.value_load(table[0:1, 4 * j + q:4 * j + q + 1], min_val=0,
                                           max_val=io["cache_kv_latent"].shape[0] - 1) for q in range(4)]
                    sp.wait_ge(pe_read_raw, 1 + j + RING * i)
                    sp.wait_ge(ones_set, 1)
                    if j == 0:
                        sp.wait_ge(lo_done, DENSE0["kvh"] + 4)
                    for q in range(4):
                        dst = RAW[:, (g0 + j) % RING, 576 * q:576 * q + 576].rearrange("p (a c) -> p a c", a=1)
                        sp.dma_start(dst[:, :, 0:CL],
                                     io["cache_kv_latent"].rearrange("n p c -> p n c")[:, bass.ds(pages[q], 1)])\
                            .then_inc(landed[(g0 + j) % RING], 16)
                        sp.dma_start(dst[:, :, CL:CL + DR],
                                     io["cache_k_rope"].rearrange("n p c -> p n c")[:, bass.ds(pages[q], 1)])\
                            .then_inc(landed[(g0 + j) % RING], 16)

        @block.sync
        def _(sp):
            def put(g, parts, dst_slot, i=None, per=0):
                for dst, src in parts:
                    sp.dma_start(dst, src).then_inc(landed[g % RING], 16)

            def slot(g, a, b):
                return RAW[:, g % RING, a:b]

            def cols(w, kt, c0, n):
                return w.rearrange("(k p) n -> p k n", p=P)[:, :, c0:c0 + n] if kt else None

            def free(g, i=0):
                kind, j = KIND[g - RING]
                if kind == "cache":
                    sp.wait_ge(pe_read_raw, 4 + j + 1)
                    return
                if kind == "kvh":
                    sp.wait_ge(pe_read_raw, j + 1)
                sp.wait_ge(lo_done, DENSE0[kind] + j + 1)

            def dense(phase, w, kt, n):
                for j in range(SLABS[phase]):
                    g = RAW0[phase] + j
                    free(g)
                    sp.dma_start(slot(g, 0, kt * n).rearrange("p (k n) -> p k n", k=kt),
                                 w.rearrange("(k p) n -> p k n", p=P)[:, :, j * n:(j + 1) * n])\
                        .then_inc(landed[g % RING], 16)

            def mlp(layer, phase):
                up = io["w_up"][layer].rearrange("(k p) (c n) -> p c k n", p=P, n=256)
                down = io["w_down"][layer].rearrange("(c k p) n -> p c k n", p=P, k=FC)
                g0, d0 = RAW0[phase], DENSE0[phase]
                with sp.Fori(0, NCH) as i:
                    for j in range(RING):
                        g = g0 + j
                        dst = slot(g, 0, WSLOT)
                        sp.wait_ge(lo_done, d0 + j - RING + 1 + RING * i)
                        sp.wait_ge(ones_set, 1)
                        if j < 2:
                            sp.dma_start(dst.rearrange("p (c k n) -> p c k n", c=1, k=KT),
                                         up[:, bass.ds(2 * i + j, 1)]).then_inc(landed[g % RING], 16)
                        else:
                            n = (j - 2) * 512
                            sp.dma_start(dst.rearrange("p (c k n) -> p c k n", c=1, k=FC),
                                         down[:, bass.ds(i, 1), :, n:n + 512]).then_inc(landed[g % RING], 16)

            def ple(layer, phase):
                g = RAW0[phase]
                free(g)
                sp.dma_start(slot(g, 0, 2 * D).rearrange("p (k n) -> p k n", k=2),
                             io["ple_proj"][layer].rearrange("(k p) n -> p k n", p=P)).then_inc(landed[g % RING], 16)

            def load_p(layer):
                for b, (t0, n) in enumerate(tokens):
                    src = io["p_prompt"][layer, 0, t0:t0 + n] if b < 4 else \
                        io["p_sample"][layer].rearrange("s t c -> (s t) c")
                    sp.dma_start(p_stage[0:n, b, :], src).then_inc(p_in, 16)

            sp.dma_start(ident[:], io["consts"][:, 0:P]).then_inc(consts, 16)
            row = 0
            vec = {"mix_pre0": io["norm_mix_pre"][0], "mix_pre1": io["norm_mix_pre"][1],
                   "mix_post0": io["norm_mix_post"][0], "mix_post1": io["norm_mix_post"][1],
                   "ff_pre0": io["norm_ff_pre"][0], "ff_pre1": io["norm_ff_pre"][1],
                   "ff_post0": io["norm_ff_post"][0], "ff_post1": io["norm_ff_post"][1],
                   "dw_bias": io["conv_dw_bias"][0], "ln_g": io["conv_ln_g"][0], "ln_b": io["conv_ln_b"][0],
                   "kv_in": io["kv_in_norm"], "kv_norm": io["kv_norm"], "q_norm": io["q_norm"][0]}
            for name, n in GAINS:
                sp.dma_start(flat["prod"][row:row + n, 0:P], vec[name].rearrange("(r c) -> r c", c=P)).then_inc(vecs, 16)
                row += n
            for b in range(4):
                sp.dma_start(yflat[:, b * D:(b + 1) * D], io["x_prompt"][0, b * P:(b + 1) * P]).then_inc(x_in, 16)
            sp.dma_start(x_stage[0:TS], io["x_sample"].rearrange("s t c -> (s t) c")).then_inc(x_in, 16)
            pw1 = io["conv_pw1"][0].rearrange("(k p) (a m n) -> p m a k n", p=P, a=2, n=P)

            def pw1_slab(g, m):
                for a in range(2):
                    sp.dma_start(slot(g, 0, WSLOT).rearrange("p (m k a n) -> p m k a n", m=1, k=KT, a=2)[:, :, :, a],
                                 pw1[:, m, a]).then_inc(landed[g % RING], 16)

            for j in range(2):
                pw1_slab(j, slice(j, j + 1))
            sp.dma_start(taps_stage[0:CW], io["conv_dw"][0]).then_inc(vecs, 16)
            for g in range(2):
                sp.dma_start(state_stage[0:SG, g, :],
                             io["state_conv"][0, 4 * g:4 * g + 4].rearrange("s j c -> (s j) c")).then_inc(vecs, 16)
            sp.wait_ge(turned, 26)
            for j in range(2, 4):
                pw1_slab(j, slice(j, j + 1))
            for j in range(4, 8):
                free(j)
                pw1_slab(j, slice(j, j + 1))
            dense("pw2", io["conv_pw2"][0], KT, 256)
            for q in state_out_sem:
                sp.wait_ge(q, 16 * len(STATES) // 2)
            sp.wait_ge(conv_step, 2 * CW * KT)
            load_p(0)
            mlp(0, "mlp0")
            ple(0, "ple0")
            dense("gate0", io["ple_gate"][0], KT, 256)
            for j in range(3):
                g = RAW0["dkv"] + j
                free(g)
                wk = io["w_dkv"].rearrange("(k p) n -> p k n", p=P)
                if j < 2:
                    sp.dma_start(slot(g, 0, WSLOT).rearrange("p (k n) -> p k n", k=KT),
                                 wk[:, :, 256 * j:256 * j + 256]).then_inc(landed[g % RING], 16)
                else:
                    for c in range(2):
                        sp.dma_start(slot(g, 0, KT * P).rearrange("p (k n) -> p k n", k=KT)[:, :, 64 * c:64 * c + 64],
                                     wk[:, :, CL:CL + DR]).then_inc(landed[g % RING], 16)
            sp.wait_ge(p_turned, 4)
            sp.dma_start(S[:, 2880:4160], io["consts"][:, 320:1600]).then_inc(rope_in, 16)
            dense("dq", io["w_dq"][0], KT, 256)
            uq = io["w_uq"][0].rearrange("(k p) (h e) -> p k h e", p=P, h=NH)
            for j in range(6):
                g = RAW0["uq"] + j
                free(g)
                dst = slot(g, 0, 6 * 256).rearrange("p (k n) -> p k n", k=6)
                heads, e0, e1 = ((2 * j, 2 * j + 1), 0, DN) if j < 4 else (range(4 * (j - 4), 4 * (j - 4) + 4), DN, DN + DR)
                for n, h in enumerate(heads):
                    sp.dma_start(dst[:, :, n * (e1 - e0):(n + 1) * (e1 - e0)], uq[:, :, h, e0:e1])\
                        .then_inc(landed[g % RING], 16)
            for j in range(4):
                g = RAW0["kvh"] + j
                free(g)
                for n, w in enumerate((io["w_uk"], io["w_uv"])):
                    sp.dma_start(slot(g, 1024 * n, 1024 * n + 1024).rearrange("p (k n) -> p k n", k=4),
                                 w.rearrange("(k p) h n -> p k (h n)", p=P)[:, :, 256 * j:256 * j + 256])\
                        .then_inc(landed[g % RING], 16)
            sp.wait_ge(sc_done, SC("cq", 1, 5))
            sp.dma_start(cmask, io["consts"][:, 128:256]).then_inc(consts, 16)
            sp.dma_start(nmask, io["consts"][0:TQ, 256:320]).then_inc(consts, 16)
            cache_loads(sp)
            for j in range(2):
                g = RAW0["uv"] + j
                free(g)
                sp.dma_start(slot(g, 0, WSLOT).rearrange("p (k n) -> p k n", k=4),
                             io["w_uv"].rearrange("(k p) h n -> p k (h n)", p=P)[:, :, 512 * j:512 * j + 512])\
                    .then_inc(landed[g % RING], 16)
            dense("wo", io["w_o"][0], KT, 256)
            sp.wait_ge(a_lo, A("o", 1, NH - 1))
            load_p(1)
            mlp(1, "mlp1")
            ple(1, "ple1")
            dense("gate1", io["ple_gate"][1], KT, 256)

        dense_slabs = [(g, k, j) for g, (k, j) in enumerate(KIND) if k != "cache"]
        floats = {"ple0": 2048, "ple1": 2048, "uq": 1536}

        def slab_size(d):
            g, k, j = dense_slabs[d]
            return 1024 if (k, j) == ("dkv", 2) else floats.get(k, 2048)

        def landed_at(d):
            g = dense_slabs[d][0]
            return landed[g % RING], LANDED[g]

        def raw_of(d):
            return RAW[:, dense_slabs[d][0] % RING, 0:slab_size(d)]


        def prev(order, key, back):
            n = order.at[key] - back
            return next((k for k, v in order.at.items() if v == n), None)

        @block.scalar
        def _(act):
            def hi(d, i=None, per=16):
                s, v = landed_at(d)
                if i is None:
                    act.wait_ge(s, v)
                    act.wait_ge(w_used, d + 1)
                else:
                    act.wait_ge(s, v + per * i)
                    act.wait_ge(w_used, d + 1 + RING * i)
                nc.scalar.activation(WH[:, d % WRING, 0:slab_size(d)], raw_of(d), ACT.Copy).then_inc(hi_done, 1)

            def square(st, h, m, src):
                before = prev(SQ, (st, h, m), 2)
                if before:
                    act.wait_ge(acc_done, ACC(*before))
                nc.scalar.activation(sq[:, SQ(st, h, m) % 2, :], src, ACT.Square).then_inc(sq_done, 1)

            def root_of(st, h):
                if st in SCALED_BY_INPUT:
                    act.wait_ge(row_step, ROW(st, h))
                    src = root[:, h, :]
                else:
                    act.wait_ge(sum_done, SUM(st, h))
                    src = bank[4 + h][:, 0:H]
                before = [k for k in ROOT.at if k[1] == h and ROOT(*k) < ROOT(st, h)]
                if before:
                    act.wait_ge(rstd_done, RSTD(*before[-1]))
                nc.scalar.activation(root[:, h, :], src, ACT.Sqrt, bias=eps[:, 0:1], scale=1.0 / (P * NT[st]))\
                    .then_inc(root_done, 1)

            def split(v, h, m, src):
                if v in read_before:
                    act.wait_ge(unit_done, unit_end(read_before[v], h))
                if v in ("g0", "g1"):
                    act.wait_ge(unit_done, UNIT0["mlp" + v[1]] + CHUNK * NCH)
                g = gain_of[v]
                if g:
                    nc.scalar.activation(half(AH, m, h), src, ACT.Copy, scale=gain(g, m)).then_inc(a_hi, 1)
                else:
                    nc.scalar.activation(half(AH, m, h), src, ACT.Copy).then_inc(a_hi, 1)

            act.wait_ge(ones_set, 3)
            for e in range(1, 26, 2):
                act.wait_ge(turned, e + 1)
                src = bank[4 + e % 4]
                if e == 1:
                    nc.scalar.activation(taps[:, :, :], src[:, 0:KT * CW].rearrange("p (m c) -> p m c", m=KT),
                                         ACT.Copy).then_inc(unturned_a, 1)
                elif e < 18:
                    nc.scalar.activation(X[:, (e - 3) // 2, TP:T], src[:, 0:TS], ACT.Copy).then_inc(unturned_a, 1)
                else:
                    nc.scalar.activation(V[:, e - 18, VP:VW].rearrange("p (s c) -> p s c", s=NS)[:, :, 0:CW - 1],
                                         src[:, 0:2 * SG].rearrange("p (s c) -> p s c", s=NS),
                                         ACT.Copy).then_inc(unturned_a, 1)
            hi(0)
            act.wait_ge(unturned_v, 13)
            act.wait_ge(unturned_a, 13)
            for h in range(2):
                for m in range(KT):
                    split("x0", h, m, half(X, m, h))
                    square("x0", h, m, half(X, m, h))
            for h in range(2):
                root_of("x0", h)

            with act.Fori(0, 2) as i:
                for j in range(4):
                    hi(j + 1, i, 32 if j < 3 else 16)
                    for h in range(2):
                        act.wait_ge(bank_free, freed(4 * j + 2 * h + 1) + 16 * i)
                        nc.scalar.activation(prod[:, h, :], prod[:, h, :], ACT.Sigmoid).then_inc(gate_sig, 1)
            for e, (m, g) in enumerate(STATES):
                act.wait_ge(state_done, e + 1)
                if e >= 2:
                    act.wait_ge(state_out_sem[e % 2], 16 * (e // 2))
                nc.scalar.activation(state_out[0:CW - 1, e % 2, :], bank[4 + e % 4][0:CW - 1, 0:512], ACT.Copy)\
                    .then_inc(state_copied, 1)
                act.wait_ge(state_copied, e + 1)
                src = state_out[0:CW - 1, e % 2, :]
                if m is None:
                    dst = io["new_conv_prompt"][0, 0, :, 512 * g:512 * g + 512]
                else:
                    dst = io["new_conv_sample"][0, 4 * g:4 * g + 4, :, m * P:(m + 1) * P].rearrange("s j c -> j s c")
                    src = src.rearrange("j (s c) -> j s c", s=4)
                act.dma_start(dst, src).then_inc(state_out_sem[e % 2], 16)

            for h in range(2):
                for m in range(KT):
                    act.wait_ge(centred, KT * h + m + 1)
                    square("lv", h, m, half(Y, m, h))
                root_of("lv", h)
                for m in range(KT):
                    n = KT * h + m
                    act.wait_ge(sc_done, SC("sw", h, m))
                    if n >= 2:
                        act.wait_ge(a_lo, A("x0", 1, KT - 1) + n - 1)
                    nc.scalar.activation(prod[:, n % 2, :], scaled[:, SC("sw", h, m) % 2, :], ACT.Sigmoid,
                                         bias=gain("ln_b", m), scale=gain("ln_g", m)).then_inc(sw_sig, 1)
                    act.wait_ge(sw_val, n + 1)
                    split("sw", h, m, prod[:, n % 2, :])

            def hi_steps(phase):
                for j in range(SLABS[phase]):
                    hi(DENSE0[phase] + j + 1)

            def after_mixer(st, v, stx):
                for h in range(2):
                    for m in range(KT):
                        act.wait_ge(bank_free, freed(unit_of(st, h, m)))
                        square(st, h, m, half(Y, m, h))
                    root_of(st, h)
                    for m in range(KT):
                        act.wait_ge(x_done, XU(st, h, m))
                        split(v, h, m, half(X, m, h))
                        square(stx, h, m, half(X, m, h))

            def mlp(layer):
                phase, v = f"mlp{layer}", f"g{layer}"
                d0, u0 = DENSE0[phase], UNIT0[phase]
                b0 = UP * NCH * layer
                with act.Fori(0, NCH) as i:
                    for j in range(4):
                        hi(d0 + j + 1, i)
                        if j >= 2:
                            continue
                        for k in range(5):
                            n = 4 * j + k
                            if k < 4:
                                act.wait_ge(unit_done, u0 + n + 1 + CHUNK * i)
                                nc.scalar.activation(scaled[:, n % 2, :], bank[(u0 + n) % BANKS][:, 0:H], ACT.Relu)\
                                    .then_inc(relu_done, 1)
                            if k:
                                n, q = n - 1, k - 1
                                act.wait_ge(bank_free, freed(u0 + n) + CHUNK * i)
                                nc.scalar.activation(half(BH, 2 * j + q % 2, q // 2), prod[:, n % 2, :], ACT.Copy)\
                                    .then_inc(u_hi, 1)
                for h in range(2):
                    root_of(f"x{2 * layer + 1}", h)
                for e in range(4):
                    kt, part = e // 2, e % 2
                    a, b = (0, TP) if part == 0 else (TP, T)
                    act.wait_ge(p_turned, 4 * layer + e + 1)
                    nc.scalar.activation(BH[:, kt, a:b], bank[6 + part][:, 0:b - a], ACT.Copy).then_inc(p_hi, 1)
                st = f"m{layer}"
                for h in range(2):
                    for m in range(KT):
                        act.wait_ge(bank_free, freed(unit_of(st, h, m)))
                        square(st, h, m, half(Y, m, h))
                    root_of(st, h)
                for h in range(2):
                    for m in range(KT):
                        act.wait_ge(x_done, XU(st, h, m))
                        split(v, h, m, half(X, m, h))

                hi(DENSE0[f"ple{layer}"] + 1)
                d0, u0 = DENSE0[f"gate{layer}"], UNIT0[f"gate{layer}"]
                for j in range(4):
                    if d0 + j + 1 < len(dense_slabs):
                        hi(d0 + j + 1)
                    for k in range(4):
                        n = 4 * j + k
                        act.wait_ge(unit_done, u0 + n + 1)
                        if n >= 2:
                            act.wait_ge(bank_free, freed(u0 + n - 2))
                        nc.scalar.activation(prod[:, n % 2, :], bank[(u0 + n) % BANKS][:, 0:H], ACT.Sigmoid)\
                            .then_inc(sig_done, 1)

            hi_steps("pw2")
            after_mixer("y0", "ff0", "x1")
            mlp(0)

            for h in range(2):
                for m in range(KT):
                    act.wait_ge(xg_done, XG(0, h, m))
                    split("kv", h, m, half(X, m, h))
                    square("x2", h, m, half(X, m, h))
            hi_steps("dkv")
            for h in range(2):
                root_of("x2", h)
            for h in range(2):
                for m in range(KT):
                    split("mx", h, m, half(X, m, h))
            hi_steps("dq")
            for h in range(2):
                for m in range(4):
                    act.wait_ge(bank_free, freed(unit_of("ck", h, m)))
                    square("ck", h, m, half(CK, m, h))
                root_of("ck", h)
            for h in range(2):
                for m in range(4):
                    act.wait_ge(ck_val, 4 * h + m + 1)
                    nc.scalar.activation(half(BH, m, h), half(CK, m, h), ACT.Copy).then_inc(b_hi, 1)
            for h in range(2):
                for m in range(6):
                    act.wait_ge(bank_free, freed(unit_of("cq", h, m)))
                    square("cq", h, m, half(Y, m, h))
                root_of("cq", h)
            for h in range(2):
                for m in range(6):
                    act.wait_ge(sc_done, SC("cq", h, m))
                    split("cq", h, m, scaled[:, SC("cq", h, m) % 2, :])
            for j in range(6):
                hi(DENSE0["uq"] + j + 1)
                if j == 5:
                    break
                t0, n = tokens[j]
                act.wait_ge(kv_turned, j + 1)
                if j:
                    act.wait_ge(kv_out, 32 * j)
                nc.scalar.activation(kv_stage[0:n, 0:CL], bank[4][0:n, 0:CL], ACT.Copy).then_inc(kv_staged, 1)
                nc.scalar.activation(kv_stage[0:n, CL:CL + DR], bank[5][0:n, 0:DR], ACT.Copy).then_inc(kv_staged, 1)
                act.wait_ge(kv_staged, 2 * j + 2)
                for a, b, prompt, sample in ((0, CL, "new_kv_prompt", "new_kv_sample"),
                                             (CL, CL + DR, "new_kr_prompt", "new_kr_sample")):
                    dst = io[prompt][0, t0:t0 + n] if j < 4 else io[sample].rearrange("s t c -> (s t) c")
                    act.dma_start(dst, kv_stage[0:n, a:b]).then_inc(kv_out, 16)

            for hd in range(NH):
                if hd % 2 == 0 and hd < NH - 2:
                    hi(DENSE0["kvh"] + hd // 2 + 1)
                act.wait_ge(kvt_done, hd + 1)
                if hd:
                    act.wait_ge(s_mm, 4 * hd)
                nc.scalar.activation(kT, bank[0][:, 0:TP], ACT.Copy).then_inc(kvt_used, 1)

                def exp(qb):
                    n, w = 4 * hd + qb, (qb + 1) * P
                    act.wait_ge(s_max, 2 * n + 2)
                    if n >= 2:
                        act.wait_ge(pt_mm, n - 1)
                    c = 4 * (n % 2)
                    nc.scalar.activation(PB[n % 2][:, 0:w], bank[4 + n % 2][:, 0:w], ACT.Exp, scale=SCALE,
                                         bias=tiny[:, c + 1:c + 2], accum_out=tiny[:, c + 2:c + 3]).then_inc(s_exp, 1)

                def pt(qb):
                    n = 4 * hd + qb
                    act.wait_ge(pt_mm, n + 1)
                    if qb == 0 and hd:
                        act.wait_ge(pv_mm, hd)
                    if n == 0:
                        act.wait_ge(kv_turned, 5)
                        act.wait_ge(cs_done, 1)
                    nc.scalar.activation(PT[:, 0:qb + 1, qb * P:(qb + 1) * P],
                                         bank[6][:, 0:(qb + 1) * P].rearrange("p (k q) -> p k q", q=P), ACT.Copy)\
                        .then_inc(pt_used, 1)
                exp(0)
                exp(1)
                pt(0)
                exp(2)
                pt(1)
                exp(3)
                pt(2)
                pt(3)
                act.wait_ge(pv_mm, hd + 1)
                if hd == 0:
                    act.wait_ge(unit_done, unit_end("uq", 1))
                nc.scalar.activation(AH[:, hd, 0:TP], bank[7][:, 0:TP], ACT.Copy).then_inc(a_hi, 1)

            with act.Fori(0, NS) as i:
                for kt in range(16):
                    act.wait_ge(page_mm, kt + 1 + 16 * i)
                    act.wait_ge(qk_mm, kt + 1 + 16 * i)
                    nc.scalar.activation(KTS[:, kt % 2, 0:CL], bank[4 + kt % 2][:, 0:CL], ACT.Copy).then_inc(page_c, 1)
                act.wait_ge(new_nat, 1 + i)
                nc.scalar.activation(flat["sq"][0:TQ, 0:CL], bank[3][0:TQ, 0:CL], ACT.Copy).then_inc(new_nat_c, 1)
                act.wait_ge(sm_step, 11 + SM * i)
                nc.scalar.activation(PS[:, 0:16, :], PS[:, 0:16, :], ACT.Exp, scale=SCALE).then_inc(prob, 1)
                nc.scalar.activation(PS[0:TQ, 16, :], PS[0:TQ, 16, :], ACT.Exp, scale=SCALE).then_inc(prob, 1)
            act.wait_ge(lat_out, 1 + NS)
            hi(DENSE0["uv"])
            nc.scalar.activation(BH[:, :, 0:TP], QLAT[:, :, :], ACT.Copy).then_inc(b_hi, 1)
            for hd in range(NH):
                if hd % 4 == 0:
                    hi(DENSE0["uv"] + hd // 4 + 1)
                act.wait_ge(uv_mm, hd + 1)
                nc.scalar.activation(AH[:, hd, TP:T], bank[hd % 4][:, 0:TS], ACT.Copy).then_inc(a_hi, 1)
            hi_steps("wo")
            after_mixer("y1", "ff1", "x3")
            mlp(1)

            for b, (t0, n) in enumerate(tokens):
                act.wait_ge(y_turned, 2 * b + 1)
                if b >= 2:
                    act.wait_ge(y_out[b % 2], 16 * (b // 2))
                nc.scalar.activation(yflat[0:n, (b % 2) * D:(b % 2) * D + 512], bank[4 + 2 * (b % 2)][0:n, 0:512],
                                     ACT.Copy).then_inc(y_copied_a, 1)
                act.wait_ge(y_copied_a, b + 1)
                act.wait_ge(y_copied_v, b + 1)
                dst = io["y_prompt"][0, t0:t0 + n] if b < 4 else io["y_sample"].rearrange("s t c -> (s t) c")
                act.dma_start(dst, yflat[0:n, (b % 2) * D:(b % 2) * D + D]).then_inc(y_out[b % 2], 16)
            act.wait_ge(y_out[0], 16 * 3)
            act.wait_ge(y_out[1], 16 * 2)
            act.wait_ge(kv_out, 32 * 5)
            for q in state_out_sem:
                act.wait_ge(q, 16 * len(STATES) // 2)

        @block.gpsimd
        def _(pool):
            def lo(d, i=None):
                pool.wait_ge(hi_done, d + 1 + (0 if i is None else RING * i))
                n = slab_size(d)
                nc.gpsimd.tensor_tensor(WL[:, d % WRING, 0:n], raw_of(d), WH[:, d % WRING, 0:n].bitcast(F32),
                                        ALU.subtract).then_inc(lo_done, 1)

            def add(st, h, m, src, own=True):
                if st == "lm":
                    pass
                else:
                    pool.wait_ge(sq_done, SQ(st, h, m))
                    src = sq[:, SQ(st, h, m) % 2, :]
                if m == 0:
                    before = [k for k in SUMS[:SUMS.index((st, h))] if k[1] == h]
                    if before:
                        pool.wait_ge(rstd_done, RSTD(*before[-1]))
                    nc.gpsimd.tensor_copy(acc[:, h, :], src).then_inc(acc_done, 1)
                else:
                    pool.wait_ge(acc_done, ACC(st, h, m - 1))
                    nc.gpsimd.tensor_tensor(acc[:, h, :], acc[:, h, :], src, ALU.add).then_inc(acc_done, 1)

            def scale(st, h, m, src):
                if m == 0:
                    pool.wait_ge(rstd_done, RSTD(NORM_OF.get(st, st), h))
                before = prev(SC, (st, h, m), 2)
                if before:
                    s, v = scaled_read(before)
                    pool.wait_ge(s, v)
                nc.gpsimd.tensor_tensor(scaled[:, SC(st, h, m) % 2, :], src, R2[:, h, :], ALU.mult).then_inc(sc_done, 1)

            nc.gpsimd.memset(ones[:], 1.0).then_inc(ones_set, 1)
            nc.gpsimd.memset(eps[:], EPS).then_inc(ones_set, 1)
            nc.gpsimd.memset(V[:, :, 0:CW - 1], 0.0).then_inc(ones_set, 1)
            for s, n in ((bank_free, BANKS), (w_used, WRING), (v_done, 3), (u_lo, 2), (qk_mm, 2), (page_c, 2),
                         (page_r, 2), (lat_out, 1)):
                pool.sem_inc(s, n)
            lo(0)
            for h in range(2):
                for m in range(KT):
                    add("x0", h, m, None)

            pool.wait_ge(unturned_v, 13)
            pool.wait_ge(unturned_a, 13)
            with pool.Fori(0, 2) as i:
                for j in range(4):
                    lo(j + 1, i)
                    vm = V[:, bass.ds(4 * i + j, 1), :]
                    pool.wait_ge(gate_sig, 2 * j + 1 + 8 * i)
                    nc.gpsimd.tensor_tensor(vm[:, 0, CW - 1:CW - 1 + H], scaled[:, 0, :], prod[:, 0, :], ALU.mult)\
                        .then_inc(v_done, 1)
                    pool.wait_ge(gate_sig, 2 * j + 2 + 8 * i)
                    nc.gpsimd.tensor_tensor(vm[:, 0, CW - 1 + H:VP], scaled[:, 1, 0:TP - H], prod[:, 1, 0:TP - H],
                                            ALU.mult).then_inc(v_done, 1)
                    nc.gpsimd.tensor_tensor(
                        vm[:, 0, VP:VW].rearrange("p (s c) -> p s c", s=NS)[:, :, CW - 1:VSQ],
                        scaled[:, 1, TP - H:H].rearrange("p (s c) -> p s c", s=NS),
                        prod[:, 1, TP - H:H].rearrange("p (s c) -> p s c", s=NS), ALU.mult).then_inc(v_done, 1)
            for h in range(2):
                for m in range(KT):
                    pool.wait_ge(conv_step, 2 * CW * (m + 1))
                    add("lm", h, m, half(Y, m, h))
            for h in range(2):
                for m in range(KT):
                    add("lv", h, m, None)
                for m in range(KT):
                    scale("sw", h, m, half(Y, m, h))

            def lo_steps(phase):
                for j in range(SLABS[phase]):
                    lo(DENSE0[phase] + j + 1)

            def after_mixer(st, stx):
                for h in range(2):
                    for m in range(KT):
                        add(st, h, m, None)
                    for m in range(KT):
                        scale(st, h, m, half(Y, m, h))
                        if m:
                            add(stx, h, m - 1, None)
                    add(stx, h, KT - 1, None)
                    pool.wait_ge(sc_done, SC(st, h, KT - 1))
                    nc.gpsimd.memset(Y[:, :, h * H:(h + 1) * H], 0.0).then_inc(y_zero, 1)

            def mlp(layer):
                phase = f"mlp{layer}"
                d0, b0 = DENSE0[phase], UP * NCH * layer
                with pool.Fori(0, NCH) as i:
                    for j in range(4):
                        lo(d0 + j + 1, i)
                        if j < 2:
                            for k in range(4):
                                n, h, m = 4 * j + k, k // 2, 2 * j + k % 2
                                pool.wait_ge(u_hi, b0 + n + 1 + UP * i)
                                nc.gpsimd.tensor_tensor(half(BL, m, h), prod[:, n % 2, :], half(BH, m, h).bitcast(F32),
                                                        ALU.subtract).then_inc(u_lo, 1)
                st = f"m{layer}"
                for h in range(2):
                    for m in range(KT):
                        add(st, h, m, None)
                for h in range(2):
                    for m in range(KT):
                        scale(st, h, m, half(Y, m, h))
                lo(DENSE0[f"ple{layer}"] + 1)
                for j in range(4):
                    if DENSE0[f"gate{layer}"] + j + 1 < len(dense_slabs):
                        lo(DENSE0[f"gate{layer}"] + j + 1)

            lo_steps("pw2")
            after_mixer("y0", "x1")
            mlp(0)
            for h in range(2):
                for m in range(KT):
                    add("x2", h, m, None)
            lo_steps("dkv")
            lo_steps("dq")
            for h in range(2):
                for m in range(4):
                    add("ck", h, m, None)
            for h in range(2):
                for m in range(4):
                    scale("ck", h, m, half(CK, m, h))
            for h in range(2):
                for m in range(6):
                    add("cq", h, m, None)
            for h in range(2):
                for m in range(6):
                    scale("cq", h, m, half(Y, m, h))
            pool.wait_ge(ck_val, 8)
            nc.gpsimd.tensor_copy(CS[:, :, :], CK[:, :, TP:T]).then_inc(cs_done, 1)
            lo_steps("uq")
            lo_steps("kvh")
            lo_steps("uv")
            lo_steps("wo")
            after_mixer("y1", "x3")
            mlp(1)

        scratch = flat["acc"]
        NK, NKR = scratch[:, 0:32].rearrange("p (c t) -> p c t", c=4), scratch[0:DR, 32:40]
        MX0, MX1, MB = scratch[:, 64:128], scratch[:, 128:192], scratch[:, 192:256]
        LS, LI, SN = scratch[:, 256:320], scratch[:, 320:384], scratch[0:TQ, 384:448]
        MROW, DIAG = scratch[0:64, 448:449], scratch[0:64, 450:514]
        QS = flat["prod"][:, 0:256].rearrange("p (c q) -> p c q", c=4)
        QSR = flat["prod"][0:DR, 256:320]
        NEWC = flat["sq"][0:TQ, 0:CL]

        @block.vector
        def _(dve):
            steps = [0]

            def link(ins):
                steps[0] += 1
                ins.then_inc(dve_step, 1)
                dve.wait_ge(dve_step, steps[0])

            def lo(v, h, m, src):
                dve.wait_ge(a_hi, A(v, h, m))
                g = gain_of[v]
                if g:
                    nc.vector.scalar_tensor_tensor(out=half(AL, m, h), in0=src, scalar=gain(g, m),
                                                   in1=half(AH, m, h).bitcast(F32), op0=ALU.mult, op1=ALU.subtract)\
                        .then_inc(a_lo, 1)
                else:
                    nc.vector.tensor_tensor(half(AL, m, h), src, half(AH, m, h).bitcast(F32), ALU.subtract)\
                        .then_inc(a_lo, 1)

            def row(st, h):
                dve.wait_ge(sum_done, SUM(st, h))
                f = R1[:, h, :]
                if st in ("m0", "m1"):
                    link(nc.vector.tensor_tensor(acc[:, h, :], f, f, ALU.mult))
                    f = acc[:, h, :]
                link(nc.vector.tensor_tensor(R2[:, h, :], f, f, ALU.mult))
                nc.vector.tensor_tensor(root[:, h, :], bank[4 + h][:, 0:H], R2[:, h, :], ALU.mult).then_inc(row_step, 1)

            def rstd(st, h):
                dve.wait_ge(root_done, ROOT(st, h))
                if st in SCALED_BY_INPUT:
                    link(nc.vector.reciprocal(root[:, h, :], root[:, h, :]))
                    f = acc[:, h, :] if st in ("m0", "m1") else R1[:, h, :]
                    nc.vector.tensor_tensor(R2[:, h, :], root[:, h, :], f, ALU.mult).then_inc(rstd_done, 1)
                else:
                    r = R1 if st[0] == "x" else R2
                    nc.vector.reciprocal(r[:, h, :], root[:, h, :]).then_inc(rstd_done, 1)

            def update(st, h, post, v):
                for m in range(KT + 1):
                    if m < KT:
                        dve.wait_ge(sc_done, SC(st, h, m))
                        nc.vector.scalar_tensor_tensor(out=half(X, m, h), in0=scaled[:, SC(st, h, m) % 2, :],
                                                       scalar=gain(post, m), in1=half(X, m, h), op0=ALU.mult,
                                                       op1=ALU.add).then_inc(x_done, 1)
                    if m:
                        lo(v, h, m - 1, half(X, m - 1, h))

            def evacuate(phase, dst, units):
                for n, (h, m) in enumerate(units):
                    u = UNIT0[phase] + n
                    dve.wait_ge(unit_done, u + 1)
                    nc.vector.tensor_copy(dst(h, m), bank[u % BANKS][:, 0:H]).then_inc(bank_free, 1)

            pairs = [(h, 2 * j + t) for j in range(4) for h in range(2) for t in range(2)]

            for e in range(0, 26, 2):
                dve.wait_ge(turned, e + 1)
                src = bank[4 + e % 4]
                if e == 0:
                    nc.vector.tensor_copy(gains[:, :], src[:, 0:NG]).then_inc(unturned_v, 1)
                elif e < 18:
                    nc.vector.tensor_copy(X[:, (e - 2) // 2, 0:TP], src[:, 0:TP]).then_inc(unturned_v, 1)
                else:
                    nc.vector.tensor_copy(V[:, e - 18, VP:VW].rearrange("p (s c) -> p s c", s=NS)[:, :, 0:CW - 1],
                                          src[:, 0:2 * SG].rearrange("p (s c) -> p s c", s=NS)).then_inc(unturned_v, 1)
            dve.wait_ge(unturned_v, 13)
            dve.wait_ge(unturned_a, 13)
            for h in range(2):
                for m in range(KT):
                    lo("x0", h, m, half(X, m, h))
            for h in range(2):
                rstd("x0", h)
            dve.wait_ge(rstd_done, 2)

            with dve.Fori(0, 2) as i:
                for j in range(4):
                    for h in range(2):
                        for t, buf in enumerate((scaled, prod)):
                            n = 4 * j + 2 * h + t
                            dve.wait_ge(unit_done, n + 1 + 16 * i)
                            if t == 0:
                                dve.wait_ge(v_done, 3 * j + 1 + 2 * h + 12 * i)
                            nc.vector.tensor_tensor(buf[:, h, :], bank[n % BANKS][:, 0:H], R1[:, h, :], ALU.mult)\
                                .then_inc(bank_free, 1)
                    vm = V[:, bass.ds(4 * i + j, 1), :]
                    ym = Y[:, bass.ds(4 * i + j, 1), :]
                    gm = gains[:, bass.ds(GCOL["dw_bias"] + 4 * i + j, 1)]
                    wm = taps[:, bass.ds(4 * i + j, 1), :]
                    dve.wait_ge(v_done, 3 * j + 6 + 12 * i)
                    for c in range(CW):
                        for part in range(2):
                            if part == 0:
                                dst, src = ym[:, 0, 0:TP], vm[:, 0, c:c + TP]
                            else:
                                dst = ym[:, 0, TP:T].rearrange("p (s t) -> p s t", s=NS)
                                src = vm[:, 0, VP:VW].rearrange("p (s c) -> p s c", s=NS)[:, :, c:c + TQ]
                            w = wm[:, 0, c:c + 1]
                            if c == 0:
                                nc.vector.tensor_scalar(dst, src, w, gm, ALU.mult, ALU.add).then_inc(conv_step, 1)
                            else:
                                dve.wait_ge(conv_step, 2 * CW * j + 2 * c + part - 1 + 8 * CW * i)
                                nc.vector.scalar_tensor_tensor(out=dst, in0=src, scalar=w, in1=dst, op0=ALU.mult,
                                                               op1=ALU.add).then_inc(conv_step, 1)
            dve.wait_ge(conv_step, 2 * CW * KT)

            for h in range(2):
                dve.wait_ge(sum_done, SUM("lm", h))
                nc.vector.tensor_scalar(R2[:, h, :], bank[4 + h][:, 0:H], 1.0 / D, None, ALU.mult).then_inc(rstd_done, 1)
            for h in range(2):
                dve.wait_ge(rstd_done, RSTD("lm", h))
                for m in range(KT):
                    nc.vector.tensor_tensor(half(Y, m, h), half(Y, m, h), R2[:, h, :], ALU.subtract).then_inc(centred, 1)
            dve.wait_ge(centred, 16)
            for h in range(2):
                rstd("lv", h)
                for m in range(KT + 1):
                    if m < KT:
                        n, k = KT * h + m, SC("sw", h, m) % 2
                        dve.wait_ge(sw_sig, n + 1)
                        nc.vector.tensor_scalar(scaled[:, k, :], scaled[:, k, :], gain("ln_g", m), gain("ln_b", m),
                                                ALU.mult, ALU.add).then_inc(sw_lin, 1)
                        dve.wait_ge(sw_lin, n + 1)
                        nc.vector.tensor_tensor(prod[:, n % 2, :], prod[:, n % 2, :], scaled[:, k, :], ALU.mult)\
                            .then_inc(sw_val, 1)
                    if m:
                        lo("sw", h, m - 1, prod[:, (n if m == KT else n - 1) % 2, :])

            def after_mixer(phase, st, post, v, stx):
                evacuate(phase, lambda h, m: half(Y, m, h), pairs)
                for h in range(2):
                    rstd(st, h)
                    update(st, h, post, v)

            def mlp(layer):
                phase, v = f"mlp{layer}", f"g{layer}"
                u0, b0 = UNIT0[phase], UP * NCH * layer
                dve.wait_ge(y_zero, 2 * layer + 2)
                with dve.Fori(0, NCH) as i:
                    for n in range(UP):
                        dve.wait_ge(relu_done, b0 + n + 1 + UP * i)
                        dve.wait_ge(u_lo, b0 + n + 1 + UP * i)
                        nc.vector.tensor_tensor(prod[:, n % 2, :], scaled[:, n % 2, :], bank[(u0 + n) % BANKS][:, 0:H],
                                                ALU.mult).then_inc(bank_free, 1)
                    for n in range(UP, CHUNK):
                        k = n - UP
                        h, m = (k % 8) // 4, 4 * (k // 8) + k % 4
                        dve.wait_ge(unit_done, u0 + n + 1 + CHUNK * i)
                        nc.vector.tensor_tensor(half(Y, m, h), half(Y, m, h), bank[(u0 + n) % BANKS][:, 0:H], ALU.add)\
                            .then_inc(bank_free, 1)
                for h in range(2):
                    rstd(f"x{2 * layer + 1}", h)
                for e in range(4):
                    kt, part = e // 2, e % 2
                    a, b = (0, TP) if part == 0 else (TP, T)
                    dve.wait_ge(p_hi, 4 * layer + e + 1)
                    nc.vector.tensor_tensor(BL[:, kt, a:b], bank[6 + part][:, 0:b - a], BH[:, kt, a:b].bitcast(F32),
                                            ALU.subtract).then_inc(p_lo, 1)
                st = f"m{layer}"
                for h in range(2):
                    dve.wait_ge(rstd_done, RSTD(f"x{2 * layer + 1}", h))
                    row(st, h)
                    rstd(st, h)
                up = UNIT0[f"ple{layer}"]
                for h in range(2):
                    update(st, h, f"ff_post{layer}", v)
                    for m in range(KT):
                        u = up + 8 * h + m
                        dve.wait_ge(unit_done, u + 1)
                        nc.vector.tensor_copy(half(Y, m, h), bank[u % BANKS][:, 0:H]).then_inc(bank_free, 1)
                ug = UNIT0[f"gate{layer}"]
                for n, (h, m) in enumerate(GATE_ORDER):
                    u = ug + n
                    dve.wait_ge(sig_done, 16 * layer + n + 1)
                    nc.vector.tensor_tensor(scaled[:, n % 2, :], prod[:, n % 2, :], half(Y, m, h), ALU.mult)\
                        .then_inc(bank_free, 1)
                    dve.wait_ge(bank_free, freed(u))
                    nc.vector.tensor_tensor(half(X, m, h), half(X, m, h), scaled[:, n % 2, :], ALU.add)\
                        .then_inc(xg_done, 1)

            after_mixer("pw2", "y0", "mix_post0", "ff0", "x1")
            mlp(0)

            for h in range(2):
                for m in range(KT):
                    lo("kv", h, m, half(X, m, h))
            krow = [(h, 4) for h in range(2)]
            evacuate("dkv", lambda h, m: half(CK, m, h) if m < 4 else KR[:, h * H:(h + 1) * H], pairs[:8] + krow)
            for h in range(2):
                rstd("x2", h)
            dve.wait_ge(rstd_done, RSTD("x2", 1))
            r1 = R1[:, :, :].rearrange("p a b -> p (a b)")
            dve.wait_ge(bank_free, freed(UNIT0["dkv"] + 9))
            link(nc.vector.tensor_tensor(KR, KR, r1, ALU.mult))
            for h in range(2):
                for m in range(KT):
                    lo("mx", h, m, half(X, m, h))
            evacuate("dq", lambda h, m: half(Y, m, h), pairs[:12])
            for h in range(2):
                row("ck", h)
                rstd("ck", h)
            for h in range(2):
                for m in range(4):
                    dve.wait_ge(sc_done, SC("ck", h, m))
                    nc.vector.tensor_scalar(half(CK, m, h), scaled[:, SC("ck", h, m) % 2, :], gain("kv_norm", m), None,
                                            ALU.mult).then_inc(ck_val, 1)
            for h in range(2):
                for m in range(4):
                    dve.wait_ge(b_hi, 4 * h + m + 1)
                    nc.vector.tensor_tensor(half(BL, m, h), half(CK, m, h), half(BH, m, h).bitcast(F32),
                                            ALU.subtract).then_inc(b_lo, 1)
            for h in range(2):
                row("cq", h)
                rstd("cq", h)
            for h in range(2):
                for m in range(6):
                    lo("cq", h, m, scaled[:, SC("cq", h, m) % 2, :])

            def rotate(n, t):
                dve.wait_ge(rot_done, n + 1)
                for b, c0, c1 in ((6, 0, TP), (7, TP, T)):
                    nc.vector.tensor_tensor(flat["prod"][:, c0:c1], bank[b][:, 0:c1 - c0], SIN[:, c0:c1], ALU.mult)\
                        .then_inc(rope_step, 1)
                nc.vector.tensor_tensor(t, t, COS, ALU.mult).then_inc(rope_step, 1)
                dve.wait_ge(rope_step, 4 * n + 3)
                nc.vector.tensor_tensor(t, t, flat["prod"][:, 0:T], ALU.add).then_inc(rope_step, 1)
                dve.wait_ge(rope_step, 4 * n + 4)

            dve.wait_ge(rope_in, 16)
            rotate(0, KR)
            for n, (h, m) in enumerate(pairs + pairs[:8]):
                u = UNIT0["uq"] + n
                dve.wait_ge(unit_done, u + 1)
                dst = half(Y, m, h) if n < 16 else half(QR, m, h)
                nc.vector.tensor_copy(dst, bank[u % BANKS][:, 0:H]).then_inc(bank_free, 1)
            dve.wait_ge(bank_free, freed(UNIT0["uq"] + 23))
            for j in range(4):
                rotate(1 + j, QR[:, j, :])
            dve.wait_ge(qrs_mm, 1)
            nc.vector.tensor_copy(QRS.rearrange("p (s h t) -> p h s t", s=NS, h=NH),
                                  bank[5][0:DR, 0:512].rearrange("p (h s t) -> p h s t", s=NS, h=NH)).then_inc(qrs_c, 1)

            dve.wait_ge(consts, 48)
            dve.wait_ge(kv_out, 32 * 5)
            for hd in range(NH):
                dve.wait_ge(v_mm, hd + 1)
                if hd:
                    dve.wait_ge(pv_mm, hd)
                nc.vector.tensor_copy(vn, bank[1][:, 0:TP]).then_inc(v_used, 1)
                dve.wait_ge(uk_mm, hd + 1)
                if hd:
                    dve.wait_ge(ql_mm, hd)
                nc.vector.tensor_copy(ukT, bank[2][:, 0:CL]).then_inc(uk_used, 1)
                dve.wait_ge(ql_mm, hd + 1)
                nc.vector.tensor_copy(QLAT.rearrange("p c (s h t) -> p c s h t", s=NS, h=NH)[:, :, :, hd, :],
                                      bank[3][:, 0:256].rearrange("p (c s t) -> p c s t", c=4, s=NS))\
                    .then_inc(ql_used, 1)

                def top(qb):
                    n, c = 4 * hd + qb, 4 * ((4 * hd + qb) % 2)
                    b = bank[4 + n % 2]
                    dve.wait_ge(s_mm, n + 1)
                    nc.vector.tensor_tensor(b[:, qb * P:(qb + 1) * P], b[:, qb * P:(qb + 1) * P], cmask, ALU.add)\
                        .then_inc(s_masked, 1)
                    dve.wait_ge(s_masked, n + 1)
                    nc.vector.tensor_reduce(tiny[:, c:c + 1], b[:, 0:(qb + 1) * P], AX.X, ALU.max).then_inc(s_max, 1)
                    dve.wait_ge(s_max, 2 * n + 1)
                    nc.vector.tensor_scalar(tiny[:, c + 1:c + 2], tiny[:, c:c + 1], -SCALE, None, ALU.mult)\
                        .then_inc(s_max, 1)

                def norm(qb):
                    n, c = 4 * hd + qb, 4 * ((4 * hd + qb) % 2)
                    dve.wait_ge(s_exp, n + 1)
                    nc.vector.reciprocal(tiny[:, c + 3:c + 4], tiny[:, c + 2:c + 3]).then_inc(s_rec, 1)
                    dve.wait_ge(s_rec, n + 1)
                    w = (qb + 1) * P
                    nc.vector.tensor_scalar(PB[n % 2][:, 0:w], PB[n % 2][:, 0:w], tiny[:, c + 3:c + 4], None,
                                            ALU.mult).then_inc(p_ready, 1)
                top(0)
                top(1)
                norm(0)
                top(2)
                norm(1)
                top(3)
                norm(2)
                norm(3)
                dve.wait_ge(a_hi, A("o", 0, hd))
                nc.vector.tensor_tensor(AL[:, hd, 0:TP], bank[7][:, 0:TP], AH[:, hd, 0:TP].bitcast(F32), ALU.subtract)\
                    .then_inc(a_lo, 1)

            dve.wait_ge(cs_done, 1)
            dve.wait_ge(ql_used, NH)
            with dve.Fori(0, NS) as i:
                dve.wait_ge(lat_out, 1 + i)
                nc.vector.tensor_copy(NK, CS[:, :, bass.ds(TQ * i, TQ)]).then_inc(new_in, 1)
                nc.vector.tensor_copy(NKR, KR[0:DR, bass.ds(TP + TQ * i, TQ)]).then_inc(new_in, 1)
                nc.vector.tensor_copy(QS, QLAT[:, :, bass.ds(64 * i, 64)]).then_inc(new_in, 1)
                nc.vector.tensor_copy(QSR, QRS[:, bass.ds(64 * i, 64)]).then_inc(new_in, 1)
                for kt in range(16):
                    dve.wait_ge(page_mm, kt + 1 + 16 * i)
                    dve.wait_ge(qk_mm, kt + 1 + 16 * i)
                    nc.vector.tensor_copy(KTS[0:DR, kt % 2, CL:CL + P], bank[6 + kt % 2][0:DR, 0:P]).then_inc(page_r, 1)

                def step(n, ins):
                    ins.then_inc(sm_step, 1)

                dve.wait_ge(new_mm, 1 + i)
                step(1, nc.vector.tensor_tensor(SN, bank[2][0:TQ, 0:64], nmask, ALU.add))
                dve.wait_ge(qk_mm, 16 + 2 + 16 * i)
                for b, mx in ((0, MX0), (1, MX1)):
                    step(2 + b, nc.vector.tensor_reduce(mx, bank[b][:, 0:512].rearrange("p (k q) -> p q k", q=64), AX.X,
                                                        ALU.max))
                dve.wait_ge(sm_step, 3 + SM * i)
                step(4, nc.vector.tensor_tensor(MX0, MX0, MX1, ALU.max))
                dve.wait_ge(sm_step, 4 + SM * i)
                step(5, nc.vector.tensor_tensor(MX0[0:TQ], MX0[0:TQ], SN, ALU.max))
                dve.wait_ge(max_t, 1 + i)
                step(6, nc.vector.tensor_reduce(MROW, bank[6][0:64, 0:P], AX.X, ALU.max))
                dve.wait_ge(sm_step, 6 + SM * i)
                step(7, nc.vector.tensor_scalar(DIAG, ident[0:64, 0:64], MROW, None, ALU.mult))
                dve.wait_ge(max_b, 1 + i)
                step(8, nc.vector.tensor_copy(MB, bank[7][:, 0:64]))
                dve.wait_ge(sm_step, 8 + SM * i)
                for b in range(2):
                    step(9 + b, nc.vector.tensor_tensor(
                        PS[:, 8 * b:8 * b + 8, :], bank[b][:, 0:512].rearrange("p (k q) -> p k q", q=64),
                        MB.rearrange("p (a q) -> p a q", a=1).to_broadcast([P, 8, 64]), ALU.subtract))
                step(11, nc.vector.tensor_tensor(PS[0:TQ, 16, :], SN, MB[0:TQ], ALU.subtract))
                dve.wait_ge(prob, 2 + 2 * i)
                step(12, nc.vector.tensor_reduce(LS, PS[:, 0:16, :].rearrange("p k q -> p q k"), AX.X, ALU.add))
                dve.wait_ge(den_b, 1 + i)
                step(13, nc.vector.reciprocal(LI, bank[6][:, 0:64]))
                dve.wait_ge(sm_step, 13 + SM * i)
                dve.wait_ge(out_mm, 1 + i)
                nc.vector.tensor_tensor(QLAT[:, :, bass.ds(64 * i, 64)],
                                        bank[3][:, 0:256].rearrange("p (c q) -> p c q", c=4),
                                        LI.rearrange("p (a q) -> p a q", a=1).to_broadcast([P, 4, 64]), ALU.mult)\
                    .then_inc(lat_out, 1)
            dve.wait_ge(b_hi, 9)
            nc.vector.tensor_tensor(BL[:, :, 0:TP], QLAT[:, :, :], BH[:, :, 0:TP].bitcast(F32), ALU.subtract)\
                .then_inc(b_lo, 1)
            for hd in range(NH):
                dve.wait_ge(a_hi, A("o", 1, hd))
                nc.vector.tensor_tensor(AL[:, hd, TP:T], bank[hd % 4][:, 0:TS], AH[:, hd, TP:T].bitcast(F32),
                                        ALU.subtract).then_inc(a_lo, 1)
            after_mixer("wo", "y1", "mix_post1", "ff1", "x3")
            mlp(1)
            for b, (t0, n) in enumerate(tokens):
                dve.wait_ge(y_turned, 2 * b + 2)
                if b >= 2:
                    dve.wait_ge(y_out[b % 2], 16 * (b // 2))
                nc.vector.tensor_copy(yflat[0:n, (b % 2) * D + 512:(b % 2) * D + D], bank[5 + 2 * (b % 2)][0:n, 0:512])\
                    .then_inc(y_copied_v, 1)

        @block.tensor
        def _(pe):
            def three(out, wsl, hl, first, last, kslices):
                (wh, wl), (xh, xl) = wsl, hl
                nc.tensor.matmul(out, wh, xh, start=first, stop=False)
                nc.tensor.matmul(out, wh, xl, start=False, stop=False)
                return nc.tensor.matmul(out, wl, xh, start=False, stop=last)

            def wslab(d, kt, n, k, c):
                a = k * n + c
                return WH[:, d % WRING, a:a + P], WL[:, d % WRING, a:a + P]

            def ab(hi_t, lo_t, k, h):
                return half(hi_t, k, h), half(lo_t, k, h)

            def unit(u, d, kt, n, c, h, src, ready=None, i=None, per_iter=0, last_of_slab=False):
                b = bank[u % BANKS][:, 0:H]
                pe.wait_ge(bank_free, u + 1 if i is None else u + 1 + per_iter * i)
                for k in range(kt):
                    if ready:
                        ready(k)
                    ins = three(b, wslab(d, kt, n, k, c), ab(*src, k, h), k == 0, k == kt - 1, None)
                ins.then_inc(unit_done, 1)

            def slab_ready(d, i=None):
                pe.wait_ge(lo_done, d + 1 if i is None else d + 1 + RING * i)

            def slab_used(d):
                pe.wait_ge(unit_done, 0)

            Asrc, Bsrc = (AH, AL), (BH, BL)

            def total(st, h):
                pe.wait_ge(acc_done, ACC(st, h, NT[st] - 1))
                before = [k for k in SUMS[:SUMS.index((st, h))] if k[1] == h]
                if before:
                    pe.wait_ge(rstd_done, RSTD(*before[-1]))
                nc.tensor.matmul(bank[4 + h][:, 0:H], ones[:, :], acc[:, h, :], start=True, stop=True)\
                    .then_inc(sum_done, 1)

            def product(phase, kt, n, tiles, v, slabs=None, src=None):
                u = UNIT0[phase]
                for j in range(SLABS[phase]):
                    d = DENSE0[phase] + j
                    slab_ready(d)
                    w = n[j] if isinstance(n, tuple) else n
                    nt = w // P if phase not in ("dkv",) else w // P
                    for h in range(2):
                        for t in range(nt):
                            def ready(k, h=h):
                                if v and j == 0 and t == 0:
                                    pe.wait_ge(a_lo, A(v, h, k))
                            b = bank[u % BANKS][:, 0:H]
                            pe.wait_ge(bank_free, u + 1)
                            for k in range(kt):
                                ready(k)
                                ins = three(b, wslab(d, kt, w, k, t * P), ab(*(src or Asrc), k, h), k == 0,
                                            k == kt - 1, None)
                            ins.then_inc(unit_done, 1)
                            u += 1
                    pe.wait_ge(unit_done, u)
                    pe.sem_inc(w_used, 1)

            pe.wait_ge(consts, 16)
            pe.wait_ge(x_in, 80)
            pe.wait_ge(vecs, 16 * (len(GAINS) + 3))
            for e in range(26):
                if e >= 4:
                    s = unturned_v if e % 2 == 0 else unturned_a
                    pe.wait_ge(s, e // 2 - 1)
                dst = bank[4 + e % 4]
                if e == 0:
                    ins = nc.tensor.transpose(dst[:, 0:NG], flat["prod"][0:NG, 0:P], ident[0:NG, 0:NG])
                elif e == 1:
                    for m in range(KT):
                        ins = nc.tensor.transpose(dst[:, m * CW:(m + 1) * CW], taps_stage[0:CW, m * P:(m + 1) * P],
                                                  ident[0:CW, 0:CW])
                elif e < 18:
                    m = (e - 2) // 2
                    if e % 2 == 0:
                        for b in range(4):
                            ins = nc.tensor.transpose(dst[:, b * P:(b + 1) * P],
                                                      yflat[:, b * D + m * P:b * D + (m + 1) * P], ident[:, :])
                    else:
                        ins = nc.tensor.transpose(dst[:, 0:TS], x_stage[0:TS, m * P:(m + 1) * P], ident[0:TS, 0:TS])
                else:
                    m = e - 18
                    for g in range(2):
                        ins = nc.tensor.transpose(dst[:, g * SG:(g + 1) * SG], state_stage[0:SG, g, m * P:(m + 1) * P],
                                                  ident[0:SG, 0:SG])
                ins.then_inc(turned, 1)
            pe.wait_ge(ones_set, 3)
            for h in range(2):
                total("x0", h)

            with pe.Fori(0, 2) as i:
                for j in range(4):
                    slab_ready(j, i)
                    for h in range(2):
                        for t in range(2):
                            u = 4 * j + 2 * h + t
                            pe.wait_ge(bank_free, u + 1 + 16 * i)
                            for k in range(KT):
                                if j == 0 and t == 0:
                                    pe.wait_ge(a_lo, A("x0", h, k))
                                ins = three(bank[u % BANKS][:, 0:H], wslab(j, KT, 256, k, t * P), ab(*Asrc, k, h),
                                            k == 0, k == KT - 1, None)
                            ins.then_inc(unit_done, 1)
                    pe.wait_ge(unit_done, 4 * j + 4 + 16 * i)
                    pe.sem_inc(w_used, 1)
            pe.wait_ge(rstd_done, RSTD("x0", 1))
            for e, (m, g) in enumerate(STATES):
                pe.wait_ge(v_done, 3 * KT + 3 if m is None else 3 * m + 6)
                if e >= 4:
                    pe.wait_ge(state_copied, e - 3)
                for q in range(4):
                    if m is None:
                        rows = V[:, 4 * g + q, TP:VP]
                    else:
                        a = VP + (4 * g + q) * VSQ + TQ
                        rows = V[:, m, a:a + CW - 1]
                    ins = nc.tensor.transpose(bank[4 + e % 4][0:CW - 1, q * P:(q + 1) * P], rows, ident[:, :])
                ins.then_inc(state_done, 1)
            pe.wait_ge(state_copied, len(STATES))
            for st in ("lm", "lv"):
                for h in range(2):
                    total(st, h)
            product("pw2", KT, 256, 2, "sw")
            for h in range(2):
                total("y0", h)

            def mlp(layer):
                phase = f"mlp{layer}"
                d0, u0, b0 = DENSE0[phase], UNIT0[phase], UP * NCH * layer
                with pe.Fori(0, NCH) as i:
                    n = 0
                    for j in range(4):
                        slab_ready(d0 + j, i)
                        for h in range(2):
                            for t in range(2 if j < 2 else 4):
                                pe.wait_ge(bank_free, u0 + n + 1 + CHUNK * i)
                                dst = bank[(u0 + n) % BANKS][:, 0:H]
                                for k in range(KT if j < 2 else FC):
                                    if j == 0 and t == 0:
                                        pe.wait_ge(a_lo, A(f"ff{layer}", h, k))
                                    if j == 2 and t == 0:
                                        pe.wait_ge(u_lo, b0 + up_n(h, k) + 3 + UP * i)
                                    if j < 2:
                                        ins = three(dst, wslab(d0 + j, KT, 256, k, t * P), ab(*Asrc, k, h), k == 0,
                                                    k == KT - 1, None)
                                    else:
                                        ins = three(dst, wslab(d0 + j, FC, 512, k, t * P), ab(*Bsrc, k, h), k == 0,
                                                    k == FC - 1, None)
                                ins.then_inc(unit_done, 1)
                                n += 1
                        pe.wait_ge(unit_done, u0 + n + CHUNK * i)
                        pe.sem_inc(w_used, 1)
                for h in range(2):
                    total(f"x{2 * layer + 1}", h)
                pe.wait_ge(p_in, 80 * (layer + 1))
                for e in range(4):
                    kt, part = e // 2, e % 2
                    if e >= 2:
                        pe.wait_ge(p_lo, 4 * layer + e - 1)
                    if part == 0:
                        for b in range(4):
                            ins = nc.tensor.transpose(bank[6][:, b * P:(b + 1) * P], p_stage[:, b, kt * P:(kt + 1) * P],
                                                      ident[:, :])
                    else:
                        ins = nc.tensor.transpose(bank[7][:, 0:TS], p_stage[0:TS, 4, kt * P:(kt + 1) * P],
                                                  ident[0:TS, 0:TS])
                    ins.then_inc(p_turned, 1)
                for h in range(2):
                    total(f"m{layer}", h)
                pe.wait_ge(p_lo, 4 * layer + 4)
                product(f"ple{layer}", 2, D, 8, None, src=Bsrc)
                product(f"gate{layer}", KT, 256, 2, f"g{layer}")

            mlp(0)
            product("dkv", KT, (256, 256, 128), 2, "kv")
            for h in range(2):
                total("x2", h)
            product("dq", KT, 256, 2, "mx")
            for st in ("ck", "cq"):
                for h in range(2):
                    total(st, h)

            def rot(n, t):
                if n:
                    pe.wait_ge(rope_step, 4 * n)
                nc.tensor.matmul(bank[6][:, 0:TP], ROT, t[:, 0:TP], start=True, stop=True)
                nc.tensor.matmul(bank[7][:, 0:TS], ROT, t[:, TP:T], start=True, stop=True).then_inc(rot_done, 1)

            pe.wait_ge(rope_in, 16)
            pe.wait_ge(dve_step, KR_STEP)
            rot(0, KR)
            u = UNIT0["uq"]
            for j in range(6):
                d = DENSE0["uq"] + j
                slab_ready(d)
                for h in range(2):
                    for t in range(2):
                        pe.wait_ge(bank_free, u + 1)
                        for k in range(6):
                            if j == 0 and t == 0:
                                pe.wait_ge(a_lo, A("cq", h, k))
                            ins = three(bank[u % BANKS][:, 0:H], wslab(d, 6, 256, k, t * P), ab(*Asrc, k, h), k == 0,
                                        k == 5, None)
                        ins.then_inc(unit_done, 1)
                        u += 1
                pe.wait_ge(unit_done, u)
                pe.sem_inc(w_used, 1)
                if j < 5:
                    t0, n = tokens[j]
                    pe.wait_ge(rope_step, 4)
                    pe.wait_ge(rstd_done, RSTD("cq", 1))
                    if j:
                        pe.wait_ge(kv_staged, 2 * j)
                    for c in range(4):
                        nc.tensor.transpose(bank[4][0:n, c * P:(c + 1) * P], CK[:, c, t0:t0 + n], ident[:, :])
                    nc.tensor.transpose(bank[5][0:n, 0:DR], KR[0:DR, t0:t0 + n], ident[0:DR, 0:DR])\
                        .then_inc(kv_turned, 1)
            pe.wait_ge(bank_free, freed(u - 1))
            for j in range(4):
                rot(1 + j, QR[:, j, :])
            pe.wait_ge(rope_step, 20)
            pe.wait_ge(kv_staged, 10)
            for h in range(NH):
                e = h % 2
                ins = nc.tensor.matmul(bank[5][0:DR, h * TS:(h + 1) * TS], ident[:, e * DR:(e + 1) * DR],
                                       QR[:, h // 2, TP:T], start=True, stop=True)
            ins.then_inc(qrs_mm, 1)

            pe.wait_ge(qrs_c, 1)
            for hd in range(NH):
                d = DENSE0["kvh"] + hd // 2
                slot = RAW[:, (RAW0["kvh"] + hd // 2) % RING]
                e = hd % 2
                if e == 0:
                    slab_ready(d)
                if hd:
                    pe.wait_ge(kvt_used, hd)
                    pe.wait_ge(v_used, hd)
                    pe.wait_ge(uk_used, hd)
                    pe.wait_ge(ql_used, hd)
                for k in range(4):
                    a = k * 256 + e * P
                    ins = three(bank[0][:, 0:TP], (WH[:, d % WRING, a:a + P], WL[:, d % WRING, a:a + P]),
                                (BH[:, k, 0:TP], BL[:, k, 0:TP]), k == 0, k == 3, None)
                ins.then_inc(kvt_done, 1)
                for kb in range(4):
                    for k in range(4):
                        a = 1024 + k * 256 + e * P
                        ins = three(bank[1][:, kb * P:(kb + 1) * P],
                                    (BH[:, k, kb * P:(kb + 1) * P], BL[:, k, kb * P:(kb + 1) * P]),
                                    (WH[:, d % WRING, a:a + P], WL[:, d % WRING, a:a + P]), k == 0, k == 3, None)
                ins.then_inc(v_mm, 1)
                if e == 1:
                    pe.wait_ge(v_mm, hd + 1)
                    pe.sem_inc(w_used, 1)
                for k in range(4):
                    a = k * 256 + e * P
                    ins = nc.tensor.transpose(bank[2][:, k * P:(k + 1) * P], slot[:, a:a + P], ident[:, :])
                ins.then_inc(uk_mm, 1)
                if e == 1:
                    pe.wait_ge(uk_mm, hd + 1)
                    pe.sem_inc(pe_read_raw, 1)
                pe.wait_ge(uk_used, hd + 1)
                for c in range(4):
                    ins = nc.tensor.matmul(bank[3][:, c * TS:(c + 1) * TS], ukT[:, c * P:(c + 1) * P], Y[:, hd, TP:T],
                                           start=True, stop=True)
                ins.then_inc(ql_mm, 1)

                def scores(qb):
                    n, w = 4 * hd + qb, (qb + 1) * P
                    if n >= 2:
                        pe.wait_ge(s_exp, n - 1)
                    r0 = DR * (hd % 2)
                    q = slice(qb * P, (qb + 1) * P)
                    dst = bank[4 + n % 2][:, 0:w]
                    nc.tensor.matmul(dst, Y[:, hd, q], kT[:, 0:w], start=True, stop=False)
                    nc.tensor.matmul(dst, QR[r0:r0 + DR, hd // 2, q], KR[r0:r0 + DR, 0:w], start=False, stop=True)\
                        .then_inc(s_mm, 1)

                def turn(qb):
                    n = 4 * hd + qb
                    pe.wait_ge(p_ready, n + 1)
                    if n:
                        pe.wait_ge(pt_used, n)
                    for k in range(qb + 1):
                        ins = nc.tensor.transpose(bank[6][:, k * P:(k + 1) * P], PB[n % 2][:, k * P:(k + 1) * P],
                                                  ident[:, :])
                    ins.then_inc(pt_mm, 1)
                pe.wait_ge(kvt_used, hd + 1)
                scores(0)
                scores(1)
                turn(0)
                scores(2)
                turn(1)
                scores(3)
                turn(2)
                turn(3)
                pe.wait_ge(pt_used, 4 * hd + 4)
                pe.wait_ge(v_used, hd + 1)
                if hd:
                    pe.wait_ge(a_lo, A("o", 0, hd - 1))
                for k in range(4):
                    ins = nc.tensor.matmul(bank[7][:, k * P:TP], vn[:, k * P:(k + 1) * P], PT[:, k, k * P:TP],
                                           start=k == 0, stop=k == 3)
                ins.then_inc(pv_mm, 1)

            pe.wait_ge(a_lo, A("o", 0, NH - 1))
            pe.wait_ge(ql_used, NH)
            g0 = RAW0["cache"]
            with pe.Fori(0, NS) as i:
                pe.wait_ge(lat_out, 1 + i)

                def page(kt):
                    j, q = kt // 4, kt % 4
                    if q == 0:
                        pe.wait_ge(landed[(g0 + j) % RING], LANDED[g0 + j] + 128 * i)
                    pe.wait_ge(page_c, kt + 1 + 16 * i)
                    pe.wait_ge(page_r, kt + 1 + 16 * i)
                    src = RAW[:, (g0 + j) % RING, q * 576:(q + 1) * 576]
                    for c in range(4):
                        nc.tensor.transpose(bank[4 + kt % 2][:, c * P:(c + 1) * P], src[:, c * P:(c + 1) * P], ident[:, :])
                    nc.tensor.transpose(bank[6 + kt % 2][0:DR, 0:P], src[:, CL:CL + DR], ident[:, :]).then_inc(page_mm, 1)

                def score(kt):
                    pe.wait_ge(page_c, kt + 3 + 16 * i)
                    pe.wait_ge(page_r, kt + 3 + 16 * i)
                    dst = bank[kt // 8][:, (kt % 8) * 64:(kt % 8 + 1) * 64]
                    for c in range(4):
                        nc.tensor.matmul(dst, KTS[:, kt % 2, c * P:(c + 1) * P], QS[:, c, :],
                                         start=c == 0, stop=False)
                    nc.tensor.matmul(dst, KTS[0:DR, kt % 2, CL:CL + P], QSR, start=False,
                                     stop=True).then_inc(qk_mm, 1)
                page(0)
                pe.wait_ge(new_in, 4 + 4 * i)
                for kt in range(16):
                    if kt < 15:
                        page(kt + 1)
                    score(kt)
                for c in range(4):
                    nc.tensor.matmul(bank[2][0:TQ, 0:64], NK[:, c, :], QS[:, c, :], start=c == 0,
                                     stop=False)
                nc.tensor.matmul(bank[2][0:TQ, 0:64], NKR, QSR, start=False, stop=True)\
                    .then_inc(new_mm, 1)
                for c in range(4):
                    ins = nc.tensor.transpose(bank[3][0:TQ, c * P:(c + 1) * P], NK[:, c, :], ident[:, :])
                ins.then_inc(new_nat, 1)
                pe.wait_ge(sm_step, 5 + SM * i)
                nc.tensor.transpose(bank[6][:, 0:P], scratch[:, 64:192], ident[:, :]).then_inc(max_t, 1)
                pe.wait_ge(sm_step, 7 + SM * i)
                nc.tensor.matmul(bank[7][:, 0:64], ones[0:64, :], DIAG, start=True, stop=True).then_inc(max_b, 1)
                pe.wait_ge(prob, 2 + 2 * i)
                pe.wait_ge(new_nat_c, 1 + i)
                for c in range(4):
                    dst = bank[3][:, c * 64:(c + 1) * 64]
                    nc.tensor.matmul(dst, NEWC[:, c * P:(c + 1) * P], PS[0:TQ, 16, :], start=True, stop=False)
                    for kt in range(16):
                        src = RAW[:, (g0 + kt // 4) % RING, (kt % 4) * 576:(kt % 4 + 1) * 576]
                        ins = nc.tensor.matmul(dst, src[:, c * P:(c + 1) * P], PS[:, kt, :], start=False, stop=kt == 15)
                        if c == 3 and kt % 4 == 3 and kt < 15:
                            ins.then_inc(pe_read_raw, 1)
                ins.then_inc(out_mm, 1)
                pe.wait_ge(sm_step, 12 + SM * i)
                nc.tensor.matmul(bank[6][:, 0:64], ones[:, :], LS, start=True, stop=False)
                nc.tensor.matmul(bank[6][:, 0:64], ones[0:TQ, :], PS[0:TQ, 16, :], start=False, stop=True)\
                    .then_inc(den_b, 1)
                pe.wait_ge(out_mm, 1 + i)
                pe.sem_inc(pe_read_raw, 1)
            pe.wait_ge(b_lo, 9)
            for hd in range(NH):
                d = DENSE0["uv"] + hd // 4
                if hd % 4 == 0:
                    slab_ready(d)
                if hd >= 4:
                    pe.wait_ge(a_lo, A("o", 1, hd - 4))
                for k in range(4):
                    a = k * 512 + (hd % 4) * P
                    rhs = [t[:, k, 0:TP].rearrange("p (s h t) -> p s h t", s=NS, h=NH)[:, :, hd, :] for t in (BH, BL)]
                    ins = three(bank[hd % 4][:, 0:TS].rearrange("p (s t) -> p s t", s=NS),
                                (WH[:, d % WRING, a:a + P], WL[:, d % WRING, a:a + P]), rhs, k == 0, k == 3, None)
                ins.then_inc(uv_mm, 1)
                if hd % 4 == 3:
                    pe.wait_ge(uv_mm, hd + 1)
                    pe.sem_inc(w_used, 1)
            pe.wait_ge(a_lo, A("o", 1, NH - 1))
            product("wo", KT, 256, 2, None)
            for h in range(2):
                total("y1", h)
            mlp(1)
            pe.wait_ge(xg_done, 32)
            for b, (t0, n) in enumerate(tokens):
                for q in range(2):
                    if b >= 2:
                        pe.wait_ge(y_copied_v if q else y_copied_a, b - 1)
                    for m in range(4):
                        ins = nc.tensor.transpose(bank[4 + 2 * (b % 2) + q][0:n, m * P:(m + 1) * P],
                                                  X[:, 4 * q + m, t0:t0 + n], ident[:, :])
                    ins.then_inc(y_turned, 1)


_INS = ["x_prompt", "x_sample", "state_conv", "cache_kv_latent", "cache_k_rope", "page_table", "p_prompt", "p_sample",
        "norm_mix_pre", "norm_mix_post", "norm_ff_pre", "norm_ff_post", "conv_pw1", "conv_dw", "conv_dw_bias",
        "conv_ln_g", "conv_ln_b", "conv_pw2", "kv_in_norm", "w_dkv", "kv_norm", "w_uk", "w_uv", "w_dq", "q_norm",
        "w_uq", "w_o", "w_up", "w_down", "ple_proj", "ple_gate"]
_OUTS = [("y_prompt", (1, TP, D)), ("y_sample", (NS, TQ, D)), ("new_conv_prompt", (1, 1, CW - 1, D)),
         ("new_conv_sample", (1, NS, CW - 1, D)), ("new_kv_prompt", (1, TP, CL)), ("new_kr_prompt", (1, TP, DR)),
         ("new_kv_sample", (NS, TQ, CL)), ("new_kr_sample", (NS, TQ, DR))]


def shape_constants():
    c = np.zeros((P, 1600), np.float32)
    c[:, 0:P] = np.eye(P)
    c[:, P:2 * P] = np.where(np.arange(P)[None, :] <= np.arange(P)[:, None], 0.0, NEG)
    new = np.where(np.arange(TQ)[:, None] <= np.arange(TQ)[None, :], 0.0, NEG)
    c[0:TQ, 256:320] = np.tile(new, (1, NH))
    hd = DR // 2
    freqs = (np.float32(1.0) / np.float32(10000.0) ** (np.arange(hd, dtype=np.float32) / np.float32(hd)))
    pos = np.concatenate([np.arange(TP), np.tile(PAGES * PAGE + np.arange(TQ), NS)]).astype(np.float32)
    ang = (pos[None, :] * freqs.astype(np.float32)[:, None]).astype(np.float32)
    c[:, 320:320 + T] = np.tile(np.cos(ang), (P // hd, 1))
    c[:, 896:896 + T] = np.tile(np.sin(ang), (P // hd, 1))
    for g in range(2):
        for r in range(hd):
            c[g * DR + hd + r, 1472 + g * DR + r] = -1.0
            c[g * DR + r, 1472 + g * DR + hd + r] = 1.0
    return c


def kernel(**inputs):
    import concourse.bacc as _bacc
    from concourse.bass_utils import run_bass_kernel_spmd as _run

    nc = _bacc.Bacc("TRN2", target_bir_lowering=False, num_devices=1)
    arrays, io = {}, {}
    for name in _INS:
        a = np.ascontiguousarray(inputs[name])
        arrays[f"in_{name}"] = a
        io[name] = nc.dram_tensor(f"in_{name}", a.shape, mybir.dt.from_np(a.dtype), kind="ExternalInput").ap()
    arrays["in_consts"] = shape_constants()
    io["consts"] = nc.dram_tensor("in_consts", (P, 1600), F32, kind="ExternalInput").ap()
    for name, shape in _OUTS:
        io[name] = nc.dram_tensor(f"out_{name}", shape, F32, kind="ExternalOutput").ap()
    decoder_step(nc, io)
    r = _run(nc, [arrays], core_ids=[0])
    return tuple(r.results[0][f"out_{name}"] for name, _ in _OUTS)
```

```python
from contextlib import ExitStack

import numpy as np

import concourse.bass as bass
from concourse import mybir

F32 = mybir.dt.float32
F32R = mybir.dt.float32r
I32 = mybir.dt.int32
ACT = mybir.ActivationFunctionType
ALU = mybir.AluOpType
AX = mybir.AxisListType

P = 128
D = 1024
KT = D // P
TP, TS = 512, 64
T = TP + TS
H = T // 2
NS, TQ = 8, 8
CW = 31
FF = 4 * D
FC = 4
NCH = FF // P // FC
PLE = 256
NH, DN, DR, DV = 8, 128, 64, 128
CL, QL = 512, 768
PAGES, PAGE = 16, 128
EPS = 1e-6
SCALE = (DN + DR) ** -0.5
NEG = -1e30
RING, WRING = 4, 2
SLOT = 4 * (CL + DR)
WSLOT = 2048
VP = TP + CW - 1
VSQ = TQ + CW - 1
VW = VP + NS * VSQ


class Order:

    def __init__(self, keys):
        self.at = {k: n + 1 for n, k in enumerate(keys)}

    def __call__(self, *key):
        return self.at[key]


PHASES = [("pw1", 8, KT, 2, 2), ("pw2", 4, KT, 2, 1), ("mlp0", 4 * NCH, 0, 0, 1), ("ple0", 1, 2, 8, 1),
          ("gate0", 4, KT, 2, 1), ("dkv", 3, KT, 2, (1, 1, 2)), ("dq", 3, KT, 2, 1),
          ("uq", 6, QL // P, 2, (2, 2, 2, 2, 4, 4)), ("kvh", 4, CL // P, 0, 2), ("cache", 32, 0, 0, 8), ("uv", 2, CL // P, 0, 1), ("wo", 4, KT, 2, 1),
          ("mlp1", 4 * NCH, 0, 0, 1), ("ple1", 1, 2, 8, 1), ("gate1", 4, KT, 2, 1)]
RAW0, DENSE0, UNIT0, UNITS = {}, {}, {}, {}
PARTS, KIND = [], []
_d = _u = 0
for _n, _s, _k, _t, _parts in PHASES:
    RAW0[_n], DENSE0[_n], UNIT0[_n] = len(PARTS), _d, _u
    PARTS += list(_parts) if isinstance(_parts, tuple) else [_parts] * _s
    KIND += [(_n, _j) for _j in range(_s)]
    _d += 0 if _n == "cache" else _s
    UNITS[_n] = {"mlp0": 24 * NCH, "mlp1": 24 * NCH, "dkv": 10}.get(_n, 2 * _t * _s)
    _u += UNITS[_n]
LANDED = [16 * sum(PARTS[g % RING:g + 1:RING]) for g in range(len(PARTS))]

STATS = [("x0", KT), ("lm", KT), ("lv", KT), ("y0", KT), ("x1", KT), ("m0", KT), ("x2", KT), ("ck", CL // P),
         ("cq", QL // P), ("y1", KT), ("x3", KT), ("m1", KT)]
NT = dict(STATS)
BLOCKS = [("x0", 0), ("x0", 1), ("lm", 0), ("lm", 1), ("lv", 0), ("lv", 1), ("y0", 0), ("x1", 0), ("y0", 1), ("x1", 1),
          ("m0", 0), ("m0", 1), ("x2", 0), ("x2", 1), ("ck", 0), ("ck", 1), ("cq", 0), ("cq", 1),
          ("y1", 0), ("x3", 0), ("y1", 1), ("x3", 1), ("m1", 0), ("m1", 1)]
SUMS = [("x0", 0), ("x0", 1), ("lm", 0), ("lm", 1), ("lv", 0), ("lv", 1), ("y0", 0), ("y0", 1), ("x1", 0), ("x1", 1),
        ("m0", 0), ("m0", 1), ("x2", 0), ("x2", 1), ("ck", 0), ("ck", 1), ("cq", 0), ("cq", 1),
        ("y1", 0), ("y1", 1), ("x3", 0), ("x3", 1), ("m1", 0), ("m1", 1)]
SQ = Order([(s, h, m) for s, h in BLOCKS if s != "lm" for m in range(NT[s])])
ACC = Order([(s, h, m) for s, h in BLOCKS for m in range(NT[s])])
SUM = Order(SUMS)
ROOT = Order([(s, h) for s, h in SUMS if s != "lm"])
SCALED_BY_INPUT = ("m0", "m1", "ck", "cq")
ROW = Order([(s, h) for s, h in SUMS if s in SCALED_BY_INPUT])
RSTD = SUM
SPLITS = [("x0", KT), ("sw", KT), ("ff0", KT), ("g0", KT), ("kv", KT), ("mx", KT), ("cq", QL // P), ("o", NH),
          ("ff1", KT), ("g1", KT)]
A = Order([(v, h, m) for v, n in SPLITS for h in range(2) for m in range(n)])
XS = ["y0", "m0", "y1", "m1"]
XU = Order([(s, h, m) for s in XS for h in range(2) for m in range(KT)])
GATE_ORDER = [(h, 2 * s + t) for s in range(4) for h in range(2) for t in range(2)]
XG = Order([(g, h, m) for g in range(2) for h, m in GATE_ORDER])
SC = Order([(s, h, m) for s in ("sw", "y0", "m0", "ck", "cq", "y1", "m1")
            for h in range(2) for m in range(NT.get(s, KT))])

GAINS = [("mix_pre0", KT), ("mix_pre1", KT), ("mix_post0", KT), ("mix_post1", KT), ("ff_pre0", KT), ("ff_pre1", KT),
         ("ff_post0", KT), ("ff_post1", KT), ("dw_bias", KT), ("ln_g", KT), ("ln_b", KT), ("kv_in", KT),
         ("kv_norm", CL // P), ("q_norm", QL // P)]
GCOL, _c = {}, 0
for _n, _t in GAINS:
    GCOL[_n] = _c
    _c += _t
NG = _c


EVACUATED = {"y0": "pw2", "y1": "wo", "m0": "mlp0", "m1": "mlp1", "ck": "dkv", "cq": "dq"}
BANKS = 4
UP = 8
CHUNK = 24


def unit_of(st, h, m):
    u0 = UNIT0[EVACUATED[st]]
    if st in ("m0", "m1"):
        return u0 + CHUNK * (NCH - 1) + UP + 8 * (m // 4) + 4 * h + m % 4
    return u0 + 4 * (m // 2) + 2 * h + m % 2


def freed(u):
    return BANKS + u + 1


def decoder_step(nc, io):
    with ExitStack() as ctx:
        def sb(name, shape, dt=F32):
            return ctx.enter_context(nc.sbuf_tensor(name, shape, dt))

        def sem(name):
            return ctx.enter_context(nc.semaphore(name))

        bank = [ctx.enter_context(nc.psum_tensor(f"bank{i}", [P, 512], F32)) for i in range(8)]
        X = sb("X", [P, KT, T])
        AH, AL = sb("AH", [P, KT, T], F32R), sb("AL", [P, KT, T], F32R)
        BH, BL = sb("BH", [P, FC, T], F32R), sb("BL", [P, FC, T], F32R)
        Y = sb("Y", [P, KT, T])
        RAW = sb("RAW", [P, RING, SLOT])
        WH, WL = sb("WH", [P, WRING, WSLOT], F32R), sb("WL", [P, WRING, WSLOT], F32R)
        R1, R2 = sb("R1", [P, 2, H]), sb("R2", [P, 2, H])
        acc, sq = sb("acc", [P, 2, H]), sb("sq", [P, 2, H])
        scaled, prod = sb("scaled", [P, 2, H]), sb("prod", [P, 2, H])
        root = sb("root", [P, 2, H])
        ident, ones = sb("ident", [P, P]), sb("ones", [P, P])
        gains = sb("gains", [P, NG])
        taps = sb("taps", [P, KT, CW])
        eps = sb("eps", [P, 1])
        tiny = sb("tiny", [P, 8])
        S = sb("S", [P, 8064])

        V = S[:, 0:KT * VW].rearrange("p (m c) -> p m c", m=KT)
        v0 = KT * VW
        state_out = S[:, v0:v0 + 1024].rearrange("p (b c) -> p b c", b=2)
        x_stage = S[:, v0:v0 + D]
        taps_stage = RAW[:, 2, 0:D]
        state_stage = RAW[:, 3, 0:2 * D].rearrange("p (g n) -> p g n", g=2)
        yflat = Y[:, :, :].rearrange("p m t -> p (m t)")
        p_stage = S[:, 0:5 * PLE].rearrange("p (b c) -> p b c", b=5)
        QR = S[:, 0:2304].rearrange("p (j t) -> p j t", j=4)
        KR = S[:, 2304:2880]
        QLAT = S[:, 2880:4928].rearrange("p (c q) -> p c q", c=4)
        CS = S[:, 4928:5184].rearrange("p (c t) -> p c t", c=4)
        QRS = S[:, 5184:5696]
        CK = S[:, 5696:8000].rearrange("p (c t) -> p c t", c=4)
        PT = S[:, 5696:7744].rearrange("p (k q) -> p k q", k=4)
        SPT = S[:, 5696:5952].rearrange("p (k q) -> p k q", k=4)
        OUT, OUTN = S[0:64, 5952:6464], S[0:64, 6464:6976]
        COS, SIN, ROT = S[:, 2880:3456], S[:, 3456:4032], S[:, 4032:4160]
        kv_stage = S[:, 4160:4736]
        kT = sq[:, :, :].rearrange("p a b -> p (a b)")[:, 0:TP]
        vn = root[:, :, :].rearrange("p a b -> p (a b)")[:, 0:TP]
        ukT = acc[:, :, :].rearrange("p a b -> p (a b)")[:, 0:TP]
        PB = [prod[:, :, :].rearrange("p a b -> p (a b)")[:, 0:TP],
              scaled[:, :, :].rearrange("p a b -> p (a b)")[:, 0:TP]]
        flat = {n: t[:, :, :].rearrange("p a b -> p (a b)") for n, t in
                (("prod", prod), ("scaled", scaled), ("sq", sq), ("root", root), ("acc", acc))}
        cmask = R2[:, :, :].rearrange("p a b -> p (a b)")[:, 0:P]
        nmask = R2[:, :, :].rearrange("p a b -> p (a b)")[0:64, P:P + TQ]

        landed = [sem(f"landed{i}") for i in range(RING)]
        hi_done, lo_done, pe_read_raw = sem("hi_done"), sem("lo_done"), sem("pe_read_raw")
        unit_done, bank_free = sem("unit_done"), sem("bank_free")
        consts, ones_set, vecs, x_in, x_stage_in = sem("consts"), sem("ones_set"), sem("vecs"), sem("x_in"), sem("x_stage_in")
        turned, unturned = sem("turned"), sem("unturned")
        sq_done, acc_done, sum_done, root_done, rstd_done = (sem("sq_done"), sem("acc_done"), sem("sum_done"),
                                                             sem("root_done"), sem("rstd_done"))
        row_step = sem("row_step")
        a_hi, a_lo, x_done, sc_done = sem("a_hi"), sem("a_lo"), sem("x_done"), sem("sc_done")
        xg_done, y_out = sem("xg_done"), [sem("y_out0"), sem("y_out1")]
        out_sem = sem("out_sem")

        SG = NS // 2 * (CW - 1)

        def half(t, m, h):
            return t[:, m, h * H:(h + 1) * H]

        def gain(name, m):
            return gains[:, GCOL[name] + m:GCOL[name] + m + 1]

        consts_sem = consts
        conv_step, v_done, gate_sig = sem("conv_step"), sem("v_done"), sem("gate_sig")
        state_done, state_copied = sem("state_done"), sem("state_copied")
        state_out_sem = [sem("state_out0"), sem("state_out1")]
        unturned_v, unturned_a = sem("unturned_v"), sem("unturned_a")
        sw_sig, sw_lin, sw_val = sem("sw_sig"), sem("sw_lin"), sem("sw_val")
        ck_val, b_hi, b_lo = sem("ck_val"), sem("b_hi"), sem("b_lo")
        relu_done, sq_relu, u_hi, u_lo = sem("relu_done"), sem("sq_relu"), sem("u_hi"), sem("u_lo")
        y_zero, p_in, p_turned, p_hi, p_lo = sem("y_zero"), sem("p_in"), sem("p_turned"), sem("p_hi"), sem("p_lo")
        sig_done, gated = sem("sig_done"), sem("gated")
        rope_in, rot_done, rope_step = sem("rope_in"), sem("rot_done"), sem("rope_step")
        kv_turned, kv_staged, kv_out, cs_done = sem("kv_turned"), sem("kv_staged"), sem("kv_out"), sem("cs_done")
        centred = sem("centred")

        def w_at(d):
            return d % WRING

        def unit_end(phase, h):
            last = {"pw1": 2, "pw2": 2, "dkv": 1, "dq": 2, "uq": 2, "wo": 2, "gate0": 2, "gate1": 2,
                    "ple0": 8, "ple1": 8}[phase]
            return UNIT0[phase] + UNITS[phase] - (last if h == 0 else 0)

        def up_n(h, m):
            return 4 * (m // 2) + 2 * h + m % 2

        read_before = {"sw": "pw1", "ff0": "pw2", "kv": "gate0", "mx": "dkv", "cq": "dq", "ff1": "wo"}
        gain_of = {"x0": "mix_pre0", "ff0": "ff_pre0", "g0": None, "kv": "kv_in", "mx": "mix_pre1",
                   "cq": "q_norm", "ff1": "ff_pre1", "g1": None, "sw": None}
        tokens = [(b * P, P) for b in range(4)] + [(TP, TS)]
        SLABS = {n: s for n, s, *_ in PHASES}
        KR_STEP = 7
        STATES = [(m, g) for m in range(KT) for g in range(2)] + [(None, 0), (None, 1)]
        NORM_OF = {"sw": "lv"}
        SM = Order([("mask",), ("new_top",)] + [(w, j) for j in range(4) for w in ("top", "bias", "sum")])
        NSM = len(SM.at)
        OUTS = 6

        def scaled_read(key):
            st, h, m = key
            if st in ("y0", "m0", "y1", "m1"):
                return x_done, XU(*key)
            if st == "sw":
                return sw_val, KT * h + m + 1
            return (ck_val, 4 * h + m + 1) if st == "ck" else (a_lo, A(*key))

        kvt_done, kvt_used = sem("kvt_done"), sem("kvt_used")
        v_mm, v_used, uk_mm, uk_used, ql_mm, ql_used = (sem("v_mm"), sem("v_used"), sem("uk_mm"), sem("uk_used"),
                                                        sem("ql_mm"), sem("ql_used"))
        s_mm, s_masked, s_max, s_exp, s_rec, p_ready = (sem("s_mm"), sem("s_masked"), sem("s_max"), sem("s_exp"),
                                                        sem("s_rec"), sem("p_ready"))
        pt_mm, pt_used, pv_mm = sem("pt_mm"), sem("pt_used"), sem("pv_mm")
        table_in, page_mm, key_hi, key_lo, score_mm, new_in, q_hi, q_lo = (
            sem("table_in"), sem("page_mm"), sem("key_hi"), sem("key_lo"), sem("score_mm"), sem("new_in"), sem("q_hi"),
            sem("q_lo"))
        new_mm, new_nat, new_nat_c, sm_step, exp_done, spt_mm, spt_c, out_mm, lat_out = (
            sem("new_mm"), sem("new_nat"), sem("new_nat_c"), sem("sm_step"), sem("exp_done"), sem("spt_mm"),
            sem("spt_c"), sem("out_mm"), sem("lat_out"))
        out_done = sem("out_done")
        dve_step, dup_set, seen, qsr_zero = sem("dve_step"), sem("dup_set"), sem("seen"), sem("qsr_zero")
        qrs_mm, qrs_c, uv_mm, y_turned, y_copied_v, y_copied_a = (sem("qrs_mm"), sem("qrs_c"), sem("uv_mm"),
                                                                  sem("y_turned"), sem("y_copied_v"), sem("y_copied_a"))
        table = sb("table", [1, PAGES], I32)

        block = ctx.enter_context(nc.Block())

        def cache_loads(sp):
            g0 = RAW0["cache"]
            with sp.Fori(0, NS) as i:
                sp.dma_start(table[:], io["page_table"][bass.ds(i, 1), :]).then_inc(table_in, 16)
                sp.wait_ge(table_in, 16)
                sp.sem_clear(table_in)
                for j in range(RING):
                    pages = [sp.value_load(table[0:1, 4 * j + q:4 * j + q + 1], min_val=0,
                                           max_val=io["cache_kv_latent"].shape[0] - 1) for q in range(4)]
                    sp.wait_ge(pe_read_raw, 1 + j + RING * i)
                    sp.wait_ge(ones_set, 1)
                    if j == 0:
                        sp.wait_ge(lo_done, DENSE0["kvh"] + 4)
                    for q in range(4):
                        dst = RAW[:, (g0 + j) % RING].rearrange("p (a c) -> p a c", a=1)
                        sp.dma_start(dst[:, :, q * CL:(q + 1) * CL],
                                     io["cache_kv_latent"].rearrange("n p c -> p n c")[:, bass.ds(pages[q], 1)])\
                            .then_inc(landed[(g0 + j) % RING], 16)
                        r = 4 * CL + DR * (q // 2 + 2 * (q % 2))
                        sp.dma_start(dst[:, :, r:r + DR],
                                     io["cache_k_rope"].rearrange("n p c -> p n c")[:, bass.ds(pages[q], 1)])\
                            .then_inc(landed[(g0 + j) % RING], 16)

        @block.sync
        def _(sp):
            def put(g, parts, dst_slot, i=None, per=0):
                for dst, src in parts:
                    sp.dma_start(dst, src).then_inc(landed[g % RING], 16)

            def slot(g, a, b):
                return RAW[:, g % RING, a:b]

            def cols(w, kt, c0, n):
                return w.rearrange("(k p) n -> p k n", p=P)[:, :, c0:c0 + n] if kt else None

            def free(g, i=0):
                kind, j = KIND[g - RING]
                if kind == "cache":
                    sp.wait_ge(pe_read_raw, 4 + j + 1)
                    return
                if kind == "kvh":
                    sp.wait_ge(pe_read_raw, j + 1)
                sp.wait_ge(lo_done, DENSE0[kind] + j + 1)

            def dense(phase, w, kt, n):
                for j in range(SLABS[phase]):
                    g = RAW0[phase] + j
                    free(g)
                    sp.dma_start(slot(g, 0, kt * n).rearrange("p (k n) -> p k n", k=kt),
                                 w.rearrange("(k p) n -> p k n", p=P)[:, :, j * n:(j + 1) * n])\
                        .then_inc(landed[g % RING], 16)

            def mlp(layer, phase):
                up = io["w_up"][layer].rearrange("(k p) (c n) -> p c k n", p=P, n=256)
                down = io["w_down"][layer].rearrange("(c k p) n -> p c k n", p=P, k=FC)
                g0, d0 = RAW0[phase], DENSE0[phase]
                with sp.Fori(0, NCH) as i:
                    for j in range(RING):
                        g = g0 + j
                        dst = slot(g, 0, WSLOT)
                        sp.wait_ge(lo_done, d0 + j - RING + 1 + RING * i)
                        sp.wait_ge(ones_set, 1)
                        if j < 2:
                            sp.dma_start(dst.rearrange("p (c k n) -> p c k n", c=1, k=KT),
                                         up[:, bass.ds(2 * i + j, 1)]).then_inc(landed[g % RING], 16)
                        else:
                            n = (j - 2) * 512
                            sp.dma_start(dst.rearrange("p (c k n) -> p c k n", c=1, k=FC),
                                         down[:, bass.ds(i, 1), :, n:n + 512]).then_inc(landed[g % RING], 16)

            def ple(layer, phase):
                g = RAW0[phase]
                free(g)
                sp.dma_start(slot(g, 0, 2 * D).rearrange("p (k n) -> p k n", k=2),
                             io["ple_proj"][layer].rearrange("(k p) n -> p k n", p=P)).then_inc(landed[g % RING], 16)

            def load_p(layer):
                for b, (t0, n) in enumerate(tokens):
                    src = io["p_prompt"][layer, 0, t0:t0 + n] if b < 4 else \
                        io["p_sample"][layer].rearrange("s t c -> (s t) c")
                    sp.dma_start(p_stage[0:n, b, :], src).then_inc(p_in, 16)

            sp.dma_start(ident[:], io["consts"][:, 0:P]).then_inc(consts, 16)
            row = 0
            vec = {"mix_pre0": io["norm_mix_pre"][0], "mix_pre1": io["norm_mix_pre"][1],
                   "mix_post0": io["norm_mix_post"][0], "mix_post1": io["norm_mix_post"][1],
                   "ff_pre0": io["norm_ff_pre"][0], "ff_pre1": io["norm_ff_pre"][1],
                   "ff_post0": io["norm_ff_post"][0], "ff_post1": io["norm_ff_post"][1],
                   "dw_bias": io["conv_dw_bias"][0], "ln_g": io["conv_ln_g"][0], "ln_b": io["conv_ln_b"][0],
                   "kv_in": io["kv_in_norm"], "kv_norm": io["kv_norm"], "q_norm": io["q_norm"][0]}
            for name, n in GAINS:
                sp.dma_start(flat["prod"][row:row + n, 0:P], vec[name].rearrange("(r c) -> r c", c=P)).then_inc(vecs, 16)
                row += n
            for b in range(4):
                sp.dma_start(yflat[:, b * D:(b + 1) * D], io["x_prompt"][0, b * P:(b + 1) * P]).then_inc(x_in, 16)
            sp.dma_start(x_stage[0:TS], io["x_sample"].rearrange("s t c -> (s t) c")).then_inc(x_in, 16)
            pw1 = io["conv_pw1"][0].rearrange("(k p) (a m n) -> p m a k n", p=P, a=2, n=P)

            def pw1_slab(g, m):
                for a in range(2):
                    sp.dma_start(slot(g, 0, WSLOT).rearrange("p (m k a n) -> p m k a n", m=1, k=KT, a=2)[:, :, :, a],
                                 pw1[:, m, a]).then_inc(landed[g % RING], 16)

            for j in range(2):
                pw1_slab(j, slice(j, j + 1))
            sp.dma_start(taps_stage[0:CW], io["conv_dw"][0]).then_inc(vecs, 16)
            for g in range(2):
                sp.dma_start(state_stage[0:SG, g, :],
                             io["state_conv"][0, 4 * g:4 * g + 4].rearrange("s j c -> (s j) c")).then_inc(vecs, 16)
            sp.wait_ge(turned, 26)
            for j in range(2, 4):
                pw1_slab(j, slice(j, j + 1))
            for j in range(4, 8):
                free(j)
                pw1_slab(j, slice(j, j + 1))
            dense("pw2", io["conv_pw2"][0], KT, 256)
            for q in state_out_sem:
                sp.wait_ge(q, 16 * len(STATES) // 2)
            sp.wait_ge(conv_step, 2 * CW * KT)
            load_p(0)
            mlp(0, "mlp0")
            ple(0, "ple0")
            dense("gate0", io["ple_gate"][0], KT, 256)
            for j in range(3):
                g = RAW0["dkv"] + j
                free(g)
                wk = io["w_dkv"].rearrange("(k p) n -> p k n", p=P)
                if j < 2:
                    sp.dma_start(slot(g, 0, WSLOT).rearrange("p (k n) -> p k n", k=KT),
                                 wk[:, :, 256 * j:256 * j + 256]).then_inc(landed[g % RING], 16)
                else:
                    for c in range(2):
                        sp.dma_start(slot(g, 0, KT * P).rearrange("p (k n) -> p k n", k=KT)[:, :, 64 * c:64 * c + 64],
                                     wk[:, :, CL:CL + DR]).then_inc(landed[g % RING], 16)
            sp.wait_ge(p_turned, 4)
            sp.dma_start(S[:, 2880:4160], io["consts"][:, 320:1600]).then_inc(rope_in, 16)
            dense("dq", io["w_dq"][0], KT, 256)
            uq = io["w_uq"][0].rearrange("(k p) (h e) -> p k h e", p=P, h=NH)
            for j in range(6):
                g = RAW0["uq"] + j
                free(g)
                dst = slot(g, 0, 6 * 256).rearrange("p (k n) -> p k n", k=6)
                heads, e0, e1 = ((2 * j, 2 * j + 1), 0, DN) if j < 4 else (range(4 * (j - 4), 4 * (j - 4) + 4), DN, DN + DR)
                for n, h in enumerate(heads):
                    sp.dma_start(dst[:, :, n * (e1 - e0):(n + 1) * (e1 - e0)], uq[:, :, h, e0:e1])\
                        .then_inc(landed[g % RING], 16)
            for j in range(4):
                g = RAW0["kvh"] + j
                free(g)
                for n, w in enumerate((io["w_uk"], io["w_uv"])):
                    sp.dma_start(slot(g, 1024 * n, 1024 * n + 1024).rearrange("p (k n) -> p k n", k=4),
                                 w.rearrange("(k p) h n -> p k (h n)", p=P)[:, :, 256 * j:256 * j + 256])\
                        .then_inc(landed[g % RING], 16)
            sp.wait_ge(sc_done, SC("cq", 1, 5))
            sp.dma_start(cmask, io["consts"][:, 128:256]).then_inc(consts, 16)
            sp.dma_start(nmask, io["consts"][0:64, 256:264]).then_inc(consts, 16)
            cache_loads(sp)
            for j in range(2):
                g = RAW0["uv"] + j
                free(g)
                sp.dma_start(slot(g, 0, WSLOT).rearrange("p (k n) -> p k n", k=4),
                             io["w_uv"].rearrange("(k p) h n -> p k (h n)", p=P)[:, :, 512 * j:512 * j + 512])\
                    .then_inc(landed[g % RING], 16)
            dense("wo", io["w_o"][0], KT, 256)
            sp.wait_ge(a_lo, A("o", 1, NH - 1))
            load_p(1)
            mlp(1, "mlp1")
            ple(1, "ple1")
            dense("gate1", io["ple_gate"][1], KT, 256)

        scratch = flat["acc"]
        NK, NKR = scratch[:, 0:32].rearrange("p (c t) -> p c t", c=4), scratch[0:DR, 32:40]
        SN, PN = scratch[0:64, 64:72], scratch[0:64, 72:80]
        TOP, NM, ALPHA, PSUMS, SUMQ = (scratch[0:64, 80 + 8 * k:88 + 8 * k] for k in range(5))
        QS = flat["prod"][:, 0:256].rearrange("p (c q) -> p c q", c=4)
        QSR = flat["prod"][:, 256:384].rearrange("p (r q) -> p r q", r=2)
        NEWC, NPT = flat["sq"][0:TQ, 0:CL], flat["root"][0:TQ, 0:64]
        SP = flat["scaled"][0:64, 0:512]
        rope_bank = bank[3][:, 0:256].rearrange("p (a b) -> p a b", a=4)
        DUP = flat["sq"][:, 0:256].rearrange("p (e c) -> p e c", e=2)

        def col(t, j):
            return t[:, j:j + 1]

        dense_slabs = [(g, k, j) for g, (k, j) in enumerate(KIND) if k != "cache"]
        floats = {"ple0": 2048, "ple1": 2048, "uq": 1536}

        def slab_size(d):
            g, k, j = dense_slabs[d]
            return 1024 if (k, j) == ("dkv", 2) else floats.get(k, 2048)

        def landed_at(d):
            g = dense_slabs[d][0]
            return landed[g % RING], LANDED[g]

        def raw_of(d):
            return RAW[:, dense_slabs[d][0] % RING, 0:slab_size(d)]


        def prev(order, key, back):
            n = order.at[key] - back
            return next((k for k, v in order.at.items() if v == n), None)

        def used_at(d):
            _, kind, j = dense_slabs[d]
            if kind == "kvh":
                return kvt_done, 2 * j + 2
            if kind == "uv":
                return uv_mm, 4 * j + 4
            if kind in ("mlp0", "mlp1"):
                return unit_done, UNIT0[kind] + CHUNK * (j // 4) + (4, 8, 16, 24)[j % 4]
            if kind == "dkv":
                return unit_done, UNIT0[kind] + (4, 8, 10)[j]
            return unit_done, UNIT0[kind] + UNITS[kind] // SLABS[kind] * (j + 1)

        @block.scalar
        def _(act):
            def hi(d, i=None, per=16):
                s, v = landed_at(d)
                act.wait_ge(s, v if i is None else v + per * i)
                if d >= WRING:
                    s, v = used_at(d - WRING)
                    act.wait_ge(s, v if i is None else v + (16 if KIND[dense_slabs[d][0]][0] == "pw1" or d == 8
                                                            else CHUNK) * i)
                elif i is not None:
                    act.wait_ge(bank_free, BANKS + 16 * i)
                nc.scalar.activation(WH[:, d % WRING, 0:slab_size(d)], raw_of(d), ACT.Copy).then_inc(hi_done, 1)

            def square(st, h, m, src):
                before = prev(SQ, (st, h, m), 2)
                if before:
                    act.wait_ge(acc_done, ACC(*before))
                nc.scalar.activation(sq[:, SQ(st, h, m) % 2, :], src, ACT.Square).then_inc(sq_done, 1)

            def root_of(st, h):
                if st in SCALED_BY_INPUT:
                    act.wait_ge(row_step, ROW(st, h))
                    src = root[:, h, :]
                else:
                    act.wait_ge(sum_done, SUM(st, h))
                    src = bank[4 + h][:, 0:H]
                before = [k for k in ROOT.at if k[1] == h and ROOT(*k) < ROOT(st, h)]
                if before:
                    act.wait_ge(rstd_done, RSTD(*before[-1]))
                nc.scalar.activation(root[:, h, :], src, ACT.Sqrt, bias=eps[:, 0:1], scale=1.0 / (P * NT[st]))\
                    .then_inc(root_done, 1)

            def split(v, h, m, src):
                if v in read_before:
                    act.wait_ge(unit_done, unit_end(read_before[v], h))
                if v in ("g0", "g1"):
                    act.wait_ge(unit_done, UNIT0["mlp" + v[1]] + CHUNK * NCH)
                g = gain_of[v]
                if g:
                    nc.scalar.activation(half(AH, m, h), src, ACT.Copy, scale=gain(g, m)).then_inc(a_hi, 1)
                else:
                    nc.scalar.activation(half(AH, m, h), src, ACT.Copy).then_inc(a_hi, 1)

            act.wait_ge(ones_set, 3)
            for e in range(1, 26, 2):
                act.wait_ge(turned, e + 1)
                src = bank[4 + e % 4]
                if e == 1:
                    nc.scalar.activation(taps[:, :, :], src[:, 0:KT * CW].rearrange("p (m c) -> p m c", m=KT),
                                         ACT.Copy).then_inc(unturned_a, 1)
                elif e < 18:
                    nc.scalar.activation(X[:, (e - 3) // 2, TP:T], src[:, 0:TS], ACT.Copy).then_inc(unturned_a, 1)
                else:
                    nc.scalar.activation(V[:, e - 18, VP:VW].rearrange("p (s c) -> p s c", s=NS)[:, :, 0:CW - 1],
                                         src[:, 0:2 * SG].rearrange("p (s c) -> p s c", s=NS),
                                         ACT.Copy).then_inc(unturned_a, 1)
            hi(0)
            act.wait_ge(unturned_v, 13)
            act.wait_ge(unturned_a, 13)
            for h in range(2):
                for m in range(KT):
                    split("x0", h, m, half(X, m, h))
                    square("x0", h, m, half(X, m, h))
            for h in range(2):
                root_of("x0", h)

            with act.Fori(0, 2) as i:
                for j in range(4):
                    hi(j + 1, i, 32 if j < 3 else 16)
                    for h in range(2):
                        act.wait_ge(bank_free, freed(4 * j + 2 * h + 1) + 16 * i)
                        nc.scalar.activation(prod[:, h, :], prod[:, h, :], ACT.Sigmoid).then_inc(gate_sig, 1)
            for e, (m, g) in enumerate(STATES):
                act.wait_ge(state_done, e + 1)
                if e >= 2:
                    act.wait_ge(state_out_sem[e % 2], 16 * (e // 2))
                nc.scalar.activation(state_out[0:CW - 1, e % 2, :], bank[4 + e % 4][0:CW - 1, 0:512], ACT.Copy)\
                    .then_inc(state_copied, 1)
                act.wait_ge(state_copied, e + 1)
                src = state_out[0:CW - 1, e % 2, :]
                if m is None:
                    dst = io["new_conv_prompt"][0, 0, :, 512 * g:512 * g + 512]
                else:
                    dst = io["new_conv_sample"][0, 4 * g:4 * g + 4, :, m * P:(m + 1) * P].rearrange("s j c -> j s c")
                    src = src.rearrange("j (s c) -> j s c", s=4)
                act.dma_start(dst, src).then_inc(state_out_sem[e % 2], 16)

            for h in range(2):
                for m in range(KT):
                    act.wait_ge(centred, KT * h + m + 1)
                    square("lv", h, m, half(Y, m, h))
                root_of("lv", h)
                for m in range(KT):
                    n = KT * h + m
                    act.wait_ge(sc_done, SC("sw", h, m))
                    if n >= 2:
                        act.wait_ge(a_lo, A("x0", 1, KT - 1) + n - 1)
                    nc.scalar.activation(prod[:, n % 2, :], scaled[:, SC("sw", h, m) % 2, :], ACT.Sigmoid,
                                         bias=gain("ln_b", m), scale=gain("ln_g", m)).then_inc(sw_sig, 1)
                    act.wait_ge(sw_val, n + 1)
                    split("sw", h, m, prod[:, n % 2, :])

            def hi_steps(phase):
                for j in range(SLABS[phase]):
                    hi(DENSE0[phase] + j + 1)

            def after_mixer(st, v, stx):
                for h in range(2):
                    for m in range(KT):
                        act.wait_ge(bank_free, freed(unit_of(st, h, m)))
                        square(st, h, m, half(Y, m, h))
                    root_of(st, h)
                    for m in range(KT):
                        act.wait_ge(x_done, XU(st, h, m))
                        split(v, h, m, half(X, m, h))
                        square(stx, h, m, half(X, m, h))

            def mlp(layer):
                phase, v = f"mlp{layer}", f"g{layer}"
                d0, u0 = DENSE0[phase], UNIT0[phase]
                b0 = UP * NCH * layer
                with act.Fori(0, NCH) as i:
                    for j in range(4):
                        hi(d0 + j + 1, i)
                        if j >= 2:
                            continue
                        for k in range(5):
                            n = 4 * j + k
                            if k < 4:
                                act.wait_ge(unit_done, u0 + n + 1 + CHUNK * i)
                                nc.scalar.activation(scaled[:, n % 2, :], bank[(u0 + n) % BANKS][:, 0:H], ACT.Relu)\
                                    .then_inc(relu_done, 1)
                            if k:
                                n, q = n - 1, k - 1
                                act.wait_ge(bank_free, freed(u0 + n) + CHUNK * i)
                                nc.scalar.activation(half(BH, 2 * j + q % 2, q // 2), prod[:, n % 2, :], ACT.Copy)\
                                    .then_inc(u_hi, 1)
                for h in range(2):
                    root_of(f"x{2 * layer + 1}", h)
                for e in range(4):
                    kt, part = e // 2, e % 2
                    a, b = (0, TP) if part == 0 else (TP, T)
                    act.wait_ge(p_turned, 4 * layer + e + 1)
                    nc.scalar.activation(BH[:, kt, a:b], bank[6 + part][:, 0:b - a], ACT.Copy).then_inc(p_hi, 1)
                st = f"m{layer}"
                for h in range(2):
                    for m in range(KT):
                        act.wait_ge(bank_free, freed(unit_of(st, h, m)))
                        square(st, h, m, half(Y, m, h))
                    root_of(st, h)
                for h in range(2):
                    for m in range(KT):
                        act.wait_ge(x_done, XU(st, h, m))
                        split(v, h, m, half(X, m, h))

                hi(DENSE0[f"ple{layer}"] + 1)
                d0, u0 = DENSE0[f"gate{layer}"], UNIT0[f"gate{layer}"]
                for j in range(4):
                    if d0 + j + 1 < len(dense_slabs):
                        hi(d0 + j + 1)
                    for k in range(4):
                        n = 4 * j + k
                        act.wait_ge(unit_done, u0 + n + 1)
                        if n >= 2:
                            act.wait_ge(bank_free, freed(u0 + n - 2))
                        nc.scalar.activation(prod[:, n % 2, :], bank[(u0 + n) % BANKS][:, 0:H], ACT.Sigmoid)\
                            .then_inc(sig_done, 1)

            hi_steps("pw2")
            after_mixer("y0", "ff0", "x1")
            mlp(0)

            for h in range(2):
                for m in range(KT):
                    act.wait_ge(xg_done, XG(0, h, m))
                    split("kv", h, m, half(X, m, h))
                    square("x2", h, m, half(X, m, h))
            hi_steps("dkv")
            for h in range(2):
                root_of("x2", h)
            for h in range(2):
                for m in range(KT):
                    split("mx", h, m, half(X, m, h))
            hi_steps("dq")
            for h in range(2):
                for m in range(4):
                    act.wait_ge(bank_free, freed(unit_of("ck", h, m)))
                    square("ck", h, m, half(CK, m, h))
                root_of("ck", h)
            for h in range(2):
                for m in range(4):
                    act.wait_ge(ck_val, 4 * h + m + 1)
                    nc.scalar.activation(half(BH, m, h), half(CK, m, h), ACT.Copy).then_inc(b_hi, 1)
            for h in range(2):
                for m in range(6):
                    act.wait_ge(bank_free, freed(unit_of("cq", h, m)))
                    square("cq", h, m, half(Y, m, h))
                root_of("cq", h)
            for h in range(2):
                for m in range(6):
                    act.wait_ge(sc_done, SC("cq", h, m))
                    split("cq", h, m, scaled[:, SC("cq", h, m) % 2, :])
            for j in range(6):
                hi(DENSE0["uq"] + j + 1)
                if j == 5:
                    break
                t0, n = tokens[j]
                act.wait_ge(kv_turned, j + 1)
                if j:
                    act.wait_ge(kv_out, 32 * j)
                nc.scalar.activation(kv_stage[0:n, 0:CL], bank[4][0:n, 0:CL], ACT.Copy).then_inc(kv_staged, 1)
                nc.scalar.activation(kv_stage[0:n, CL:CL + DR], bank[5][0:n, 0:DR], ACT.Copy).then_inc(kv_staged, 1)
                act.wait_ge(kv_staged, 2 * j + 2)
                for a, b, prompt, sample in ((0, CL, "new_kv_prompt", "new_kv_sample"),
                                             (CL, CL + DR, "new_kr_prompt", "new_kr_sample")):
                    dst = io[prompt][0, t0:t0 + n] if j < 4 else io[sample].rearrange("s t c -> (s t) c")
                    act.dma_start(dst, kv_stage[0:n, a:b]).then_inc(kv_out, 16)

            def head_keys(hd):
                act.wait_ge(kvt_done, hd + 1)
                if hd:
                    act.wait_ge(s_mm, 4 * hd)
                nc.scalar.activation(kT, bank[0][:, 0:TP], ACT.Copy).then_inc(kvt_used, 1)

            def exp(hd, qb):
                n, w = 4 * hd + qb, (qb + 1) * P
                act.wait_ge(s_max, 2 * n + 2)
                if n >= 2:
                    act.wait_ge(pt_mm, n - 1)
                c = 4 * (n % 2)
                nc.scalar.activation(PB[n % 2][:, 0:w], bank[4 + n % 2][:, 0:w], ACT.Exp, scale=SCALE,
                                     bias=tiny[:, c + 1:c + 2], accum_out=tiny[:, c + 2:c + 3]).then_inc(s_exp, 1)

            def pt(hd, qb):
                n = 4 * hd + qb
                act.wait_ge(pt_mm, n + 1)
                if qb == 0 and hd:
                    act.wait_ge(pv_mm, hd)
                if n == 0:
                    act.wait_ge(kv_turned, 5)
                    act.wait_ge(cs_done, 1)
                nc.scalar.activation(PT[:, 0:qb + 1, qb * P:(qb + 1) * P],
                                     bank[6][:, 0:(qb + 1) * P].rearrange("p (k q) -> p k q", q=P), ACT.Copy)\
                    .then_inc(pt_used, 1)

            def head_out(hd):
                act.wait_ge(pv_mm, hd + 1)
                if hd == 0:
                    act.wait_ge(unit_done, unit_end("uq", 1))
                nc.scalar.activation(AH[:, hd, 0:TP], bank[7][:, 0:TP], ACT.Copy).then_inc(a_hi, 1)

            head_keys(0)
            for hd in range(NH):
                exp(hd, 0)
                if hd:
                    pt(hd - 1, 3)
                    head_out(hd - 1)
                exp(hd, 1)
                pt(hd, 0)
                exp(hd, 2)
                pt(hd, 1)
                if hd % 2 == 0 and hd < NH - 2:
                    hi(DENSE0["kvh"] + hd // 2 + 1)
                if hd < NH - 1:
                    head_keys(hd + 1)
                exp(hd, 3)
                pt(hd, 2)
            pt(NH - 1, 3)
            head_out(NH - 1)

            def key(c, n):
                act.wait_ge(page_mm, c + 1 + 5 * n)
                if c == 0:
                    act.wait_ge(score_mm, n + 1)
                dst, src = (BH[:, c, 0:TP], bank[4 + c][:, 0:TP]) if c < 4 else (BH[:, :, TP:T], rope_bank)
                nc.scalar.activation(dst, src, ACT.Copy).then_inc(key_hi, 1)

            def queries(i):
                act.wait_ge(new_in, 5 + 5 * i)
                act.wait_ge(score_mm, 1 + 4 * i)
                nc.scalar.activation(AH[:, 0:4, TP:T], QS, ACT.Copy).then_inc(q_hi, 1)
                nc.scalar.activation(AH[:, 4:6, TP:T], QSR, ACT.Copy).then_inc(q_hi, 1)

            def new_values(i):
                act.wait_ge(new_nat, 2 + i)
                nc.scalar.activation(NEWC, bank[4][0:TQ, 0:CL], ACT.Copy).then_inc(new_nat_c, 1)

            def slab(j, i, last):
                act.wait_ge(sm_step, SM("bias", j) + NSM * i)
                nc.scalar.activation(SP, bank[0][0:64, :], ACT.Exp, scale=SCALE, bias=col(NM, j), accum_out=col(PSUMS, j))\
                    .then_inc(exp_done, 1)
                if j == 0:
                    nc.scalar.activation(PN, SN, ACT.Exp, scale=SCALE, bias=col(NM, 0), accum_out=col(PSUMS, 4))\
                        .then_inc(exp_done, 1)
                else:
                    nc.scalar.activation(col(ALPHA, j), col(NM, j - 1), ACT.Exp, scale=-1.0, bias=col(NM, j))\
                        .then_inc(exp_done, 1)
                if not last:
                    for c in range(5):
                        key(c, j + 1 + 4 * i)
                act.wait_ge(spt_mm, j + 1 + 4 * i)
                act.wait_ge(pe_read_raw, 4 + j + 4 * i)
                nc.scalar.activation(SPT, bank[1][:, 0:256].rearrange("p (k q) -> p k q", k=4), ACT.Copy)\
                    .then_inc(spt_c, 1)
                if j == 0:
                    nc.scalar.activation(NPT, bank[1][0:TQ, 256:320], ACT.Copy).then_inc(spt_c, 1)

            def sequence(i, last):
                for j in range(4):
                    slab(j, i, last and j == 3)
                if not last:
                    queries(i + 1)
                    new_values(i + 1)

            queries(0)
            for c in range(5):
                key(c, 0)
            new_values(0)
            with act.Fori(0, NS - 1) as i:
                sequence(i, False)
            sequence(NS - 1, True)
            act.wait_ge(lat_out, 1 + NS)
            hi(DENSE0["uv"])
            nc.scalar.activation(BH[:, :, 0:TP], QLAT[:, :, :], ACT.Copy).then_inc(b_hi, 1)
            for hd in range(NH):
                if hd % 4 == 0:
                    hi(DENSE0["uv"] + hd // 4 + 1)
                act.wait_ge(uv_mm, hd + 1)
                nc.scalar.activation(AH[:, hd, TP:T], bank[hd % 4][:, 0:TS], ACT.Copy).then_inc(a_hi, 1)
            hi_steps("wo")
            after_mixer("y1", "ff1", "x3")
            mlp(1)

            for b, (t0, n) in enumerate(tokens):
                act.wait_ge(y_turned, 2 * b + 1)
                if b >= 2:
                    act.wait_ge(y_out[b % 2], 16 * (b // 2))
                nc.scalar.activation(yflat[0:n, (b % 2) * D:(b % 2) * D + 512], bank[4 + 2 * (b % 2)][0:n, 0:512],
                                     ACT.Copy).then_inc(y_copied_a, 1)
                act.wait_ge(y_copied_a, b + 1)
                act.wait_ge(y_copied_v, b + 1)
                dst = io["y_prompt"][0, t0:t0 + n] if b < 4 else io["y_sample"].rearrange("s t c -> (s t) c")
                act.dma_start(dst, yflat[0:n, (b % 2) * D:(b % 2) * D + D]).then_inc(y_out[b % 2], 16)
            act.wait_ge(y_out[0], 16 * 3)
            act.wait_ge(y_out[1], 16 * 2)
            act.wait_ge(kv_out, 32 * 5)
            for q in state_out_sem:
                act.wait_ge(q, 16 * len(STATES) // 2)

        @block.gpsimd
        def _(pool):
            def lo(d, i=None):
                pool.wait_ge(hi_done, d + 1 + (0 if i is None else RING * i))
                n = slab_size(d)
                nc.gpsimd.tensor_tensor(WL[:, d % WRING, 0:n], raw_of(d), WH[:, d % WRING, 0:n].bitcast(F32),
                                        ALU.subtract).then_inc(lo_done, 1)

            def add(st, h, m, src, own=True):
                if st == "lm":
                    pass
                else:
                    pool.wait_ge(sq_done, SQ(st, h, m))
                    src = sq[:, SQ(st, h, m) % 2, :]
                if m == 0:
                    before = [k for k in SUMS[:SUMS.index((st, h))] if k[1] == h]
                    if before:
                        pool.wait_ge(rstd_done, RSTD(*before[-1]))
                    nc.gpsimd.tensor_copy(acc[:, h, :], src).then_inc(acc_done, 1)
                else:
                    pool.wait_ge(acc_done, ACC(st, h, m - 1))
                    nc.gpsimd.tensor_tensor(acc[:, h, :], acc[:, h, :], src, ALU.add).then_inc(acc_done, 1)

            def scale(st, h, m, src):
                if m == 0:
                    pool.wait_ge(rstd_done, RSTD(NORM_OF.get(st, st), h))
                before = prev(SC, (st, h, m), 2)
                if before:
                    s, v = scaled_read(before)
                    pool.wait_ge(s, v)
                nc.gpsimd.tensor_tensor(scaled[:, SC(st, h, m) % 2, :], src, R2[:, h, :], ALU.mult).then_inc(sc_done, 1)

            nc.gpsimd.memset(ones[:], 1.0).then_inc(ones_set, 1)
            nc.gpsimd.memset(eps[:], EPS).then_inc(ones_set, 1)
            nc.gpsimd.memset(V[:, :, 0:CW - 1], 0.0).then_inc(ones_set, 1)
            for s, n in ((bank_free, BANKS), (v_done, 3), (u_lo, 2), (key_lo, 5), (score_mm, 1), (new_nat, 1),
                         (lat_out, 1)):
                pool.sem_inc(s, n)
            lo(0)
            for h in range(2):
                for m in range(KT):
                    add("x0", h, m, None)

            pool.wait_ge(unturned_v, 13)
            pool.wait_ge(unturned_a, 13)
            with pool.Fori(0, 2) as i:
                for j in range(4):
                    lo(j + 1, i)
                    vm = V[:, bass.ds(4 * i + j, 1), :]
                    pool.wait_ge(gate_sig, 2 * j + 1 + 8 * i)
                    nc.gpsimd.tensor_tensor(vm[:, 0, CW - 1:CW - 1 + H], scaled[:, 0, :], prod[:, 0, :], ALU.mult)\
                        .then_inc(v_done, 1)
                    pool.wait_ge(gate_sig, 2 * j + 2 + 8 * i)
                    nc.gpsimd.tensor_tensor(vm[:, 0, CW - 1 + H:VP], scaled[:, 1, 0:TP - H], prod[:, 1, 0:TP - H],
                                            ALU.mult).then_inc(v_done, 1)
                    nc.gpsimd.tensor_tensor(
                        vm[:, 0, VP:VW].rearrange("p (s c) -> p s c", s=NS)[:, :, CW - 1:VSQ],
                        scaled[:, 1, TP - H:H].rearrange("p (s c) -> p s c", s=NS),
                        prod[:, 1, TP - H:H].rearrange("p (s c) -> p s c", s=NS), ALU.mult).then_inc(v_done, 1)
            for h in range(2):
                for m in range(KT):
                    pool.wait_ge(conv_step, 2 * CW * (m + 1))
                    add("lm", h, m, half(Y, m, h))
            for h in range(2):
                for m in range(KT):
                    add("lv", h, m, None)
                for m in range(KT):
                    scale("sw", h, m, half(Y, m, h))

            def lo_steps(phase):
                for j in range(SLABS[phase]):
                    lo(DENSE0[phase] + j + 1)

            def after_mixer(st, stx):
                for h in range(2):
                    for m in range(KT):
                        add(st, h, m, None)
                    for m in range(KT):
                        scale(st, h, m, half(Y, m, h))
                        if m:
                            add(stx, h, m - 1, None)
                    add(stx, h, KT - 1, None)
                    pool.wait_ge(sc_done, SC(st, h, KT - 1))
                    nc.gpsimd.memset(Y[:, :, h * H:(h + 1) * H], 0.0).then_inc(y_zero, 1)

            def mlp(layer):
                phase = f"mlp{layer}"
                d0, b0 = DENSE0[phase], UP * NCH * layer
                with pool.Fori(0, NCH) as i:
                    for j in range(4):
                        lo(d0 + j + 1, i)
                        if j < 2:
                            for k in range(4):
                                n, h, m = 4 * j + k, k // 2, 2 * j + k % 2
                                pool.wait_ge(u_hi, b0 + n + 1 + UP * i)
                                nc.gpsimd.tensor_tensor(half(BL, m, h), prod[:, n % 2, :], half(BH, m, h).bitcast(F32),
                                                        ALU.subtract).then_inc(u_lo, 1)
                st = f"m{layer}"
                for h in range(2):
                    for m in range(KT):
                        add(st, h, m, None)
                for h in range(2):
                    for m in range(KT):
                        scale(st, h, m, half(Y, m, h))
                lo(DENSE0[f"ple{layer}"] + 1)
                for j in range(4):
                    if DENSE0[f"gate{layer}"] + j + 1 < len(dense_slabs):
                        lo(DENSE0[f"gate{layer}"] + j + 1)

            lo_steps("pw2")
            after_mixer("y0", "x1")
            mlp(0)
            for h in range(2):
                for m in range(KT):
                    add("x2", h, m, None)
            lo_steps("dkv")
            lo_steps("dq")
            for h in range(2):
                for m in range(4):
                    add("ck", h, m, None)
            for h in range(2):
                for m in range(4):
                    scale("ck", h, m, half(CK, m, h))
            for h in range(2):
                for m in range(6):
                    add("cq", h, m, None)
            for h in range(2):
                for m in range(6):
                    scale("cq", h, m, half(Y, m, h))
            pool.wait_ge(ck_val, 8)
            nc.gpsimd.tensor_copy(CS[:, :, :], CK[:, :, TP:T]).then_inc(cs_done, 1)
            lo_steps("uq")
            lo_steps("kvh")
            lo_steps("uv")
            lo_steps("wo")
            after_mixer("y1", "x3")
            mlp(1)

        @block.vector
        def _(dve):
            steps = [0]

            def link(ins):
                steps[0] += 1
                ins.then_inc(dve_step, 1)
                dve.wait_ge(dve_step, steps[0])

            def lo(v, h, m, src):
                dve.wait_ge(a_hi, A(v, h, m))
                g = gain_of[v]
                if g:
                    nc.vector.scalar_tensor_tensor(out=half(AL, m, h), in0=src, scalar=gain(g, m),
                                                   in1=half(AH, m, h).bitcast(F32), op0=ALU.mult, op1=ALU.subtract)\
                        .then_inc(a_lo, 1)
                else:
                    nc.vector.tensor_tensor(half(AL, m, h), src, half(AH, m, h).bitcast(F32), ALU.subtract)\
                        .then_inc(a_lo, 1)

            def row(st, h):
                dve.wait_ge(sum_done, SUM(st, h))
                f = R1[:, h, :]
                if st in ("m0", "m1"):
                    link(nc.vector.tensor_tensor(acc[:, h, :], f, f, ALU.mult))
                    f = acc[:, h, :]
                link(nc.vector.tensor_tensor(R2[:, h, :], f, f, ALU.mult))
                nc.vector.tensor_tensor(root[:, h, :], bank[4 + h][:, 0:H], R2[:, h, :], ALU.mult).then_inc(row_step, 1)

            def rstd(st, h):
                dve.wait_ge(root_done, ROOT(st, h))
                if st in SCALED_BY_INPUT:
                    link(nc.vector.reciprocal(root[:, h, :], root[:, h, :]))
                    f = acc[:, h, :] if st in ("m0", "m1") else R1[:, h, :]
                    nc.vector.tensor_tensor(R2[:, h, :], root[:, h, :], f, ALU.mult).then_inc(rstd_done, 1)
                else:
                    r = R1 if st[0] == "x" else R2
                    nc.vector.reciprocal(r[:, h, :], root[:, h, :]).then_inc(rstd_done, 1)

            def update(st, h, post, v):
                for m in range(KT + 1):
                    if m < KT:
                        dve.wait_ge(sc_done, SC(st, h, m))
                        nc.vector.scalar_tensor_tensor(out=half(X, m, h), in0=scaled[:, SC(st, h, m) % 2, :],
                                                       scalar=gain(post, m), in1=half(X, m, h), op0=ALU.mult,
                                                       op1=ALU.add).then_inc(x_done, 1)
                    if m:
                        lo(v, h, m - 1, half(X, m - 1, h))

            def evacuate(phase, dst, units):
                for n, (h, m) in enumerate(units):
                    u = UNIT0[phase] + n
                    dve.wait_ge(unit_done, u + 1)
                    nc.vector.tensor_copy(dst(h, m), bank[u % BANKS][:, 0:H]).then_inc(bank_free, 1)

            pairs = [(h, 2 * j + t) for j in range(4) for h in range(2) for t in range(2)]

            for e in range(0, 26, 2):
                dve.wait_ge(turned, e + 1)
                src = bank[4 + e % 4]
                if e == 0:
                    nc.vector.tensor_copy(gains[:, :], src[:, 0:NG]).then_inc(unturned_v, 1)
                elif e < 18:
                    nc.vector.tensor_copy(X[:, (e - 2) // 2, 0:TP], src[:, 0:TP]).then_inc(unturned_v, 1)
                else:
                    nc.vector.tensor_copy(V[:, e - 18, VP:VW].rearrange("p (s c) -> p s c", s=NS)[:, :, 0:CW - 1],
                                          src[:, 0:2 * SG].rearrange("p (s c) -> p s c", s=NS)).then_inc(unturned_v, 1)
            dve.wait_ge(unturned_v, 13)
            dve.wait_ge(unturned_a, 13)
            for h in range(2):
                for m in range(KT):
                    lo("x0", h, m, half(X, m, h))
            for h in range(2):
                rstd("x0", h)
            dve.wait_ge(rstd_done, 2)

            with dve.Fori(0, 2) as i:
                for j in range(4):
                    for h in range(2):
                        for t, buf in enumerate((scaled, prod)):
                            n = 4 * j + 2 * h + t
                            dve.wait_ge(unit_done, n + 1 + 16 * i)
                            if t == 0:
                                dve.wait_ge(v_done, 3 * j + 1 + 2 * h + 12 * i)
                            nc.vector.tensor_tensor(buf[:, h, :], bank[n % BANKS][:, 0:H], R1[:, h, :], ALU.mult)\
                                .then_inc(bank_free, 1)
                    vm = V[:, bass.ds(4 * i + j, 1), :]
                    ym = Y[:, bass.ds(4 * i + j, 1), :]
                    gm = gains[:, bass.ds(GCOL["dw_bias"] + 4 * i + j, 1)]
                    wm = taps[:, bass.ds(4 * i + j, 1), :]
                    dve.wait_ge(v_done, 3 * j + 6 + 12 * i)
                    for c in range(CW):
                        for part in range(2):
                            if part == 0:
                                dst, src = ym[:, 0, 0:TP], vm[:, 0, c:c + TP]
                            else:
                                dst = ym[:, 0, TP:T].rearrange("p (s t) -> p s t", s=NS)
                                src = vm[:, 0, VP:VW].rearrange("p (s c) -> p s c", s=NS)[:, :, c:c + TQ]
                            w = wm[:, 0, c:c + 1]
                            if c == 0:
                                nc.vector.tensor_scalar(dst, src, w, gm, ALU.mult, ALU.add).then_inc(conv_step, 1)
                            else:
                                dve.wait_ge(conv_step, 2 * CW * j + 2 * c + part - 1 + 8 * CW * i)
                                nc.vector.scalar_tensor_tensor(out=dst, in0=src, scalar=w, in1=dst, op0=ALU.mult,
                                                               op1=ALU.add).then_inc(conv_step, 1)
            dve.wait_ge(conv_step, 2 * CW * KT)

            for h in range(2):
                dve.wait_ge(sum_done, SUM("lm", h))
                nc.vector.tensor_scalar(R2[:, h, :], bank[4 + h][:, 0:H], 1.0 / D, None, ALU.mult).then_inc(rstd_done, 1)
            for h in range(2):
                dve.wait_ge(rstd_done, RSTD("lm", h))
                for m in range(KT):
                    nc.vector.tensor_tensor(half(Y, m, h), half(Y, m, h), R2[:, h, :], ALU.subtract).then_inc(centred, 1)
            dve.wait_ge(centred, 16)
            for h in range(2):
                rstd("lv", h)
                for m in range(KT + 1):
                    if m < KT:
                        n, k = KT * h + m, SC("sw", h, m) % 2
                        dve.wait_ge(sw_sig, n + 1)
                        nc.vector.tensor_scalar(scaled[:, k, :], scaled[:, k, :], gain("ln_g", m), gain("ln_b", m),
                                                ALU.mult, ALU.add).then_inc(sw_lin, 1)
                        dve.wait_ge(sw_lin, n + 1)
                        nc.vector.tensor_tensor(prod[:, n % 2, :], prod[:, n % 2, :], scaled[:, k, :], ALU.mult)\
                            .then_inc(sw_val, 1)
                    if m:
                        lo("sw", h, m - 1, prod[:, (n if m == KT else n - 1) % 2, :])

            def after_mixer(phase, st, post, v, stx):
                evacuate(phase, lambda h, m: half(Y, m, h), pairs)
                for h in range(2):
                    rstd(st, h)
                    update(st, h, post, v)

            def mlp(layer):
                phase, v = f"mlp{layer}", f"g{layer}"
                u0, b0 = UNIT0[phase], UP * NCH * layer
                dve.wait_ge(y_zero, 2 * layer + 2)
                with dve.Fori(0, NCH) as i:
                    for n in range(UP):
                        dve.wait_ge(relu_done, b0 + n + 1 + UP * i)
                        dve.wait_ge(u_lo, b0 + n + 1 + UP * i)
                        nc.vector.tensor_tensor(prod[:, n % 2, :], scaled[:, n % 2, :], bank[(u0 + n) % BANKS][:, 0:H],
                                                ALU.mult).then_inc(bank_free, 1)
                    for n in range(UP, CHUNK):
                        k = n - UP
                        h, m = (k % 8) // 4, 4 * (k // 8) + k % 4
                        dve.wait_ge(unit_done, u0 + n + 1 + CHUNK * i)
                        nc.vector.tensor_tensor(half(Y, m, h), half(Y, m, h), bank[(u0 + n) % BANKS][:, 0:H], ALU.add)\
                            .then_inc(bank_free, 1)
                for h in range(2):
                    rstd(f"x{2 * layer + 1}", h)
                for e in range(4):
                    kt, part = e // 2, e % 2
                    a, b = (0, TP) if part == 0 else (TP, T)
                    dve.wait_ge(p_hi, 4 * layer + e + 1)
                    nc.vector.tensor_tensor(BL[:, kt, a:b], bank[6 + part][:, 0:b - a], BH[:, kt, a:b].bitcast(F32),
                                            ALU.subtract).then_inc(p_lo, 1)
                st = f"m{layer}"
                for h in range(2):
                    dve.wait_ge(rstd_done, RSTD(f"x{2 * layer + 1}", h))
                    row(st, h)
                    rstd(st, h)
                up = UNIT0[f"ple{layer}"]
                for h in range(2):
                    update(st, h, f"ff_post{layer}", v)
                    for m in range(KT):
                        u = up + 8 * h + m
                        dve.wait_ge(unit_done, u + 1)
                        nc.vector.tensor_copy(half(Y, m, h), bank[u % BANKS][:, 0:H]).then_inc(bank_free, 1)
                ug = UNIT0[f"gate{layer}"]
                for n, (h, m) in enumerate(GATE_ORDER):
                    u = ug + n
                    dve.wait_ge(sig_done, 16 * layer + n + 1)
                    nc.vector.tensor_tensor(scaled[:, n % 2, :], prod[:, n % 2, :], half(Y, m, h), ALU.mult)\
                        .then_inc(bank_free, 1)
                    dve.wait_ge(bank_free, freed(u))
                    nc.vector.tensor_tensor(half(X, m, h), half(X, m, h), scaled[:, n % 2, :], ALU.add)\
                        .then_inc(xg_done, 1)

            after_mixer("pw2", "y0", "mix_post0", "ff0", "x1")
            mlp(0)

            for h in range(2):
                for m in range(KT):
                    lo("kv", h, m, half(X, m, h))
            krow = [(h, 4) for h in range(2)]
            evacuate("dkv", lambda h, m: half(CK, m, h) if m < 4 else KR[:, h * H:(h + 1) * H], pairs[:8] + krow)
            for h in range(2):
                rstd("x2", h)
            dve.wait_ge(rstd_done, RSTD("x2", 1))
            r1 = R1[:, :, :].rearrange("p a b -> p (a b)")
            dve.wait_ge(bank_free, freed(UNIT0["dkv"] + 9))
            link(nc.vector.tensor_tensor(KR, KR, r1, ALU.mult))
            for h in range(2):
                for m in range(KT):
                    lo("mx", h, m, half(X, m, h))
            evacuate("dq", lambda h, m: half(Y, m, h), pairs[:12])
            for h in range(2):
                row("ck", h)
                rstd("ck", h)
            for h in range(2):
                for m in range(4):
                    dve.wait_ge(sc_done, SC("ck", h, m))
                    nc.vector.tensor_scalar(half(CK, m, h), scaled[:, SC("ck", h, m) % 2, :], gain("kv_norm", m), None,
                                            ALU.mult).then_inc(ck_val, 1)
            for h in range(2):
                for m in range(4):
                    dve.wait_ge(b_hi, 4 * h + m + 1)
                    nc.vector.tensor_tensor(half(BL, m, h), half(CK, m, h), half(BH, m, h).bitcast(F32),
                                            ALU.subtract).then_inc(b_lo, 1)
            for h in range(2):
                row("cq", h)
                rstd("cq", h)
            for h in range(2):
                for m in range(6):
                    lo("cq", h, m, scaled[:, SC("cq", h, m) % 2, :])

            def rotate(n, t):
                dve.wait_ge(rot_done, n + 1)
                for b, c0, c1 in ((6, 0, TP), (7, TP, T)):
                    nc.vector.tensor_tensor(flat["prod"][:, c0:c1], bank[b][:, 0:c1 - c0], SIN[:, c0:c1], ALU.mult)\
                        .then_inc(rope_step, 1)
                nc.vector.tensor_tensor(t, t, COS, ALU.mult).then_inc(rope_step, 1)
                dve.wait_ge(rope_step, 4 * n + 3)
                nc.vector.tensor_tensor(t, t, flat["prod"][:, 0:T], ALU.add).then_inc(rope_step, 1)
                dve.wait_ge(rope_step, 4 * n + 4)

            dve.wait_ge(rope_in, 16)
            rotate(0, KR)
            for n, (h, m) in enumerate(pairs + pairs[:8]):
                u = UNIT0["uq"] + n
                dve.wait_ge(unit_done, u + 1)
                dst = half(Y, m, h) if n < 16 else half(QR, m, h)
                nc.vector.tensor_copy(dst, bank[u % BANKS][:, 0:H]).then_inc(bank_free, 1)
            dve.wait_ge(bank_free, freed(UNIT0["uq"] + 23))
            for j in range(4):
                rotate(1 + j, QR[:, j, :])
            for e in range(2):
                for r in range(2):
                    nc.vector.tensor_copy(DUP[:, e, DR * r:DR * r + DR], ident[:, DR * e:DR * e + DR]).then_inc(dup_set, 1)
            dve.wait_ge(qrs_mm, 1)
            nc.vector.tensor_copy(QRS.rearrange("p (s h t) -> p h s t", s=NS, h=NH),
                                  bank[5][:, 0:512].rearrange("p (h s t) -> p h s t", s=NS, h=NH)).then_inc(qrs_c, 1)

            dve.wait_ge(consts, 48)
            dve.wait_ge(kv_out, 32 * 5)
            def head_values(hd):
                dve.wait_ge(v_mm, hd // 2 + 1)
                if hd:
                    dve.wait_ge(pv_mm, hd)
                for q in range(2):
                    nc.vector.tensor_copy(vn[:, 256 * q:256 * q + 256].rearrange("p (k v) -> p k v", k=2),
                                          bank[1 + q][:, 0:512].rearrange("p (k e v) -> p k e v", k=2, e=2)[:, :, hd % 2])\
                        .then_inc(v_used, 1)

            def head_uk(hd):
                dve.wait_ge(uk_mm, hd + 1)
                if hd:
                    dve.wait_ge(ql_mm, hd)
                nc.vector.tensor_copy(ukT, bank[3][:, 0:CL]).then_inc(uk_used, 1)

            def head_latent(hd):
                dve.wait_ge(ql_mm, hd + 1)
                nc.vector.tensor_copy(QLAT.rearrange("p c (s h t) -> p c s h t", s=NS, h=NH)[:, :, :, hd, :],
                                      bank[3][:, 0:256].rearrange("p (c s t) -> p c s t", c=4, s=NS))\
                    .then_inc(ql_used, 1)

            def top(hd, qb):
                n, c = 4 * hd + qb, 4 * (qb % 2)
                b = bank[4 + n % 2]
                dve.wait_ge(s_mm, n + 1)
                nc.vector.tensor_tensor(b[:, qb * P:(qb + 1) * P], b[:, qb * P:(qb + 1) * P], cmask, ALU.add)\
                    .then_inc(s_masked, 1)
                dve.wait_ge(s_masked, n + 1)
                nc.vector.tensor_reduce(tiny[:, c:c + 1], b[:, 0:(qb + 1) * P], AX.X, ALU.max).then_inc(s_max, 1)
                dve.wait_ge(s_max, 2 * n + 1)
                nc.vector.tensor_scalar(tiny[:, c + 1:c + 2], tiny[:, c:c + 1], -SCALE, None, ALU.mult)\
                    .then_inc(s_max, 1)

            def norm(hd, qb):
                n, c = 4 * hd + qb, 4 * (qb % 2)
                dve.wait_ge(s_exp, n + 1)
                nc.vector.reciprocal(tiny[:, c + 3:c + 4], tiny[:, c + 2:c + 3]).then_inc(s_rec, 1)
                dve.wait_ge(s_rec, n + 1)
                w = (qb + 1) * P
                nc.vector.tensor_scalar(PB[n % 2][:, 0:w], PB[n % 2][:, 0:w], tiny[:, c + 3:c + 4], None,
                                        ALU.mult).then_inc(p_ready, 1)

            def head_out(hd):
                dve.wait_ge(a_hi, A("o", 0, hd))
                nc.vector.tensor_tensor(AL[:, hd, 0:TP], bank[7][:, 0:TP], AH[:, hd, 0:TP].bitcast(F32), ALU.subtract)\
                    .then_inc(a_lo, 1)

            head_uk(0)
            head_latent(0)
            for hd in range(NH):
                top(hd, 0)
                head_values(hd)
                top(hd, 1)
                norm(hd, 0)
                norm(hd, 1)
                top(hd, 2)
                if hd < NH - 1:
                    head_uk(hd + 1)
                norm(hd, 2)
                if hd:
                    head_out(hd - 1)
                top(hd, 3)
                if hd < NH - 1:
                    head_latent(hd + 1)
                norm(hd, 3)
            head_out(NH - 1)

            dve.wait_ge(cs_done, 1)
            dve.wait_ge(ql_used, NH)

            def gather(i):
                dve.wait_ge(new_nat, i + 1)
                nc.vector.tensor_copy(NK, CS[:, :, bass.ds(TQ * i, TQ)]).then_inc(new_in, 1)
                nc.vector.tensor_copy(NKR, KR[0:DR, bass.ds(TP + TQ * i, TQ)]).then_inc(new_in, 1)
                nc.vector.tensor_copy(QS, QLAT[:, :, bass.ds(64 * i, 64)]).then_inc(new_in, 1)
                for r in range(2):
                    rows = slice(DR * r, DR * r + DR)
                    nc.vector.tensor_copy(QSR[rows, r, :], QRS[rows, bass.ds(64 * i, 64)]).then_inc(new_in, 1)

            def queries(i):
                dve.wait_ge(q_hi, 2 + 2 * i)
                nc.vector.tensor_tensor(AL[:, 0:4, TP:T], QS, AH[:, 0:4, TP:T].bitcast(F32), ALU.subtract)\
                    .then_inc(q_lo, 1)
                nc.vector.tensor_tensor(AL[:, 4:6, TP:T], QSR, AH[:, 4:6, TP:T].bitcast(F32), ALU.subtract)\
                    .then_inc(q_lo, 1)

            def key(c, n):
                dve.wait_ge(key_hi, c + 1 + 5 * n)
                dst, part, src = (BL[:, c, 0:TP], BH[:, c, 0:TP], bank[4 + c][:, 0:TP]) if c < 4 else \
                    (BL[:, :, TP:T], BH[:, :, TP:T], rope_bank)
                nc.vector.tensor_tensor(dst, src, part.bitcast(F32), ALU.subtract).then_inc(key_lo, 1)

            def step(ins):
                ins.then_inc(sm_step, 1)

            def new_top(i):
                dve.wait_ge(new_mm, 1 + i)
                step(nc.vector.tensor_tensor(SN, bank[3][0:64, 256:264], nmask, ALU.add))
                dve.wait_ge(sm_step, SM("mask") + NSM * i)
                step(nc.vector.tensor_reduce(col(TOP, 4), SN, AX.X, ALU.max))

            def keep(i):
                dve.wait_ge(out_mm, 1 + i)
                nc.vector.tensor_copy(QLAT[:, :, bass.ds(64 * i, 64)],
                                      bank[7][:, 0:256].rearrange("p (c q) -> p c q", c=4)).then_inc(lat_out, 1)

            def slab(j, i, first, last):
                if j == 3 and not last:
                    gather(i + 1)
                dve.wait_ge(score_mm, j + 2 + 4 * i)
                step(nc.vector.tensor_reduce(col(TOP, j), bank[0][0:64, :], AX.X, ALU.max))
                dve.wait_ge(sm_step, SM("top", j) + NSM * i)
                if j == 0:
                    step(nc.vector.tensor_scalar(col(NM, 0), col(TOP, 0), col(TOP, 4), -SCALE, ALU.max, ALU.mult))
                else:
                    step(nc.vector.tensor_scalar(col(NM, j), col(TOP, j), -SCALE, col(NM, j - 1), ALU.mult, ALU.min))
                if j == 1 and not first:
                    keep(i - 1)
                if not last:
                    for c in range(5):
                        key(c, j + 1 + 4 * i)
                    if j == 3:
                        queries(i + 1)
                dve.wait_ge(exp_done, 2 * j + 2 + 8 * i)
                if j == 0:
                    step(nc.vector.tensor_tensor(col(SUMQ, 0), col(PSUMS, 0), col(PSUMS, 4), ALU.add))
                else:
                    step(nc.vector.tensor_scalar(col(SUMQ, j), col(SUMQ, j - 1), col(ALPHA, j), col(PSUMS, j),
                                                 ALU.mult, ALU.add))

            def gain_output(j, i):
                dve.wait_ge(pe_read_raw, 5 + j + 4 * i)
                if j == 0:
                    nc.vector.tensor_copy(OUT, bank[2][0:64, :]).then_inc(out_done, 1)
                else:
                    dve.wait_ge(out_done, j + OUTS * i)
                    nc.vector.scalar_tensor_tensor(out=OUT, in0=OUT, scalar=col(ALPHA, j), in1=bank[2][0:64, :],
                                                   op0=ALU.mult, op1=ALU.add).then_inc(out_done, 1)

            def finish(i):
                gain_output(3, i)
                dve.wait_ge(out_done, 4 + OUTS * i)
                nc.vector.reciprocal(col(SUMQ, 4), col(SUMQ, 3)).then_inc(out_done, 1)
                dve.wait_ge(out_done, 5 + OUTS * i)
                nc.vector.tensor_scalar(OUTN, OUT, col(SUMQ, 4), None, ALU.mult).then_inc(out_done, 1)

            def sequence(i, first, last):
                for j in range(4):
                    slab(j, i, first, last and j == 3)
                    if j:
                        gain_output(j - 1, i)
                    elif not first:
                        finish(i - 1)
                if not last:
                    new_top(i + 1)

            nc.vector.memset(QSR, 0.0).then_inc(qsr_zero, 1)
            dve.wait_ge(qsr_zero, 1)
            gather(0)
            queries(0)
            for c in range(5):
                key(c, 0)
            new_top(0)
            sequence(0, True, False)
            with dve.Fori(1, NS - 1) as i:
                sequence(i, False, False)
            sequence(NS - 1, False, True)
            finish(NS - 1)
            keep(NS - 1)
            dve.wait_ge(b_hi, 9)
            nc.vector.tensor_tensor(BL[:, :, 0:TP], QLAT[:, :, :], BH[:, :, 0:TP].bitcast(F32), ALU.subtract)\
                .then_inc(b_lo, 1)
            for hd in range(NH):
                dve.wait_ge(a_hi, A("o", 1, hd))
                nc.vector.tensor_tensor(AL[:, hd, TP:T], bank[hd % 4][:, 0:TS], AH[:, hd, TP:T].bitcast(F32),
                                        ALU.subtract).then_inc(a_lo, 1)
            after_mixer("wo", "y1", "mix_post1", "ff1", "x3")
            mlp(1)
            for b, (t0, n) in enumerate(tokens):
                dve.wait_ge(y_turned, 2 * b + 2)
                if b >= 2:
                    dve.wait_ge(y_out[b % 2], 16 * (b // 2))
                nc.vector.tensor_copy(yflat[0:n, (b % 2) * D + 512:(b % 2) * D + D], bank[5 + 2 * (b % 2)][0:n, 0:512])\
                    .then_inc(y_copied_v, 1)

        @block.tensor
        def _(pe):
            def three(out, wsl, hl, first, last, kslices):
                (wh, wl), (xh, xl) = wsl, hl
                nc.tensor.matmul(out, wh, xh, start=first, stop=False)
                nc.tensor.matmul(out, wh, xl, start=False, stop=False)
                return nc.tensor.matmul(out, wl, xh, start=False, stop=last)

            def wslab(d, kt, n, k, c):
                a = k * n + c
                return WH[:, d % WRING, a:a + P], WL[:, d % WRING, a:a + P]

            def ab(hi_t, lo_t, k, h):
                return half(hi_t, k, h), half(lo_t, k, h)

            def unit(u, d, kt, n, c, h, src, ready=None, i=None, per_iter=0, last_of_slab=False):
                b = bank[u % BANKS][:, 0:H]
                pe.wait_ge(bank_free, u + 1 if i is None else u + 1 + per_iter * i)
                for k in range(kt):
                    if ready:
                        ready(k)
                    ins = three(b, wslab(d, kt, n, k, c), ab(*src, k, h), k == 0, k == kt - 1, None)
                ins.then_inc(unit_done, 1)

            def slab_ready(d, i=None):
                pe.wait_ge(lo_done, d + 1 if i is None else d + 1 + RING * i)

            def slab_used(d):
                pe.wait_ge(unit_done, 0)

            Asrc, Bsrc = (AH, AL), (BH, BL)

            def total(st, h):
                pe.wait_ge(acc_done, ACC(st, h, NT[st] - 1))
                before = [k for k in SUMS[:SUMS.index((st, h))] if k[1] == h]
                if before:
                    pe.wait_ge(rstd_done, RSTD(*before[-1]))
                nc.tensor.matmul(bank[4 + h][:, 0:H], ones[:, :], acc[:, h, :], start=True, stop=True)\
                    .then_inc(sum_done, 1)

            def product(phase, kt, n, tiles, v, slabs=None, src=None):
                u = UNIT0[phase]
                for j in range(SLABS[phase]):
                    d = DENSE0[phase] + j
                    slab_ready(d)
                    w = n[j] if isinstance(n, tuple) else n
                    nt = w // P if phase not in ("dkv",) else w // P
                    for h in range(2):
                        for t in range(nt):
                            def ready(k, h=h):
                                if v and j == 0 and t == 0:
                                    pe.wait_ge(a_lo, A(v, h, k))
                            b = bank[u % BANKS][:, 0:H]
                            pe.wait_ge(bank_free, u + 1)
                            for k in range(kt):
                                ready(k)
                                ins = three(b, wslab(d, kt, w, k, t * P), ab(*(src or Asrc), k, h), k == 0,
                                            k == kt - 1, None)
                            ins.then_inc(unit_done, 1)
                            u += 1

            pe.wait_ge(consts, 16)
            pe.wait_ge(x_in, 80)
            pe.wait_ge(vecs, 16 * (len(GAINS) + 3))
            for e in range(26):
                if e >= 4:
                    s = unturned_v if e % 2 == 0 else unturned_a
                    pe.wait_ge(s, e // 2 - 1)
                dst = bank[4 + e % 4]
                if e == 0:
                    ins = nc.tensor.transpose(dst[:, 0:NG], flat["prod"][0:NG, 0:P], ident[0:NG, 0:NG])
                elif e == 1:
                    for m in range(KT):
                        ins = nc.tensor.transpose(dst[:, m * CW:(m + 1) * CW], taps_stage[0:CW, m * P:(m + 1) * P],
                                                  ident[0:CW, 0:CW])
                elif e < 18:
                    m = (e - 2) // 2
                    if e % 2 == 0:
                        for b in range(4):
                            ins = nc.tensor.transpose(dst[:, b * P:(b + 1) * P],
                                                      yflat[:, b * D + m * P:b * D + (m + 1) * P], ident[:, :])
                    else:
                        ins = nc.tensor.transpose(dst[:, 0:TS], x_stage[0:TS, m * P:(m + 1) * P], ident[0:TS, 0:TS])
                else:
                    m = e - 18
                    for g in range(2):
                        ins = nc.tensor.transpose(dst[:, g * SG:(g + 1) * SG], state_stage[0:SG, g, m * P:(m + 1) * P],
                                                  ident[0:SG, 0:SG])
                ins.then_inc(turned, 1)
            pe.wait_ge(ones_set, 3)
            for h in range(2):
                total("x0", h)

            with pe.Fori(0, 2) as i:
                for j in range(4):
                    slab_ready(j, i)
                    for h in range(2):
                        for t in range(2):
                            u = 4 * j + 2 * h + t
                            pe.wait_ge(bank_free, u + 1 + 16 * i)
                            for k in range(KT):
                                if j == 0 and t == 0:
                                    pe.wait_ge(a_lo, A("x0", h, k))
                                ins = three(bank[u % BANKS][:, 0:H], wslab(j, KT, 256, k, t * P), ab(*Asrc, k, h),
                                            k == 0, k == KT - 1, None)
                            ins.then_inc(unit_done, 1)
            pe.wait_ge(rstd_done, RSTD("x0", 1))
            for e, (m, g) in enumerate(STATES):
                pe.wait_ge(v_done, 3 * KT + 3 if m is None else 3 * m + 6)
                if e >= 4:
                    pe.wait_ge(state_copied, e - 3)
                for q in range(4):
                    if m is None:
                        rows = V[:, 4 * g + q, TP:VP]
                    else:
                        a = VP + (4 * g + q) * VSQ + TQ
                        rows = V[:, m, a:a + CW - 1]
                    ins = nc.tensor.transpose(bank[4 + e % 4][0:CW - 1, q * P:(q + 1) * P], rows, ident[:, :])
                ins.then_inc(state_done, 1)
            pe.wait_ge(state_copied, len(STATES))
            for st in ("lm", "lv"):
                for h in range(2):
                    total(st, h)
            product("pw2", KT, 256, 2, "sw")
            for h in range(2):
                total("y0", h)

            def mlp(layer):
                phase = f"mlp{layer}"
                d0, u0, b0 = DENSE0[phase], UNIT0[phase], UP * NCH * layer
                with pe.Fori(0, NCH) as i:
                    n = 0
                    for j in range(4):
                        slab_ready(d0 + j, i)
                        for h in range(2):
                            for t in range(2 if j < 2 else 4):
                                pe.wait_ge(bank_free, u0 + n + 1 + CHUNK * i)
                                dst = bank[(u0 + n) % BANKS][:, 0:H]
                                for k in range(KT if j < 2 else FC):
                                    if j == 0 and t == 0:
                                        pe.wait_ge(a_lo, A(f"ff{layer}", h, k))
                                    if j == 2 and t == 0:
                                        pe.wait_ge(u_lo, b0 + up_n(h, k) + 3 + UP * i)
                                    if j < 2:
                                        ins = three(dst, wslab(d0 + j, KT, 256, k, t * P), ab(*Asrc, k, h), k == 0,
                                                    k == KT - 1, None)
                                    else:
                                        ins = three(dst, wslab(d0 + j, FC, 512, k, t * P), ab(*Bsrc, k, h), k == 0,
                                                    k == FC - 1, None)
                                ins.then_inc(unit_done, 1)
                                n += 1
                for h in range(2):
                    total(f"x{2 * layer + 1}", h)
                pe.wait_ge(p_in, 80 * (layer + 1))
                for e in range(4):
                    kt, part = e // 2, e % 2
                    if e >= 2:
                        pe.wait_ge(p_lo, 4 * layer + e - 1)
                    if part == 0:
                        for b in range(4):
                            ins = nc.tensor.transpose(bank[6][:, b * P:(b + 1) * P], p_stage[:, b, kt * P:(kt + 1) * P],
                                                      ident[:, :])
                    else:
                        ins = nc.tensor.transpose(bank[7][:, 0:TS], p_stage[0:TS, 4, kt * P:(kt + 1) * P],
                                                  ident[0:TS, 0:TS])
                    ins.then_inc(p_turned, 1)
                for h in range(2):
                    total(f"m{layer}", h)
                pe.wait_ge(p_lo, 4 * layer + 4)
                product(f"ple{layer}", 2, D, 8, None, src=Bsrc)
                product(f"gate{layer}", KT, 256, 2, f"g{layer}")

            mlp(0)
            product("dkv", KT, (256, 256, 128), 2, "kv")
            for h in range(2):
                total("x2", h)
            product("dq", KT, 256, 2, "mx")
            for st in ("ck", "cq"):
                for h in range(2):
                    total(st, h)

            def rot(n, t):
                if n:
                    pe.wait_ge(rope_step, 4 * n)
                nc.tensor.matmul(bank[6][:, 0:TP], ROT, t[:, 0:TP], start=True, stop=True)
                nc.tensor.matmul(bank[7][:, 0:TS], ROT, t[:, TP:T], start=True, stop=True).then_inc(rot_done, 1)

            pe.wait_ge(rope_in, 16)
            pe.wait_ge(dve_step, KR_STEP)
            rot(0, KR)
            u = UNIT0["uq"]
            for j in range(6):
                d = DENSE0["uq"] + j
                slab_ready(d)
                for h in range(2):
                    for t in range(2):
                        pe.wait_ge(bank_free, u + 1)
                        for k in range(6):
                            if j == 0 and t == 0:
                                pe.wait_ge(a_lo, A("cq", h, k))
                            ins = three(bank[u % BANKS][:, 0:H], wslab(d, 6, 256, k, t * P), ab(*Asrc, k, h), k == 0,
                                        k == 5, None)
                        ins.then_inc(unit_done, 1)
                        u += 1
                if j < 5:
                    t0, n = tokens[j]
                    pe.wait_ge(rope_step, 4)
                    pe.wait_ge(rstd_done, RSTD("cq", 1))
                    if j:
                        pe.wait_ge(kv_staged, 2 * j)
                    for c in range(4):
                        nc.tensor.transpose(bank[4][0:n, c * P:(c + 1) * P], CK[:, c, t0:t0 + n], ident[:, :])
                    nc.tensor.transpose(bank[5][0:n, 0:DR], KR[0:DR, t0:t0 + n], ident[0:DR, 0:DR])\
                        .then_inc(kv_turned, 1)
            pe.wait_ge(bank_free, freed(u - 1))
            for j in range(4):
                rot(1 + j, QR[:, j, :])
            pe.wait_ge(rope_step, 20)
            pe.wait_ge(kv_staged, 10)
            pe.wait_ge(dup_set, 4)
            for h in range(NH):
                e = h % 2
                ins = nc.tensor.matmul(bank[5][:, h * TS:(h + 1) * TS], DUP[:, e, :],
                                       QR[:, h // 2, TP:T], start=True, stop=True)
            ins.then_inc(qrs_mm, 1)

            pe.wait_ge(qrs_c, 1)

            def head_slab(hd):
                return (DENSE0["kvh"] + hd // 2) % WRING, RAW[:, (RAW0["kvh"] + hd // 2) % RING]

            def head_keys(hd):
                w = head_slab(hd)[0]
                slab_ready(DENSE0["kvh"] + hd // 2)
                if hd:
                    pe.wait_ge(kvt_used, hd)
                for k in range(4):
                    a = k * 256 + hd % 2 * P
                    ins = three(bank[0][:, 0:TP], (WH[:, w, a:a + P], WL[:, w, a:a + P]),
                                (BH[:, k, 0:TP], BL[:, k, 0:TP]), k == 0, k == 3, None)
                ins.then_inc(kvt_done, 1)

            def pair_values(hd, q):
                w = head_slab(hd)[0]
                if hd and q == 0:
                    pe.wait_ge(v_used, 2 * hd)
                for kb in (2 * q, 2 * q + 1):
                    for k in range(4):
                        a = 1024 + k * 256
                        ins = three(bank[1 + q][:, (kb % 2) * 256:(kb % 2) * 256 + 256],
                                    (BH[:, k, kb * P:(kb + 1) * P], BL[:, k, kb * P:(kb + 1) * P]),
                                    (WH[:, w, a:a + 256], WL[:, w, a:a + 256]), k == 0, k == 3, None)
                if q == 1:
                    ins.then_inc(v_mm, 1)

            def head_uk(hd):
                raw = head_slab(hd)[1]
                if hd:
                    pe.wait_ge(ql_used, hd)
                for k in range(4):
                    a = k * 256 + hd % 2 * P
                    ins = nc.tensor.transpose(bank[3][:, k * P:(k + 1) * P], raw[:, a:a + P], ident[:, :])
                ins.then_inc(uk_mm, 1)

            def head_latent(hd):
                pe.wait_ge(uk_used, hd + 1)
                if hd % 2:
                    pe.sem_inc(pe_read_raw, 1)
                for c in range(4):
                    ins = nc.tensor.matmul(bank[3][:, c * TS:(c + 1) * TS], ukT[:, c * P:(c + 1) * P], Y[:, hd, TP:T],
                                           start=True, stop=True)
                ins.then_inc(ql_mm, 1)

            def head_scores(hd, qb):
                n, w = 4 * hd + qb, (qb + 1) * P
                if qb == 0:
                    pe.wait_ge(kvt_used, hd + 1)
                if n >= 2:
                    pe.wait_ge(s_exp, n - 1)
                r0 = DR * (hd % 2)
                q = slice(qb * P, (qb + 1) * P)
                dst = bank[4 + n % 2][:, 0:w]
                nc.tensor.matmul(dst, Y[:, hd, q], kT[:, 0:w], start=True, stop=False)
                nc.tensor.matmul(dst, QR[r0:r0 + DR, hd // 2, q], KR[r0:r0 + DR, 0:w], start=False, stop=True)\
                    .then_inc(s_mm, 1)

            def head_turn(hd, qb):
                n = 4 * hd + qb
                pe.wait_ge(p_ready, n + 1)
                if n:
                    pe.wait_ge(pt_used, n)
                for k in range(qb + 1):
                    ins = nc.tensor.transpose(bank[6][:, k * P:(k + 1) * P], PB[n % 2][:, k * P:(k + 1) * P],
                                              ident[:, :])
                ins.then_inc(pt_mm, 1)

            def head_out(hd):
                pe.wait_ge(pt_used, 4 * hd + 4)
                pe.wait_ge(v_used, 2 * hd + 2)
                if hd:
                    pe.wait_ge(a_lo, A("o", 0, hd - 1))
                for k in range(4):
                    ins = nc.tensor.matmul(bank[7][:, k * P:TP], vn[:, k * P:(k + 1) * P], PT[:, k, k * P:TP],
                                           start=k == 0, stop=k == 3)
                ins.then_inc(pv_mm, 1)

            head_keys(0)
            head_uk(0)
            for q in range(2):
                pair_values(0, q)
            head_latent(0)
            for hd in range(NH):
                more, pair = hd < NH - 1, hd % 2 == 1 and hd < NH - 1
                head_scores(hd, 0)
                if hd:
                    head_turn(hd - 1, 3)
                head_scores(hd, 1)
                if hd:
                    head_out(hd - 1)
                if more:
                    head_keys(hd + 1)
                head_turn(hd, 0)
                head_scores(hd, 2)
                if more:
                    head_uk(hd + 1)
                head_turn(hd, 1)
                if pair:
                    pair_values(hd + 1, 0)
                head_scores(hd, 3)
                if more:
                    head_latent(hd + 1)
                if pair:
                    pair_values(hd + 1, 1)
                head_turn(hd, 2)
            head_turn(NH - 1, 3)
            head_out(NH - 1)

            pe.wait_ge(a_lo, A("o", 0, NH - 1))
            pe.wait_ge(ql_used, NH)
            g0 = RAW0["cache"]

            def page_slab(j, c):
                src = RAW[:, (g0 + j) % RING]
                if c < 4:
                    for q in range(4):
                        ins = nc.tensor.transpose(bank[4 + c][:, q * P:(q + 1) * P],
                                                  src[:, q * CL + c * P:q * CL + (c + 1) * P], ident[:, :])
                else:
                    for q in range(2):
                        a = 4 * CL + q * P
                        ins = nc.tensor.transpose(bank[3][:, q * P:(q + 1) * P], src[:, a:a + P], ident[:, :])
                ins.then_inc(page_mm, 1)

            def keys(j, i, cs):
                if 0 in cs:
                    pe.wait_ge(landed[(g0 + j) % RING], LANDED[g0 + j] + 128 * i)
                for c in cs:
                    pe.wait_ge(key_lo, c + 1 + 5 * j + 20 * i)
                    if j == 1 and c == 4:
                        pe.wait_ge(sm_step, SM("mask") + NSM * i)
                    if j == 2 and c == 3:
                        pe.wait_ge(lat_out, 1 + i)
                    if j == 1 and c == 0:
                        pe.wait_ge(new_nat_c, 1 + i)
                    page_slab(j, c)

            def new_keys(i):
                pe.wait_ge(new_in, 5 + 5 * i)
                pe.wait_ge(key_lo, 10 + 20 * i)
                dst = bank[3][0:64, 256:264]
                for c in range(4):
                    nc.tensor.matmul(dst, QS[:, c, :], NK[:, c, :], start=c == 0, stop=False)
                nc.tensor.matmul(dst, QSR[0:DR, 0, :], NKR, start=False, stop=True).then_inc(new_mm, 1)
                for c in range(4):
                    ins = nc.tensor.transpose(bank[4][0:TQ, c * P:(c + 1) * P], NK[:, c, :], ident[:, :])
                ins.then_inc(new_nat, 1)

            def scores(j, i):
                pe.wait_ge(key_lo, 10 + 5 * j + 20 * i)
                if j == 0:
                    pe.wait_ge(q_lo, 2 + 2 * i)
                for c in range(4):
                    three(bank[0][0:64, 0:512], (AH[:, c, TP:T], AL[:, c, TP:T]), (BH[:, c, 0:TP], BL[:, c, 0:TP]),
                          c == 0, False, None)
                for r in range(2):
                    ins = three(bank[0][0:64, 256 * r:256 * r + 256].rearrange("p (a b) -> p a b", a=4),
                                (AH[:, 4 + r, TP:T], AL[:, 4 + r, TP:T]), (BH[:, :, TP:T], BL[:, :, TP:T]),
                                False, r == 1, None)
                ins.then_inc(score_mm, 1)

            def turn(j, i):
                pe.wait_ge(exp_done, (2 if j == 0 else 2 * j + 1) + 8 * i)
                pe.sem_inc(seen, 1)
                for k in range(4):
                    ins = nc.tensor.transpose(bank[1][:, k * 64:(k + 1) * 64], SP[:, k * P:(k + 1) * P],
                                              ident[0:64, 0:64])
                if j == 0:
                    ins = nc.tensor.transpose(bank[1][0:TQ, 256:320], PN, ident[0:64, 0:64])
                ins.then_inc(spt_mm, 1)

            def values(j, i):
                pe.wait_ge(spt_c, (j + 2 if j else 2) + 5 * i)
                dst = bank[2][0:64, 0:512]
                if j == 0:
                    pe.wait_ge(new_nat_c, 1 + i)
                    nc.tensor.matmul(dst, NPT, NEWC, start=True, stop=False)
                else:
                    pe.wait_ge(out_done, j + OUTS * i)
                src = RAW[:, (g0 + j) % RING]
                for k in range(4):
                    ins = nc.tensor.matmul(dst, SPT[:, k, :], src[:, k * CL:(k + 1) * CL], start=j > 0 and k == 0,
                                           stop=k == 3)
                ins.then_inc(pe_read_raw, 1)

            def give(i):
                pe.wait_ge(out_done, OUTS + OUTS * i)
                pe.sem_inc(seen, 1)
                for c in range(4):
                    ins = nc.tensor.transpose(bank[7][:, c * 64:(c + 1) * 64], OUTN[:, c * P:(c + 1) * P],
                                              ident[0:64, 0:64])
                ins.then_inc(out_mm, 1)

            def sequence(i, first, last):
                for j in range(4):
                    scores(j, i)
                    if j == 1 and not first:
                        give(i - 1)
                    if not (last and j == 3):
                        keys(*((j + 1, i) if j < 3 else (0, i + 1)), range(5))
                    if j:
                        values(j - 1, i)
                    elif not first:
                        values(3, i - 1)
                    turn(j, i)
                if not last:
                    new_keys(i + 1)

            keys(0, 0, range(5))
            new_keys(0)
            sequence(0, True, False)
            with pe.Fori(1, NS - 1) as i:
                sequence(i, False, False)
            sequence(NS - 1, False, True)
            values(3, NS - 1)
            give(NS - 1)
            pe.wait_ge(b_lo, 9)
            for hd in range(NH):
                d = DENSE0["uv"] + hd // 4
                if hd % 4 == 0:
                    slab_ready(d)
                if hd >= 4:
                    pe.wait_ge(a_lo, A("o", 1, hd - 4))
                for k in range(4):
                    a = k * 512 + (hd % 4) * P
                    rhs = [t[:, k, 0:TP].rearrange("p (s h t) -> p s h t", s=NS, h=NH)[:, :, hd, :] for t in (BH, BL)]
                    ins = three(bank[hd % 4][:, 0:TS].rearrange("p (s t) -> p s t", s=NS),
                                (WH[:, d % WRING, a:a + P], WL[:, d % WRING, a:a + P]), rhs, k == 0, k == 3, None)
                ins.then_inc(uv_mm, 1)
            pe.wait_ge(a_lo, A("o", 1, NH - 1))
            product("wo", KT, 256, 2, None)
            for h in range(2):
                total("y1", h)
            mlp(1)
            pe.wait_ge(xg_done, 32)
            for b, (t0, n) in enumerate(tokens):
                for q in range(2):
                    if b >= 2:
                        pe.wait_ge(y_copied_v if q else y_copied_a, b - 1)
                    for m in range(4):
                        ins = nc.tensor.transpose(bank[4 + 2 * (b % 2) + q][0:n, m * P:(m + 1) * P],
                                                  X[:, 4 * q + m, t0:t0 + n], ident[:, :])
                    ins.then_inc(y_turned, 1)


_INS = ["x_prompt", "x_sample", "state_conv", "cache_kv_latent", "cache_k_rope", "page_table", "p_prompt", "p_sample",
        "norm_mix_pre", "norm_mix_post", "norm_ff_pre", "norm_ff_post", "conv_pw1", "conv_dw", "conv_dw_bias",
        "conv_ln_g", "conv_ln_b", "conv_pw2", "kv_in_norm", "w_dkv", "kv_norm", "w_uk", "w_uv", "w_dq", "q_norm",
        "w_uq", "w_o", "w_up", "w_down", "ple_proj", "ple_gate"]
_OUTS = [("y_prompt", (1, TP, D)), ("y_sample", (NS, TQ, D)), ("new_conv_prompt", (1, 1, CW - 1, D)),
         ("new_conv_sample", (1, NS, CW - 1, D)), ("new_kv_prompt", (1, TP, CL)), ("new_kr_prompt", (1, TP, DR)),
         ("new_kv_sample", (NS, TQ, CL)), ("new_kr_sample", (NS, TQ, DR))]


def shape_constants():
    c = np.zeros((P, 1600), np.float32)
    c[:, 0:P] = np.eye(P)
    c[:, P:2 * P] = np.where(np.arange(P)[None, :] <= np.arange(P)[:, None], 0.0, NEG)
    new = np.where(np.arange(TQ)[None, :] <= np.arange(TQ)[:, None], 0.0, NEG)
    c[0:64, 256:264] = np.tile(new, (NH, 1))
    hd = DR // 2
    freqs = (np.float32(1.0) / np.float32(10000.0) ** (np.arange(hd, dtype=np.float32) / np.float32(hd)))
    pos = np.concatenate([np.arange(TP), np.tile(PAGES * PAGE + np.arange(TQ), NS)]).astype(np.float32)
    ang = (pos[None, :] * freqs.astype(np.float32)[:, None]).astype(np.float32)
    c[:, 320:320 + T] = np.tile(np.cos(ang), (P // hd, 1))
    c[:, 896:896 + T] = np.tile(np.sin(ang), (P // hd, 1))
    for g in range(2):
        for r in range(hd):
            c[g * DR + hd + r, 1472 + g * DR + r] = -1.0
            c[g * DR + r, 1472 + g * DR + hd + r] = 1.0
    return c


def kernel(**inputs):
    import concourse.bacc as _bacc
    from concourse.bass_utils import run_bass_kernel_spmd as _run

    nc = _bacc.Bacc("TRN2", target_bir_lowering=False, num_devices=1)
    arrays, io = {}, {}
    for name in _INS:
        a = np.ascontiguousarray(inputs[name])
        arrays[f"in_{name}"] = a
        io[name] = nc.dram_tensor(f"in_{name}", a.shape, mybir.dt.from_np(a.dtype), kind="ExternalInput").ap()
    arrays["in_consts"] = shape_constants()
    io["consts"] = nc.dram_tensor("in_consts", (P, 1600), F32, kind="ExternalInput").ap()
    for name, shape in _OUTS:
        io[name] = nc.dram_tensor(f"out_{name}", shape, F32, kind="ExternalOutput").ap()
    decoder_step(nc, io)
    r = _run(nc, [arrays], core_ids=[0])
    return tuple(r.results[0][f"out_{name}"] for name, _ in _OUTS)
```

```python
from contextlib import ExitStack

import numpy as np

import concourse.bass as bass
from concourse import mybir

F32 = mybir.dt.float32
F32R = mybir.dt.float32r
I32 = mybir.dt.int32
ACT = mybir.ActivationFunctionType
ALU = mybir.AluOpType
AX = mybir.AxisListType

P = 128
D = 1024
KT = D // P
TP, TS = 512, 64
T = TP + TS
H = T // 2
NS, TQ = 8, 8
CW = 31
CWV = 21
CWP = CW - CWV
FF = 4 * D
FC = 4
NCH = FF // P // FC
PLE = 256
NH, DN, DR, DV = 8, 128, 64, 128
CL, QL = 512, 768
PAGES, PAGE = 16, 128
EPS = 1e-6
SCALE = (DN + DR) ** -0.5
NEG = -1e30
RING, WRING = 4, 2
SLOT = 4 * (CL + DR)
WSLOT = 2048
VP = TP + CW - 1
VSQ = TQ + CW - 1
VW = VP + NS * VSQ


class Order:

    def __init__(self, keys):
        self.at = {k: n + 1 for n, k in enumerate(keys)}

    def __call__(self, *key):
        return self.at[key]


PHASES = [("pw1", 8, KT, 2, 2), ("pw2", 4, KT, 2, 1), ("mlp0", 4 * NCH, 0, 0, 1), ("ple0", 1, 2, 8, 1),
          ("gate0", 4, KT, 2, 1), ("dkv", 3, KT, 2, (1, 1, 2)), ("dq", 3, KT, 2, 1),
          ("uq", 6, QL // P, 2, (2, 2, 2, 2, 4, 4)), ("kvh", 4, CL // P, 0, 2), ("cache", 32, 0, 0, 8), ("uv", 2, CL // P, 0, 1), ("wo", 4, KT, 2, 1),
          ("mlp1", 4 * NCH, 0, 0, 1), ("ple1", 1, 2, 8, 1), ("gate1", 4, KT, 2, 1)]
RAW0, DENSE0, UNIT0, UNITS = {}, {}, {}, {}
PARTS, KIND = [], []
_d = _u = 0
for _n, _s, _k, _t, _parts in PHASES:
    RAW0[_n], DENSE0[_n], UNIT0[_n] = len(PARTS), _d, _u
    PARTS += list(_parts) if isinstance(_parts, tuple) else [_parts] * _s
    KIND += [(_n, _j) for _j in range(_s)]
    _d += 0 if _n == "cache" else _s
    UNITS[_n] = {"mlp0": 24 * NCH, "mlp1": 24 * NCH, "dkv": 10}.get(_n, 2 * _t * _s)
    _u += UNITS[_n]
LANDED = [16 * sum(PARTS[g % RING:g + 1:RING]) for g in range(len(PARTS))]

STATS = [("x0", KT), ("lm", KT), ("lv", KT), ("y0", KT), ("x1", KT), ("m0", KT), ("x2", KT), ("ck", CL // P),
         ("cq", QL // P), ("y1", KT), ("x3", KT), ("m1", KT)]
NT = dict(STATS)

PAIRS = [(h, 2 * j + t) for j in range(4) for h in range(2) for t in range(2)]


def tiles_of(s):
    if s in ("y0", "y1", "ck", "cq"):
        return PAIRS[:2 * NT[s]]
    if s in ("x1", "x3"):
        return [(h, m) for m in range(KT) for h in range(2)]
    if s in ("m0", "m1"):
        return [(h, 4 * g + m) for g in range(2) for h in range(2) for m in range(4)]
    return [(h, m) for h in range(2) for m in range(NT[s])]


SUMS = [("x0", 0), ("x0", 1), ("lm", 0), ("lm", 1), ("lv", 0), ("lv", 1), ("y0", 0), ("y0", 1), ("x1", 0), ("x1", 1),
        ("m0", 0), ("m0", 1), ("x2", 0), ("x2", 1), ("ck", 0), ("ck", 1), ("cq", 0), ("cq", 1),
        ("y1", 0), ("y1", 1), ("x3", 0), ("x3", 1), ("m1", 0), ("m1", 1)]
SQ = Order([(s, h, m) for s, _ in STATS if s != "lm" for h, m in tiles_of(s)])
ACC = SQ
DIRECT = ("lm", "lv")
SUM = Order([k for k in SUMS if k[0] not in DIRECT])
ROOT = Order([(s, h) for s, h in SUMS if s != "lm"])
SCALED_BY_INPUT = ("m0", "m1", "ck", "cq")
ROW = Order([(s, h) for s, h in SUMS if s in SCALED_BY_INPUT])
RSTD = Order(SUMS)
SPLITS = [("x0", KT), ("sw", KT), ("ff0", KT), ("g0", KT), ("kv", KT), ("mx", KT), ("cq", QL // P), ("o", NH),
          ("ff1", KT), ("g1", KT)]
A = Order([(v, h, m) for v, n in SPLITS for h in range(2) for m in range(n)])
XS = ["y0", "m0", "y1", "m1"]
XU = Order([(s, h, m) for s in XS for h in range(2) for m in range(KT)])
GATE_ORDER = [(h, 2 * s + t) for s in range(4) for h in range(2) for t in range(2)]
XG = Order([(g, h, m) for g in range(2) for h, m in GATE_ORDER])
SC = Order([(s, h, m) for s in ("sw", "y0", "m0", "ck", "cq", "y1", "m1")
            for h in range(2) for m in range(NT.get(s, KT))])

GAINS = [("mix_pre0", KT), ("mix_pre1", KT), ("mix_post0", KT), ("mix_post1", KT), ("ff_pre0", KT), ("ff_pre1", KT),
         ("ff_post0", KT), ("ff_post1", KT), ("dw_bias", KT), ("ln_g", KT), ("ln_b", KT), ("kv_in", KT),
         ("kv_norm", CL // P), ("q_norm", QL // P)]
GCOL, _c = {}, 0
for _n, _t in GAINS:
    GCOL[_n] = _c
    _c += _t
NG = _c


EVACUATED = {"y0": "pw2", "y1": "wo", "m0": "mlp0", "m1": "mlp1", "ck": "dkv", "cq": "dq"}
BANKS = 4
UP = 8
CHUNK = 24


def unit_of(st, h, m):
    u0 = UNIT0[EVACUATED[st]]
    if st in ("m0", "m1"):
        return u0 + CHUNK * (NCH - 1) + UP + 8 * (m // 4) + 4 * h + m % 4
    return u0 + 4 * (m // 2) + 2 * h + m % 2


def freed(u):
    return BANKS + u + 1


def decoder_step(nc, io):
    with ExitStack() as ctx:
        def sb(name, shape, dt=F32):
            return ctx.enter_context(nc.sbuf_tensor(name, shape, dt))

        def sem(name):
            return ctx.enter_context(nc.semaphore(name))

        bank = [ctx.enter_context(nc.psum_tensor(f"bank{i}", [P, 512], F32)) for i in range(8)]
        X = sb("X", [P, KT, T])
        AH, AL = sb("AH", [P, KT, T], F32R), sb("AL", [P, KT, T], F32R)
        BH, BL = sb("BH", [P, FC, T], F32R), sb("BL", [P, FC, T], F32R)
        Y = sb("Y", [P, KT, T])
        RAW = sb("RAW", [P, RING, SLOT])
        WH, WL = sb("WH", [P, WRING, WSLOT], F32R), sb("WL", [P, WRING, WSLOT], F32R)
        R1, R2 = sb("R1", [P, 2, H]), sb("R2", [P, 2, H])
        acc, sq = sb("acc", [P, 2, H]), sb("sq", [P, 2, H])
        scaled, prod = sb("scaled", [P, 2, H]), sb("prod", [P, 2, H])
        root = sb("root", [P, 2, H])
        ident, ones = sb("ident", [P, P]), sb("ones", [P, P])
        gains = sb("gains", [P, NG])
        taps = sb("taps", [P, KT, CW])
        eps = sb("eps", [P, 1])
        tiny = sb("tiny", [P, 8])
        S = sb("S", [P, 8064])

        V = S[:, 0:KT * VW].rearrange("p (m c) -> p m c", m=KT)
        v0 = KT * VW
        state_out = S[:, v0:v0 + 768].rearrange("p (b c) -> p b c", b=2)
        state_in = S[:, v0 + 768:v0 + 1248].rearrange("p (b c) -> p b c", b=2)
        x_stage = S[:, v0:v0 + D]
        taps_stage = RAW[:, 2, 0:D]
        state_stage = RAW[:, 3, 0:2 * D].rearrange("p (g n) -> p g n", g=2)
        yflat = Y[:, :, :].rearrange("p m t -> p (m t)")
        p_stage = S[:, 0:5 * PLE].rearrange("p (b c) -> p b c", b=5)
        E = S[:, 5 * PLE:5 * PLE + KT * T].rearrange("p (m t) -> p m t", m=KT)
        QR = S[:, 0:2304].rearrange("p (j t) -> p j t", j=4)
        KR = S[:, 2304:2880]
        QLAT = S[:, 2880:4928].rearrange("p (c q) -> p c q", c=4)
        CS = S[:, 4928:5184].rearrange("p (c t) -> p c t", c=4)
        QRS = S[:, 5184:5696]
        CK = S[:, 5696:8000].rearrange("p (c t) -> p c t", c=4)
        PT = S[:, 5696:7744].rearrange("p (k q) -> p k q", k=4)
        SPT = S[:, 5696:5952].rearrange("p (k q) -> p k q", k=4)
        OUT, OUTN = S[0:64, 5952:6464], S[0:64, 6464:6976]
        COS, SIN, ROT = S[:, 2880:3456], S[:, 3456:4032], S[:, 4032:4160]
        kv_stage = S[:, 4160:4736]
        kT = sq[:, :, :].rearrange("p a b -> p (a b)")[:, 0:TP]
        vn = root[:, :, :].rearrange("p a b -> p (a b)")[:, 0:TP]
        ukT = acc[:, :, :].rearrange("p a b -> p (a b)")[:, 0:TP]
        PB = [prod[:, :, :].rearrange("p a b -> p (a b)")[:, 0:TP],
              scaled[:, :, :].rearrange("p a b -> p (a b)")[:, 0:TP]]
        flat = {n: t[:, :, :].rearrange("p a b -> p (a b)") for n, t in
                (("R2", R2), ("prod", prod), ("scaled", scaled), ("sq", sq), ("root", root), ("acc", acc))}
        cmask = R2[:, :, :].rearrange("p a b -> p (a b)")[:, 0:P]
        nmask = R2[:, :, :].rearrange("p a b -> p (a b)")[0:64, P:P + TQ]

        landed = [sem(f"landed{i}") for i in range(RING)]
        hi_done, lo_done, pe_read_raw = sem("hi_done"), sem("lo_done"), sem("pe_read_raw")
        unit_done, bank_free = sem("unit_done"), sem("bank_free")
        consts, ones_set, vecs, x_in = sem("consts"), sem("ones_set"), sem("vecs"), sem("x_in")
        turned = sem("turned")
        sq_done, acc_done, sum_done, root_done, rstd_done = (sem("sq_done"), sem("acc_done"), sem("sum_done"),
                                                             sem("root_done"), sem("rstd_done"))
        row_step = sem("row_step")
        a_hi, a_lo, x_done, sc_done = sem("a_hi"), sem("a_lo"), sem("x_done"), sem("sc_done")
        acc_zero, x_first = sem("acc_zero"), sem("x_first")
        xg_done, y_out = sem("xg_done"), [sem("y_out0"), sem("y_out1")]

        SG = NS // 2 * (CW - 1)

        def half(t, m, h):
            return t[:, m, h * H:(h + 1) * H]

        def gathered(st, h):
            return (R2 if st in ("m0", "m1") else acc)[:, h, :]

        def gain(name, m):
            return gains[:, GCOL[name] + m:GCOL[name] + m + 1]

        conv_step, v_done, gate_sig = sem("conv_step"), sem("v_done"), sem("gate_sig")
        state_gathered, state_turned, state_copied = sem("state_gathered"), sem("state_turned"), sem("state_copied")
        stage_in, prod_done, z_step, tile_done, mean_done = (sem("stage_in"), sem("prod_done"), sem("z_step"),
                                                             sem("tile_done"), sem("mean_done"))
        state_out_sem = [sem("state_out0"), sem("state_out1")]
        unturned_v, unturned_a = sem("unturned_v"), sem("unturned_a")
        sw_sig, sw_lin, sw_val = sem("sw_sig"), sem("sw_lin"), sem("sw_val")
        ck_val, b_hi, b_lo = sem("ck_val"), sem("b_hi"), sem("b_lo")
        relu_done, u_hi, u_lo = sem("relu_done"), sem("u_hi"), sem("u_lo")
        y_zero, p_in, p_turned, p_hi, p_lo = sem("y_zero"), sem("p_in"), sem("p_turned"), sem("p_hi"), sem("p_lo")
        sig_done, gated = sem("sig_done"), sem("gated")
        rope_in, rot_done, rope_step = sem("rope_in"), sem("rot_done"), sem("rope_step")
        kv_turned, kv_staged, kv_out, cs_done = sem("kv_turned"), sem("kv_staged"), sem("kv_out"), sem("cs_done")
        centred = sem("centred")

        def unit_end(phase, h):
            last = {"pw1": 2, "pw2": 2, "dkv": 1, "dq": 2, "uq": 2, "wo": 2, "gate0": 2, "gate1": 2,
                    "ple0": 8, "ple1": 8}[phase]
            return UNIT0[phase] + UNITS[phase] - (last if h == 0 else 0)

        def up_n(h, m):
            return 4 * (m // 2) + 2 * h + m % 2

        read_before = {"sw": "pw1", "ff0": "pw2", "kv": "gate0", "mx": "dkv", "cq": "dq", "ff1": "wo"}
        gain_of = {"x0": "mix_pre0", "ff0": "ff_pre0", "g0": None, "kv": "kv_in", "mx": "mix_pre1",
                   "cq": "q_norm", "ff1": "ff_pre1", "g1": None, "sw": None}
        tokens = [(b * P, P) for b in range(4)] + [(TP, TS)]
        SLABS = {n: s for n, s, *_ in PHASES}
        KR_STEP = 7
        NORM_OF = {"sw": "lv"}
        SM = Order([("mask",), ("new_top",)] + [(w, j) for j in range(4) for w in ("top", "bias", "sum")])
        NSM = len(SM.at)
        OUTS = 6

        def scaled_read(key):
            st, h, m = key
            if st in ("y0", "m0", "y1", "m1"):
                return x_done, XU(*key)
            if st == "sw":
                return sw_val, KT * h + m + 1
            return (ck_val, 4 * h + m + 1) if st == "ck" else (a_lo, A(*key))

        kvt_done, kvt_used = sem("kvt_done"), sem("kvt_used")
        v_mm, v_used, uk_mm, uk_used, ql_mm, ql_used = (sem("v_mm"), sem("v_used"), sem("uk_mm"), sem("uk_used"),
                                                        sem("ql_mm"), sem("ql_used"))
        s_mm, s_masked, s_max, s_exp, s_rec, p_ready = (sem("s_mm"), sem("s_masked"), sem("s_max"), sem("s_exp"),
                                                        sem("s_rec"), sem("p_ready"))
        pt_mm, pt_used, pv_mm = sem("pt_mm"), sem("pt_used"), sem("pv_mm")
        table_in, page_mm, key_hi, key_lo, score_mm, new_in, q_hi, q_lo = (
            sem("table_in"), sem("page_mm"), sem("key_hi"), sem("key_lo"), sem("score_mm"), sem("new_in"), sem("q_hi"),
            sem("q_lo"))
        new_mm, new_nat, new_nat_c, sm_step, exp_done, spt_mm, spt_c, out_mm, lat_out = (
            sem("new_mm"), sem("new_nat"), sem("new_nat_c"), sem("sm_step"), sem("exp_done"), sem("spt_mm"),
            sem("spt_c"), sem("out_mm"), sem("lat_out"))
        out_done = sem("out_done")
        dve_step, dup_set, seen, qsr_zero = sem("dve_step"), sem("dup_set"), sem("seen"), sem("qsr_zero")
        qrs_mm, qrs_c, uv_mm, y_turned, y_copied_v, y_copied_a = (sem("qrs_mm"), sem("qrs_c"), sem("uv_mm"),
                                                                  sem("y_turned"), sem("y_copied_v"), sem("y_copied_a"))
        table = sb("table", [1, PAGES], I32)

        block = ctx.enter_context(nc.Block())

        def cache_loads(sp):
            g0 = RAW0["cache"]
            with sp.Fori(0, NS) as i:
                sp.dma_start(table[:], io["page_table"][bass.ds(i, 1), :]).then_inc(table_in, 16)
                sp.wait_ge(table_in, 16)
                sp.sem_clear(table_in)
                for j in range(RING):
                    pages = [sp.value_load(table[0:1, 4 * j + q:4 * j + q + 1], min_val=0,
                                           max_val=io["cache_kv_latent"].shape[0] - 1) for q in range(4)]
                    sp.wait_ge(pe_read_raw, 1 + j + RING * i)
                    sp.wait_ge(ones_set, 1)
                    if j == 0:
                        sp.wait_ge(lo_done, DENSE0["kvh"] + 4)
                    for q in range(4):
                        dst = RAW[:, (g0 + j) % RING].rearrange("p (a c) -> p a c", a=1)
                        sp.dma_start(dst[:, :, q * CL:(q + 1) * CL],
                                     io["cache_kv_latent"].rearrange("n p c -> p n c")[:, bass.ds(pages[q], 1)])\
                            .then_inc(landed[(g0 + j) % RING], 16)
                        r = 4 * CL + DR * (q // 2 + 2 * (q % 2))
                        sp.dma_start(dst[:, :, r:r + DR],
                                     io["cache_k_rope"].rearrange("n p c -> p n c")[:, bass.ds(pages[q], 1)])\
                            .then_inc(landed[(g0 + j) % RING], 16)

        @block.sync
        def _(sp):
            def slot(g, a, b):
                return RAW[:, g % RING, a:b]

            def free(g, i=0):
                kind, j = KIND[g - RING]
                if kind == "cache":
                    sp.wait_ge(pe_read_raw, 4 + j + 1)
                    return
                if kind == "kvh":
                    sp.wait_ge(pe_read_raw, j + 1)
                sp.wait_ge(lo_done, DENSE0[kind] + j + 1)

            def dense(phase, w, kt, n):
                for j in range(SLABS[phase]):
                    g = RAW0[phase] + j
                    free(g)
                    sp.dma_start(slot(g, 0, kt * n).rearrange("p (k n) -> p k n", k=kt),
                                 w.rearrange("(k p) n -> p k n", p=P)[:, :, j * n:(j + 1) * n])\
                        .then_inc(landed[g % RING], 16)

            def mlp(layer, phase):
                up = io["w_up"][layer].rearrange("(k p) (c n) -> p c k n", p=P, n=256)
                down = io["w_down"][layer].rearrange("(c k p) n -> p c k n", p=P, k=FC)
                g0, d0 = RAW0[phase], DENSE0[phase]
                with sp.Fori(0, NCH) as i:
                    for j in range(RING):
                        g = g0 + j
                        dst = slot(g, 0, WSLOT)
                        sp.wait_ge(lo_done, d0 + j - RING + 1 + RING * i)
                        sp.wait_ge(ones_set, 1)
                        if j < 2:
                            sp.dma_start(dst.rearrange("p (c k n) -> p c k n", c=1, k=KT),
                                         up[:, bass.ds(2 * i + j, 1)]).then_inc(landed[g % RING], 16)
                        else:
                            n = (j - 2) * 512
                            sp.dma_start(dst.rearrange("p (c k n) -> p c k n", c=1, k=FC),
                                         down[:, bass.ds(i, 1), :, n:n + 512]).then_inc(landed[g % RING], 16)

            def ple(layer, phase):
                g = RAW0[phase]
                free(g)
                sp.dma_start(slot(g, 0, 2 * D).rearrange("p (k n) -> p k n", k=2),
                             io["ple_proj"][layer].rearrange("(k p) n -> p k n", p=P)).then_inc(landed[g % RING], 16)

            def load_p(layer):
                for b, (t0, n) in enumerate(tokens):
                    src = io["p_prompt"][layer, 0, t0:t0 + n] if b < 4 else \
                        io["p_sample"][layer].rearrange("s t c -> (s t) c")
                    sp.dma_start(p_stage[0:n, b, :], src).then_inc(p_in, 16)

            for q in range(2):
                for b in range(4):
                    c = q * D // 2
                    sp.dma_start(yflat[:, b * D + c:b * D + c + D // 2],
                                 io["x_prompt"][0, b * P:(b + 1) * P, c:c + D // 2]).then_inc(x_in if q else x_first, 16)
                if q == 0:
                    sp.dma_start(x_stage[0:TS], io["x_sample"].rearrange("s t c -> (s t) c")).then_inc(x_first, 16)
            pw1 = io["conv_pw1"][0].rearrange("(k p) (a m n) -> p m a k n", p=P, a=2, n=P)

            def pw1_slab(g, m):
                for a in range(2):
                    sp.dma_start(slot(g, 0, WSLOT).rearrange("p (m k a n) -> p m k a n", m=1, k=KT, a=2)[:, :, :, a],
                                 pw1[:, m, a]).then_inc(landed[g % RING], 16)

            for j in range(2):
                pw1_slab(j, slice(j, j + 1))
            sp.wait_ge(turned, 26)
            for j in range(2, 4):
                pw1_slab(j, slice(j, j + 1))
            for j in range(4, 8):
                free(j)
                pw1_slab(j, slice(j, j + 1))
            dense("pw2", io["conv_pw2"][0], KT, 256)
            for q in state_out_sem:
                sp.wait_ge(q, 16 * KT)
            sp.wait_ge(tile_done, KT)
            load_p(0)
            mlp(0, "mlp0")
            ple(0, "ple0")
            dense("gate0", io["ple_gate"][0], KT, 256)
            for j in range(3):
                g = RAW0["dkv"] + j
                free(g)
                wk = io["w_dkv"].rearrange("(k p) n -> p k n", p=P)
                if j < 2:
                    sp.dma_start(slot(g, 0, WSLOT).rearrange("p (k n) -> p k n", k=KT),
                                 wk[:, :, 256 * j:256 * j + 256]).then_inc(landed[g % RING], 16)
                else:
                    for c in range(2):
                        sp.dma_start(slot(g, 0, KT * P).rearrange("p (k n) -> p k n", k=KT)[:, :, 64 * c:64 * c + 64],
                                     wk[:, :, CL:CL + DR]).then_inc(landed[g % RING], 16)
            sp.wait_ge(xg_done, 2 * KT)
            sp.dma_start(S[:, 2880:4160], io["consts"][:, 320:1600]).then_inc(rope_in, 16)
            dense("dq", io["w_dq"][0], KT, 256)
            uq = io["w_uq"][0].rearrange("(k p) (h e) -> p k h e", p=P, h=NH)
            for j in range(6):
                g = RAW0["uq"] + j
                free(g)
                dst = slot(g, 0, 6 * 256).rearrange("p (k n) -> p k n", k=6)
                heads, e0, e1 = ((2 * j, 2 * j + 1), 0, DN) if j < 4 else (range(4 * (j - 4), 4 * (j - 4) + 4), DN, DN + DR)
                for n, h in enumerate(heads):
                    sp.dma_start(dst[:, :, n * (e1 - e0):(n + 1) * (e1 - e0)], uq[:, :, h, e0:e1])\
                        .then_inc(landed[g % RING], 16)
            for j in range(4):
                g = RAW0["kvh"] + j
                free(g)
                for n, w in enumerate((io["w_uk"], io["w_uv"])):
                    sp.dma_start(slot(g, 1024 * n, 1024 * n + 1024).rearrange("p (k n) -> p k n", k=4),
                                 w.rearrange("(k p) h n -> p k (h n)", p=P)[:, :, 256 * j:256 * j + 256])\
                        .then_inc(landed[g % RING], 16)
            sp.wait_ge(sc_done, SC("cq", 1, 5))
            sp.dma_start(cmask, io["consts"][:, 128:256]).then_inc(consts, 16)
            sp.dma_start(nmask, io["consts"][0:64, 256:264]).then_inc(consts, 16)
            cache_loads(sp)
            for j in range(2):
                g = RAW0["uv"] + j
                free(g)
                sp.dma_start(slot(g, 0, WSLOT).rearrange("p (k n) -> p k n", k=4),
                             io["w_uv"].rearrange("(k p) h n -> p k (h n)", p=P)[:, :, 512 * j:512 * j + 512])\
                    .then_inc(landed[g % RING], 16)
            dense("wo", io["w_o"][0], KT, 256)
            sp.wait_ge(a_lo, A("o", 1, NH - 1))
            load_p(1)
            mlp(1, "mlp1")
            ple(1, "ple1")
            dense("gate1", io["ple_gate"][1], KT, 256)

        STAGES, GATHER = ("sq", "acc"), ("R2", "root")
        scratch = flat["acc"]
        NK, NKR = scratch[:, 0:32].rearrange("p (c t) -> p c t", c=4), scratch[0:DR, 32:40]
        SN, PN = scratch[0:64, 64:72], scratch[0:64, 72:80]
        TOP, NM, ALPHA, PSUMS, SUMQ = (scratch[0:64, 80 + 8 * k:88 + 8 * k] for k in range(5))
        QS = flat["prod"][:, 0:256].rearrange("p (c q) -> p c q", c=4)
        QSR = flat["prod"][:, 256:384].rearrange("p (r q) -> p r q", r=2)
        NEWC, NPT = flat["sq"][0:TQ, 0:CL], flat["root"][0:TQ, 0:64]
        SP = flat["scaled"][0:64, 0:512]
        rope_bank = bank[3][:, 0:256].rearrange("p (a b) -> p a b", a=4)
        DUP = flat["root"][:, 0:256].rearrange("p (e c) -> p e c", e=2)

        def col(t, j):
            return t[:, j:j + 1]

        dense_slabs = [(g, k, j) for g, (k, j) in enumerate(KIND) if k != "cache"]
        floats = {"ple0": 2048, "ple1": 2048, "uq": 1536}

        def slab_size(d):
            g, k, j = dense_slabs[d]
            return 1024 if (k, j) == ("dkv", 2) else floats.get(k, 2048)

        def landed_at(d):
            g = dense_slabs[d][0]
            return landed[g % RING], LANDED[g]

        def raw_of(d):
            return RAW[:, dense_slabs[d][0] % RING, 0:slab_size(d)]


        def prev(order, key, back):
            n = order.at[key] - back
            return next((k for k, v in order.at.items() if v == n), None)

        def used_at(d):
            _, kind, j = dense_slabs[d]
            if kind == "kvh":
                return kvt_done, 2 * j + 2
            if kind == "uv":
                return uv_mm, 4 * j + 4
            if kind in ("mlp0", "mlp1"):
                return unit_done, UNIT0[kind] + CHUNK * (j // 4) + (4, 8, 16, 24)[j % 4]
            if kind == "dkv":
                return unit_done, UNIT0[kind] + (4, 8, 10)[j]
            return unit_done, UNIT0[kind] + UNITS[kind] // SLABS[kind] * (j + 1)

        @block.scalar
        def _(act):
            def hi(d, i=None, per=16):
                s, v = landed_at(d)
                act.wait_ge(s, v if i is None else v + per * i)
                if d >= WRING:
                    s, v = used_at(d - WRING)
                    act.wait_ge(s, v if i is None else v + (16 if KIND[dense_slabs[d][0]][0] == "pw1" or d == 8
                                                            else CHUNK) * i)
                elif i is not None:
                    act.wait_ge(bank_free, BANKS + 16 * i)
                nc.scalar.activation(WH[:, d % WRING, 0:slab_size(d)], raw_of(d), ACT.Copy).then_inc(hi_done, 1)

            def square(st, h, m, src):
                before = prev(SQ, (st, h, m), 2)
                if before:
                    act.wait_ge(acc_done, ACC(*before))
                nc.scalar.activation(sq[:, SQ(st, h, m) % 2, :], src, ACT.Square).then_inc(sq_done, 1)

            def root_of(st, h):
                if st in SCALED_BY_INPUT:
                    act.wait_ge(row_step, ROW(st, h))
                    src = root[:, h, :]
                else:
                    if st in DIRECT:
                        act.wait_ge(acc_done, ACC(st, h, NT[st] - 1))
                    else:
                        act.wait_ge(sum_done, SUM(st, h))
                    src = bank[4 + h][:, 0:H]
                before = [k for k in ROOT.at if k[1] == h and ROOT(*k) < ROOT(st, h)]
                if before:
                    act.wait_ge(rstd_done, RSTD(*before[-1]))
                nc.scalar.activation(root[:, h, :], src, ACT.Sqrt, bias=eps[:, 0:1], scale=1.0 / (P * NT[st]))\
                    .then_inc(root_done, 1)

            def split(v, h, m, src):
                if v in read_before:
                    act.wait_ge(unit_done, unit_end(read_before[v], h))
                if v in ("g0", "g1"):
                    act.wait_ge(unit_done, UNIT0["mlp" + v[1]] + CHUNK * NCH)
                g = gain_of[v]
                if g:
                    nc.scalar.activation(half(AH, m, h), src, ACT.Copy, scale=gain(g, m)).then_inc(a_hi, 1)
                else:
                    nc.scalar.activation(half(AH, m, h), src, ACT.Copy).then_inc(a_hi, 1)

            act.dma_start(ident[:], io["consts"][:, 0:P]).then_inc(consts, 16)
            row = 0
            vec = {"mix_pre0": io["norm_mix_pre"][0], "mix_pre1": io["norm_mix_pre"][1],
                   "mix_post0": io["norm_mix_post"][0], "mix_post1": io["norm_mix_post"][1],
                   "ff_pre0": io["norm_ff_pre"][0], "ff_pre1": io["norm_ff_pre"][1],
                   "ff_post0": io["norm_ff_post"][0], "ff_post1": io["norm_ff_post"][1],
                   "dw_bias": io["conv_dw_bias"][0], "ln_g": io["conv_ln_g"][0], "ln_b": io["conv_ln_b"][0],
                   "kv_in": io["kv_in_norm"], "kv_norm": io["kv_norm"], "q_norm": io["q_norm"][0]}
            for name, n in GAINS:
                act.dma_start(flat["prod"][row:row + n, 0:P], vec[name].rearrange("(r c) -> r c", c=P)).then_inc(vecs, 16)
                row += n
            act.dma_start(taps_stage[0:CW], io["conv_dw"][0]).then_inc(stage_in, 16)
            for g in range(2):
                act.dma_start(state_stage[0:SG, g, :],
                              io["state_conv"][0, 4 * g:4 * g + 4].rearrange("s j c -> (s j) c")).then_inc(stage_in, 16)

            def turned_input(e):
                act.wait_ge(turned, e + 1)
                src = bank[4 + e % 4]
                if e < 17:
                    nc.scalar.activation(X[:, e // 2, TP:T], src[:, 0:TS], ACT.Copy).then_inc(unturned_a, 1)
                elif e == 17:
                    nc.scalar.activation(taps[:, :, :], src[:, 0:KT * CW].rearrange("p (m c) -> p m c", m=KT),
                                         ACT.Copy).then_inc(unturned_a, 1)
                else:
                    nc.scalar.activation(V[:, e - 18, VP:VW].rearrange("p (s c) -> p s c", s=NS)[:, :, 0:CW - 1],
                                         src[:, 0:2 * SG].rearrange("p (s c) -> p s c", s=NS),
                                         ACT.Copy).then_inc(unturned_a, 1)

            act.wait_ge(ones_set, 3)
            for e in range(1, 17, 2):
                turned_input(e)
            hi(0)
            act.wait_ge(unturned_v, 9)
            for m in range(KT):
                split("x0", 0, m, half(X, m, 0))
            for m in range(KT):
                square("x0", 0, m, half(X, m, 0))
            act.wait_ge(unturned_a, 8)
            for m in range(KT):
                split("x0", 1, m, half(X, m, 1))
            root_of("x0", 0)
            for m in range(KT):
                square("x0", 1, m, half(X, m, 1))
            hi(1)
            root_of("x0", 1)
            for e in range(17, 26, 2):
                turned_input(e)

            def gates(m):
                for h in range(2):
                    act.wait_ge(bank_free, freed(4 * m + 2 * h + 1))
                    nc.scalar.activation(prod[:, h, :], prod[:, h, :], ACT.Sigmoid).then_inc(gate_sig, 1)

            def products(m):
                act.wait_ge(v_done, 3 * m + 6)
                for n in range(CWP):
                    c, k = CWV + n, (CWP - 1) * m + n - 1
                    dst = flat[STAGES[k % 2]] if n else flat[GATHER[m % 2]]
                    if n == 0:
                        act.wait_ge(tile_done, m - 1) if m >= 2 else act.wait_ge(rstd_done, 2)
                    elif k >= 2:
                        act.wait_ge(z_step, k - 1)
                    w = taps[:, m, c:c + 1]
                    nc.scalar.activation(dst[:, 0:TP], V[:, m, c:c + TP], ACT.Copy, scale=w).then_inc(prod_done, 1)
                    nc.scalar.activation(dst[:, TP:T].rearrange("p (s t) -> p s t", s=NS),
                                         V[:, m, VP:VW].rearrange("p (s c) -> p s c", s=NS)[:, :, c:c + TQ], ACT.Copy,
                                         scale=w).then_inc(prod_done, 1)

            def gather_state(m):
                if m >= 2:
                    act.wait_ge(state_turned, m - 1)
                nc.scalar.activation(state_in[:, m % 2, :].rearrange("p (s j) -> p s j", s=NS),
                                     V[:, m, VP:VW].rearrange("p (s c) -> p s c", s=NS)[:, :, TQ:VSQ], ACT.Copy)\
                    .then_inc(state_gathered, 1)

            def give_state(m):
                act.wait_ge(state_turned, m + 1)
                if m >= 2:
                    act.wait_ge(state_out_sem[m % 2], 32 * (m // 2))
                nc.scalar.activation(state_out[0:SG, m % 2, 0:2 * P], bank[6 + m % 2][0:SG, 0:2 * P], ACT.Copy)\
                    .then_inc(state_copied, 1)
                nc.scalar.activation(state_out[0:CW - 1, m % 2, 2 * P:3 * P], bank[6 + m % 2][0:CW - 1, 2 * P:3 * P],
                                     ACT.Copy).then_inc(state_copied, 1)
                act.wait_ge(state_copied, 2 * m + 2)
                act.dma_start(io["new_conv_sample"][0, :, :, m * P:(m + 1) * P].rearrange("(g s) j c -> (s j) g c", g=2),
                              state_out[0:SG, m % 2, 0:2 * P].rearrange("p (g c) -> p g c", g=2))\
                    .then_inc(state_out_sem[m % 2], 16)
                act.dma_start(io["new_conv_prompt"][0, 0, :, m * P:(m + 1) * P],
                              state_out[0:CW - 1, m % 2, 2 * P:3 * P]).then_inc(state_out_sem[m % 2], 16)

            act.wait_ge(unturned_v, 13)
            act.wait_ge(unturned_a, 13)
            gates(0)
            hi(2)
            for m in range(KT):
                if m < KT - 1:
                    hi(m + 3)
                    gates(m + 1)
                products(m)
                if m >= KT - 2:
                    for q in range(4 * (m - KT + 2), 4 * (m - KT + 2) + 4):
                        gather_state(q)
                        if q:
                            give_state(q - 1)
            give_state(KT - 1)

            for h in range(2):
                for m in range(KT):
                    act.wait_ge(centred, KT * h + m + 1)
                    square("lv", h, m, half(Y, m, h))
            for h in range(2):
                root_of("lv", h)
            for n in range(2 * KT + 1):
                if n < 2 * KT:
                    h, m = divmod(n, KT)
                    act.wait_ge(sc_done, SC("sw", h, m))
                    if n >= 2:
                        act.wait_ge(a_lo, A("x0", 1, KT - 1) + n - 1)
                    nc.scalar.activation(prod[:, n % 2, :], scaled[:, SC("sw", h, m) % 2, :], ACT.Sigmoid,
                                         bias=gain("ln_b", m), scale=gain("ln_g", m)).then_inc(sw_sig, 1)
                if n:
                    h, m = divmod(n - 1, KT)
                    act.wait_ge(sw_val, n)
                    split("sw", h, m, prod[:, (n - 1) % 2, :])

            def hi_steps(phase):
                for j in range(SLABS[phase]):
                    hi(DENSE0[phase] + j + 1)

            def after_mixer(phase, st, v, done=0):
                for j in range(5):
                    if done <= j < 4:
                        hi(DENSE0[phase] + j + 1)
                    if j:
                        for h, m in PAIRS[4 * j - 4:4 * j]:
                            act.wait_ge(bank_free, freed(unit_of(st, h, m)))
                            square(st, h, m, half(Y, m, h))
                for h in range(2):
                    root_of(st, h)
                for h in range(2):
                    for m in range(KT):
                        act.wait_ge(x_done, XU(st, h, m))
                        split(v, h, m, half(X, m, h))

            def mlp(layer):
                phase, v = f"mlp{layer}", f"g{layer}"
                d0, u0, stx = DENSE0[phase], UNIT0[phase], f"x{2 * layer + 1}"
                b0 = UP * NCH * layer
                with act.Fori(0, NCH) as i:
                    for j in range(4):
                        hi(d0 + j + 1, i)
                        if j == 3:
                            for h in range(2):
                                act.wait_ge(acc_done, SQ(stx, h, 0) - 2 + 2 * i)
                                act.wait_ge(ones_set, 3)
                                nc.scalar.activation(sq[:, SQ(stx, h, 0) % 2, :],
                                                     X[:, bass.ds(i, 1), h * H:(h + 1) * H]
                                                     .rearrange("p a t -> p (a t)"), ACT.Square).then_inc(sq_done, 1)
                        if j >= 2:
                            continue
                        for k in range(5):
                            n = 4 * j + k
                            if k < 4:
                                act.wait_ge(unit_done, u0 + n + 1 + CHUNK * i)
                                nc.scalar.activation(scaled[:, n % 2, :], bank[(u0 + n) % BANKS][:, 0:H], ACT.Relu)\
                                    .then_inc(relu_done, 1)
                            if k:
                                n, q = n - 1, k - 1
                                act.wait_ge(bank_free, freed(u0 + n) + CHUNK * i)
                                nc.scalar.activation(half(BH, 2 * j + q % 2, q // 2), prod[:, n % 2, :], ACT.Copy)\
                                    .then_inc(u_hi, 1)
                st = f"m{layer}"

                def squares(a, b):
                    for h, m in tiles_of(st)[a:b]:
                        act.wait_ge(bank_free, freed(unit_of(st, h, m)))
                        square(st, h, m, half(Y, m, h))
                squares(0, 12)
                for e in range(4):
                    if e == 2:
                        squares(12, 16)
                    kt, part = e // 2, e % 2
                    a, b = (0, TP) if part == 0 else (TP, T)
                    act.wait_ge(p_turned, 4 * layer + e + 1)
                    nc.scalar.activation(BH[:, kt, a:b], bank[6 + part][:, 0:b - a], ACT.Copy).then_inc(p_hi, 1)
                for h in range(2):
                    root_of(f"x{2 * layer + 1}", h)
                hi(DENSE0[f"ple{layer}"] + 1)
                for h in range(2):
                    root_of(st, h)
                for h in range(2):
                    for m in range(KT):
                        act.wait_ge(x_done, XU(st, h, m))
                        split(v, h, m, half(X, m, h))

                d0, u0 = DENSE0[f"gate{layer}"], UNIT0[f"gate{layer}"]
                for j in range(4):
                    if d0 + j + 1 < len(dense_slabs):
                        hi(d0 + j + 1)
                    for k in range(4):
                        n = 4 * j + k
                        act.wait_ge(unit_done, u0 + n + 1)
                        if n >= 2:
                            act.wait_ge(bank_free, freed(u0 + n - 2))
                        nc.scalar.activation(prod[:, n % 2, :], bank[(u0 + n) % BANKS][:, 0:H], ACT.Sigmoid)\
                            .then_inc(sig_done, 1)

            after_mixer("pw2", "y0", "ff0", 1)
            mlp(0)

            for h in range(2):
                for m in range(KT):
                    act.wait_ge(xg_done, XG(0, h, m))
                    split("kv", h, m, half(X, m, h))
                    square("x2", h, m, half(X, m, h))
            hi_steps("dkv")
            for h in range(2):
                root_of("x2", h)
            for h in range(2):
                for m in range(KT):
                    split("mx", h, m, half(X, m, h))
            hi(DENSE0["dq"] + 1)
            for h, m in tiles_of("ck"):
                act.wait_ge(bank_free, freed(unit_of("ck", h, m)))
                square("ck", h, m, half(CK, m, h))
            hi(DENSE0["dq"] + 2)
            for h in range(2):
                root_of("ck", h)
            for h in range(2):
                for m in range(4):
                    act.wait_ge(ck_val, 4 * h + m + 1)
                    nc.scalar.activation(half(BH, m, h), half(CK, m, h), ACT.Copy).then_inc(b_hi, 1)
            for n, (h, m) in enumerate(tiles_of("cq")):
                if n == 4:
                    hi(DENSE0["dq"] + 3)
                act.wait_ge(bank_free, freed(unit_of("cq", h, m)))
                square("cq", h, m, half(Y, m, h))
            for h in range(2):
                root_of("cq", h)
            for h in range(2):
                for m in range(6):
                    act.wait_ge(sc_done, SC("cq", h, m))
                    split("cq", h, m, scaled[:, SC("cq", h, m) % 2, :])
            for j in range(6):
                hi(DENSE0["uq"] + j + 1)
                if j == 5:
                    break
                t0, n = tokens[j]
                act.wait_ge(kv_turned, j + 1)
                if j:
                    act.wait_ge(kv_out, 32 * j)
                nc.scalar.activation(kv_stage[0:n, 0:CL], bank[4][0:n, 0:CL], ACT.Copy).then_inc(kv_staged, 1)
                nc.scalar.activation(kv_stage[0:n, CL:CL + DR], bank[5][0:n, 0:DR], ACT.Copy).then_inc(kv_staged, 1)
                act.wait_ge(kv_staged, 2 * j + 2)
                for a, b, prompt, sample in ((0, CL, "new_kv_prompt", "new_kv_sample"),
                                             (CL, CL + DR, "new_kr_prompt", "new_kr_sample")):
                    dst = io[prompt][0, t0:t0 + n] if j < 4 else io[sample].rearrange("s t c -> (s t) c")
                    act.dma_start(dst, kv_stage[0:n, a:b]).then_inc(kv_out, 16)

            def head_keys(hd):
                act.wait_ge(kvt_done, hd + 1)
                if hd:
                    act.wait_ge(s_mm, 4 * hd)
                nc.scalar.activation(kT, bank[0][:, 0:TP], ACT.Copy).then_inc(kvt_used, 1)

            def exp(hd, qb):
                n, w = 4 * hd + qb, (qb + 1) * P
                act.wait_ge(s_max, 2 * n + 2)
                if n >= 2:
                    act.wait_ge(pt_mm, n - 1)
                c = 4 * (n % 2)
                nc.scalar.activation(PB[n % 2][:, 0:w], bank[4 + n % 2][:, 0:w], ACT.Exp, scale=SCALE,
                                     bias=tiny[:, c + 1:c + 2], accum_out=tiny[:, c + 2:c + 3]).then_inc(s_exp, 1)

            def pt(hd, qb):
                n = 4 * hd + qb
                act.wait_ge(pt_mm, n + 1)
                if qb == 0 and hd:
                    act.wait_ge(pv_mm, hd)
                if n == 0:
                    act.wait_ge(kv_turned, 5)
                    act.wait_ge(cs_done, 1)
                nc.scalar.activation(PT[:, 0:qb + 1, qb * P:(qb + 1) * P],
                                     bank[6][:, 0:(qb + 1) * P].rearrange("p (k q) -> p k q", q=P), ACT.Copy)\
                    .then_inc(pt_used, 1)

            def head_out(hd):
                act.wait_ge(pv_mm, hd + 1)
                if hd == 0:
                    act.wait_ge(unit_done, unit_end("uq", 1))
                nc.scalar.activation(AH[:, hd, 0:TP], bank[7][:, 0:TP], ACT.Copy).then_inc(a_hi, 1)

            head_keys(0)
            for hd in range(NH):
                exp(hd, 0)
                if hd:
                    pt(hd - 1, 3)
                    head_out(hd - 1)
                exp(hd, 1)
                pt(hd, 0)
                exp(hd, 2)
                pt(hd, 1)
                if hd % 2 == 0 and hd < NH - 2:
                    hi(DENSE0["kvh"] + hd // 2 + 1)
                if hd < NH - 1:
                    head_keys(hd + 1)
                exp(hd, 3)
                pt(hd, 2)
            pt(NH - 1, 3)
            head_out(NH - 1)

            def key(c, n):
                act.wait_ge(page_mm, c + 1 + 5 * n)
                if c == 0:
                    act.wait_ge(score_mm, n + 1)
                dst, src = (BH[:, c, 0:TP], bank[4 + c][:, 0:TP]) if c < 4 else (BH[:, :, TP:T], rope_bank)
                nc.scalar.activation(dst, src, ACT.Copy).then_inc(key_hi, 1)

            def queries(i):
                act.wait_ge(new_in, 5 + 5 * i)
                act.wait_ge(score_mm, 1 + 4 * i)
                nc.scalar.activation(AH[:, 0:4, TP:T], QS, ACT.Copy).then_inc(q_hi, 1)
                nc.scalar.activation(AH[:, 4:6, TP:T], QSR, ACT.Copy).then_inc(q_hi, 1)

            def new_values(i):
                act.wait_ge(new_nat, 2 + i)
                nc.scalar.activation(NEWC, bank[4][0:TQ, 0:CL], ACT.Copy).then_inc(new_nat_c, 1)

            def slab(j, i, last):
                act.wait_ge(sm_step, SM("bias", j) + NSM * i)
                nc.scalar.activation(SP, bank[0][0:64, :], ACT.Exp, scale=SCALE, bias=col(NM, j), accum_out=col(PSUMS, j))\
                    .then_inc(exp_done, 1)
                if j == 0:
                    nc.scalar.activation(PN, SN, ACT.Exp, scale=SCALE, bias=col(NM, 0), accum_out=col(PSUMS, 4))\
                        .then_inc(exp_done, 1)
                else:
                    nc.scalar.activation(col(ALPHA, j), col(NM, j - 1), ACT.Exp, scale=-1.0, bias=col(NM, j))\
                        .then_inc(exp_done, 1)
                if not last:
                    for c in range(5):
                        key(c, j + 1 + 4 * i)
                act.wait_ge(spt_mm, j + 1 + 4 * i)
                act.wait_ge(pe_read_raw, 4 + j + 4 * i)
                nc.scalar.activation(SPT, bank[1][:, 0:256].rearrange("p (k q) -> p k q", k=4), ACT.Copy)\
                    .then_inc(spt_c, 1)
                if j == 0:
                    nc.scalar.activation(NPT, bank[1][0:TQ, 256:320], ACT.Copy).then_inc(spt_c, 1)

            def sequence(i, last):
                for j in range(4):
                    slab(j, i, last and j == 3)
                if not last:
                    queries(i + 1)
                    new_values(i + 1)

            queries(0)
            for c in range(5):
                key(c, 0)
            new_values(0)
            with act.Fori(0, NS - 1) as i:
                sequence(i, False)
            sequence(NS - 1, True)
            act.wait_ge(lat_out, 1 + NS)
            hi(DENSE0["uv"])
            nc.scalar.activation(BH[:, :, 0:TP], QLAT[:, :, :], ACT.Copy).then_inc(b_hi, 1)
            for hd in range(NH):
                if hd % 4 == 0:
                    hi(DENSE0["uv"] + hd // 4 + 1)
                act.wait_ge(uv_mm, hd + 1)
                nc.scalar.activation(AH[:, hd, TP:T], bank[hd % 4][:, 0:TS], ACT.Copy).then_inc(a_hi, 1)
            after_mixer("wo", "y1", "ff1")
            mlp(1)

            for b, (t0, n) in enumerate(tokens):
                act.wait_ge(y_turned, 2 * b + 1)
                if b >= 2:
                    act.wait_ge(y_out[b % 2], 16 * (b // 2))
                nc.scalar.activation(yflat[0:n, (b % 2) * D:(b % 2) * D + 512], bank[4 + 2 * (b % 2)][0:n, 0:512],
                                     ACT.Copy).then_inc(y_copied_a, 1)
                act.wait_ge(y_copied_a, b + 1)
                act.wait_ge(y_copied_v, b + 1)
                dst = io["y_prompt"][0, t0:t0 + n] if b < 4 else io["y_sample"].rearrange("s t c -> (s t) c")
                act.dma_start(dst, yflat[0:n, (b % 2) * D:(b % 2) * D + D]).then_inc(y_out[b % 2], 16)
            act.wait_ge(y_out[0], 16 * 3)
            act.wait_ge(y_out[1], 16 * 2)
            act.wait_ge(kv_out, 32 * 5)
            for q in state_out_sem:
                act.wait_ge(q, 16 * KT)

        @block.gpsimd
        def _(pool):
            def lo(d, i=None):
                pool.wait_ge(hi_done, d + 1 + (0 if i is None else RING * i))
                n = slab_size(d)
                nc.gpsimd.tensor_tensor(WL[:, d % WRING, 0:n], raw_of(d), WH[:, d % WRING, 0:n].bitcast(F32),
                                        ALU.subtract).then_inc(lo_done, 1)

            def add(st, h, m):
                pool.wait_ge(sq_done, SQ(st, h, m))
                src, dst = sq[:, SQ(st, h, m) % 2, :], gathered(st, h)
                if m == 0:
                    before = [k for k in SUMS[:SUMS.index((st, h))] if k[1] == h]
                    if before and st not in ("m0", "m1"):
                        pool.wait_ge(rstd_done, RSTD(*before[-1]))
                    nc.gpsimd.tensor_copy(dst, src).then_inc(acc_done, 1)
                else:
                    pool.wait_ge(acc_done, ACC(st, h, m - 1))
                    nc.gpsimd.tensor_tensor(dst, dst, src, ALU.add).then_inc(acc_done, 1)

            def scale(st, h, m, src):
                if m == 0:
                    pool.wait_ge(rstd_done, RSTD(NORM_OF.get(st, st), h))
                before = prev(SC, (st, h, m), 2)
                if before:
                    s, v = scaled_read(before)
                    pool.wait_ge(s, v)
                nc.gpsimd.tensor_tensor(scaled[:, SC(st, h, m) % 2, :], src, R2[:, h, :], ALU.mult).then_inc(sc_done, 1)

            nc.gpsimd.memset(ones[:], 1.0).then_inc(ones_set, 1)
            nc.gpsimd.memset(eps[:], EPS).then_inc(ones_set, 1)
            nc.gpsimd.memset(V[:, :, 0:CW - 1], 0.0).then_inc(ones_set, 1)
            for s, n in ((bank_free, BANKS), (v_done, 3), (u_lo, 2), (key_lo, 5), (score_mm, 1), (new_nat, 1),
                         (lat_out, 1)):
                pool.sem_inc(s, n)
            lo(0)
            for h in range(2):
                for m in range(KT):
                    add("x0", h, m)

            lo(1)

            def gated_rows(m):
                pool.wait_ge(gate_sig, 2 * m + 1)
                nc.gpsimd.tensor_tensor(V[:, m, CW - 1:CW - 1 + H], scaled[:, 0, :], prod[:, 0, :], ALU.mult)\
                    .then_inc(v_done, 1)
                pool.wait_ge(gate_sig, 2 * m + 2)
                nc.gpsimd.tensor_tensor(V[:, m, CW - 1 + H:VP], scaled[:, 1, 0:TP - H], prod[:, 1, 0:TP - H],
                                        ALU.mult).then_inc(v_done, 1)
                nc.gpsimd.tensor_tensor(
                    V[:, m, VP:VW].rearrange("p (s c) -> p s c", s=NS)[:, :, CW - 1:VSQ],
                    scaled[:, 1, TP - H:H].rearrange("p (s c) -> p s c", s=NS),
                    prod[:, 1, TP - H:H].rearrange("p (s c) -> p s c", s=NS), ALU.mult).then_inc(v_done, 1)

            gated_rows(0)
            lo(2)
            for m in range(KT):
                if m < KT - 1:
                    lo(m + 3)
                    gated_rows(m + 1)
                z = flat[GATHER[m % 2]]
                for n in range(1, CWP):
                    k = (CWP - 1) * m + n - 1
                    pool.wait_ge(prod_done, 2 * (CWP * m + n + 1))
                    if n > 1:
                        pool.wait_ge(z_step, k)
                    nc.gpsimd.tensor_tensor(z, z, flat[STAGES[k % 2]], ALU.add).then_inc(z_step, 1)
            for h in range(2):
                for m in range(KT):
                    scale("sw", h, m, half(Y, m, h))

            def lo_steps(phase):
                for j in range(SLABS[phase]):
                    lo(DENSE0[phase] + j + 1)

            def after_mixer(phase, st, done=0):
                for j in range(5):
                    if done <= j < 4:
                        lo(DENSE0[phase] + j + 1)
                    if j:
                        for h, m in PAIRS[4 * j - 4:4 * j]:
                            add(st, h, m)
                for h in range(2):
                    for m in range(KT):
                        scale(st, h, m, half(Y, m, h))
                for h in range(2):
                    pool.wait_ge(sc_done, SC(st, h, KT - 1))
                    nc.gpsimd.memset(Y[:, :, h * H:(h + 1) * H], 0.0).then_inc(y_zero, 1)
                    nc.gpsimd.memset(acc[:, h, :], 0.0).then_inc(acc_zero, 1)

            def mlp(layer):
                phase = f"mlp{layer}"
                d0, b0, stx = DENSE0[phase], UP * NCH * layer, f"x{2 * layer + 1}"
                pool.wait_ge(acc_zero, 2 * layer + 2)
                with pool.Fori(0, NCH) as i:
                    for j in range(4):
                        lo(d0 + j + 1, i)
                        if j == 3:
                            for h in range(2):
                                pool.wait_ge(sq_done, SQ(stx, h, 0) + 2 * i)
                                pool.wait_ge(acc_done, SQ(stx, h, 0) - 2 + 2 * i)
                                nc.gpsimd.tensor_tensor(acc[:, h, :], acc[:, h, :], sq[:, SQ(stx, h, 0) % 2, :], ALU.add)\
                                    .then_inc(acc_done, 1)
                        if j < 2:
                            for k in range(4):
                                n, h, m = 4 * j + k, k // 2, 2 * j + k % 2
                                pool.wait_ge(u_hi, b0 + n + 1 + UP * i)
                                nc.gpsimd.tensor_tensor(half(BL, m, h), prod[:, n % 2, :], half(BH, m, h).bitcast(F32),
                                                        ALU.subtract).then_inc(u_lo, 1)
                st = f"m{layer}"
                for h, m in tiles_of(st):
                    add(st, h, m)
                lo(DENSE0[f"ple{layer}"] + 1)
                for h in range(2):
                    for m in range(KT):
                        scale(st, h, m, half(Y, m, h))
                for j in range(4):
                    if DENSE0[f"gate{layer}"] + j + 1 < len(dense_slabs):
                        lo(DENSE0[f"gate{layer}"] + j + 1)

            after_mixer("pw2", "y0", 1)
            mlp(0)
            for h in range(2):
                for m in range(KT):
                    add("x2", h, m)
            lo_steps("dkv")
            lo(DENSE0["dq"] + 1)
            for h, m in tiles_of("ck"):
                add("ck", h, m)
            lo(DENSE0["dq"] + 2)
            for h in range(2):
                for m in range(4):
                    scale("ck", h, m, half(CK, m, h))
            for n, (h, m) in enumerate(tiles_of("cq")):
                if n == 4:
                    lo(DENSE0["dq"] + 3)
                add("cq", h, m)
            for h in range(2):
                for m in range(6):
                    scale("cq", h, m, half(Y, m, h))
            pool.wait_ge(ck_val, 8)
            nc.gpsimd.tensor_copy(CS[:, :, :], CK[:, :, TP:T]).then_inc(cs_done, 1)
            lo_steps("uq")
            lo_steps("kvh")
            lo_steps("uv")
            after_mixer("wo", "y1")
            mlp(1)

        @block.vector
        def _(dve):
            steps = [0]

            def link(ins):
                steps[0] += 1
                ins.then_inc(dve_step, 1)
                dve.wait_ge(dve_step, steps[0])

            def lo(v, h, m, src):
                dve.wait_ge(a_hi, A(v, h, m))
                g = gain_of[v]
                if g:
                    nc.vector.scalar_tensor_tensor(out=half(AL, m, h), in0=src, scalar=gain(g, m),
                                                   in1=half(AH, m, h).bitcast(F32), op0=ALU.mult, op1=ALU.subtract)\
                        .then_inc(a_lo, 1)
                else:
                    nc.vector.tensor_tensor(half(AL, m, h), src, half(AH, m, h).bitcast(F32), ALU.subtract)\
                        .then_inc(a_lo, 1)

            def row(st, h):
                dve.wait_ge(sum_done, SUM(st, h))
                f = R1[:, h, :]
                if st in ("m0", "m1"):
                    link(nc.vector.tensor_tensor(acc[:, h, :], f, f, ALU.mult))
                    f = acc[:, h, :]
                link(nc.vector.tensor_tensor(R2[:, h, :], f, f, ALU.mult))
                nc.vector.tensor_tensor(root[:, h, :], bank[4 + h][:, 0:H], R2[:, h, :], ALU.mult).then_inc(row_step, 1)

            def rstd(st, h):
                dve.wait_ge(root_done, ROOT(st, h))
                if st in SCALED_BY_INPUT:
                    link(nc.vector.reciprocal(root[:, h, :], root[:, h, :]))
                    f = acc[:, h, :] if st in ("m0", "m1") else R1[:, h, :]
                    nc.vector.tensor_tensor(R2[:, h, :], root[:, h, :], f, ALU.mult).then_inc(rstd_done, 1)
                else:
                    r = R1 if st[0] == "x" else R2
                    nc.vector.reciprocal(r[:, h, :], root[:, h, :]).then_inc(rstd_done, 1)

            def update(st, h, post, v):
                for m in range(KT + 1):
                    if m < KT:
                        dve.wait_ge(sc_done, SC(st, h, m))
                        nc.vector.scalar_tensor_tensor(out=half(X, m, h), in0=scaled[:, SC(st, h, m) % 2, :],
                                                       scalar=gain(post, m), in1=half(X, m, h), op0=ALU.mult,
                                                       op1=ALU.add).then_inc(x_done, 1)
                    if m:
                        lo(v, h, m - 1, half(X, m - 1, h))

            def evacuate(phase, dst, units, done=0):
                for n, (h, m) in list(enumerate(units))[done:]:
                    u = UNIT0[phase] + n
                    dve.wait_ge(unit_done, u + 1)
                    nc.vector.tensor_copy(dst(h, m), bank[u % BANKS][:, 0:H]).then_inc(bank_free, 1)

            pairs = PAIRS

            def turned_input(e):
                dve.wait_ge(turned, e + 1)
                src = bank[4 + e % 4]
                if e == 16:
                    nc.vector.tensor_copy(gains[:, :], src[:, 0:NG]).then_inc(unturned_v, 1)
                elif e < 16:
                    nc.vector.tensor_copy(X[:, e // 2, 0:TP], src[:, 0:TP]).then_inc(unturned_v, 1)
                else:
                    nc.vector.tensor_copy(V[:, e - 18, VP:VW].rearrange("p (s c) -> p s c", s=NS)[:, :, 0:CW - 1],
                                          src[:, 0:2 * SG].rearrange("p (s c) -> p s c", s=NS)).then_inc(unturned_v, 1)

            def scaled_rows(m, h):
                for t, buf in enumerate((scaled, prod)):
                    n = 2 * h + t
                    dve.wait_ge(unit_done, 4 * m + n + 1)
                    if t == 0:
                        dve.wait_ge(v_done, 3 * m + 1 + 2 * h)
                    nc.vector.tensor_tensor(buf[:, h, :], bank[n][:, 0:H], R1[:, h, :], ALU.mult).then_inc(bank_free, 1)

            def convolve(m, parity):
                vm, ym = V[:, bass.ds(m, 1), :], Y[:, bass.ds(m, 1), :]
                gm = gains[:, bass.ds(GCOL["dw_bias"] + m, 1)]
                wm = taps[:, bass.ds(m, 1), :]
                dve.wait_ge(v_done, 3 * m + 6)
                for c in range(CWV):
                    for part in range(2):
                        if part == 0:
                            dst, src = ym[:, 0, 0:TP], vm[:, 0, c:c + TP]
                        else:
                            dst = ym[:, 0, TP:T].rearrange("p (s t) -> p s t", s=NS)
                            src = vm[:, 0, VP:VW].rearrange("p (s c) -> p s c", s=NS)[:, :, c:c + TQ]
                        w = wm[:, 0, c:c + 1]
                        if c == 0:
                            nc.vector.tensor_scalar(dst, src, w, gm, ALU.mult, ALU.add).then_inc(conv_step, 1)
                        else:
                            dve.wait_ge(conv_step, 2 * c + part - 1 + 2 * CWV * m)
                            nc.vector.scalar_tensor_tensor(out=dst, in0=src, scalar=w, in1=dst, op0=ALU.mult,
                                                           op1=ALU.add).then_inc(conv_step, 1)
                dve.wait_ge(z_step, CWP - 1 + (CWP - 1) * m)
                dve.wait_ge(conv_step, 2 * CWV + 2 * CWV * m)
                nc.vector.tensor_tensor(ym[:, 0, :], ym[:, 0, :], flat[GATHER[parity]], ALU.add).then_inc(tile_done, 1)

            for e in range(0, 17, 2):
                turned_input(e)
            dve.wait_ge(unturned_v, 9)
            for m in range(KT):
                lo("x0", 0, m, half(X, m, 0))
            dve.wait_ge(unturned_a, 8)
            for m in range(KT):
                lo("x0", 1, m, half(X, m, 1))
            for h in range(2):
                rstd("x0", h)
                dve.wait_ge(rstd_done, RSTD("x0", h))
                scaled_rows(0, h)
            for e in range(18, 25, 2):
                turned_input(e)
            dve.wait_ge(unturned_v, 13)
            dve.wait_ge(unturned_a, 13)
            with dve.Fori(0, KT // 2 - 1) as i:
                for j in range(2):
                    for h in range(2):
                        scaled_rows(2 * i + j + 1, h)
                    convolve(2 * i + j, j)
            for h in range(2):
                scaled_rows(KT - 1, h)
            convolve(KT - 2, 0)
            convolve(KT - 1, 1)

            for h in range(2):
                dve.wait_ge(mean_done, KT * 2 - 1 + h)
                nc.vector.tensor_scalar(R2[:, h, :], bank[4 + h][:, 0:H], 1.0 / D, None, ALU.mult).then_inc(rstd_done, 1)
            for h in range(2):
                dve.wait_ge(rstd_done, RSTD("lm", h))
                for m in range(KT):
                    nc.vector.tensor_tensor(half(Y, m, h), half(Y, m, h), R2[:, h, :], ALU.subtract).then_inc(centred, 1)
            dve.wait_ge(centred, 16)
            for h in range(2):
                rstd("lv", h)
            for h in range(2):
                for m in range(KT + 1):
                    if m < KT:
                        n, k = KT * h + m, SC("sw", h, m) % 2
                        dve.wait_ge(sw_sig, n + 1)
                        nc.vector.tensor_scalar(scaled[:, k, :], scaled[:, k, :], gain("ln_g", m), gain("ln_b", m),
                                                ALU.mult, ALU.add).then_inc(sw_lin, 1)
                        dve.wait_ge(sw_lin, n + 1)
                        nc.vector.tensor_tensor(prod[:, n % 2, :], prod[:, n % 2, :], scaled[:, k, :], ALU.mult)\
                            .then_inc(sw_val, 1)
                    if m:
                        lo("sw", h, m - 1, prod[:, (n if m == KT else n - 1) % 2, :])

            def after_mixer(phase, st, post, v, stx):
                evacuate(phase, lambda h, m: half(Y, m, h), pairs)
                for h in range(2):
                    rstd(st, h)
                    update(st, h, post, v)

            def mlp(layer):
                phase, v = f"mlp{layer}", f"g{layer}"
                u0, b0 = UNIT0[phase], UP * NCH * layer
                dve.wait_ge(y_zero, 2 * layer + 2)
                with dve.Fori(0, NCH) as i:
                    for n in range(UP):
                        dve.wait_ge(relu_done, b0 + n + 1 + UP * i)
                        dve.wait_ge(u_lo, b0 + n + 1 + UP * i)
                        nc.vector.tensor_tensor(prod[:, n % 2, :], scaled[:, n % 2, :], bank[(u0 + n) % BANKS][:, 0:H],
                                                ALU.mult).then_inc(bank_free, 1)
                    for n in range(UP, CHUNK):
                        k = n - UP
                        h, m = (k % 8) // 4, 4 * (k // 8) + k % 4
                        dve.wait_ge(unit_done, u0 + n + 1 + CHUNK * i)
                        nc.vector.tensor_tensor(half(Y, m, h), half(Y, m, h), bank[(u0 + n) % BANKS][:, 0:H], ALU.add)\
                            .then_inc(bank_free, 1)
                for e in range(4):
                    kt, part = e // 2, e % 2
                    a, b = (0, TP) if part == 0 else (TP, T)
                    dve.wait_ge(p_hi, 4 * layer + e + 1)
                    nc.vector.tensor_tensor(BL[:, kt, a:b], bank[6 + part][:, 0:b - a], BH[:, kt, a:b].bitcast(F32),
                                            ALU.subtract).then_inc(p_lo, 1)
                for h in range(2):
                    rstd(f"x{2 * layer + 1}", h)
                st, tiles = f"m{layer}", [(h, m) for h in range(2) for m in range(KT)]
                evacuate(f"ple{layer}", lambda h, m: half(E, m, h), tiles[:KT])
                for h in range(2):
                    dve.wait_ge(rstd_done, RSTD(f"x{2 * layer + 1}", h))
                    row(st, h)
                rstd(st, 0)
                evacuate(f"ple{layer}", lambda h, m: half(E, m, h), tiles[:KT + 4], KT)
                update(st, 0, f"ff_post{layer}", v)
                rstd(st, 1)
                evacuate(f"ple{layer}", lambda h, m: half(E, m, h), tiles, KT + 4)
                update(st, 1, f"ff_post{layer}", v)
                ug = UNIT0[f"gate{layer}"]
                for n, (h, m) in enumerate(GATE_ORDER):
                    u = ug + n
                    dve.wait_ge(sig_done, 16 * layer + n + 1)
                    nc.vector.tensor_tensor(scaled[:, n % 2, :], prod[:, n % 2, :], half(E, m, h), ALU.mult)\
                        .then_inc(bank_free, 1)
                    dve.wait_ge(bank_free, freed(u))
                    nc.vector.tensor_tensor(half(X, m, h), half(X, m, h), scaled[:, n % 2, :], ALU.add)\
                        .then_inc(xg_done, 1)

            after_mixer("pw2", "y0", "mix_post0", "ff0", "x1")
            mlp(0)

            for h in range(2):
                for m in range(KT):
                    lo("kv", h, m, half(X, m, h))
            krow = [(h, 4) for h in range(2)]
            evacuate("dkv", lambda h, m: half(CK, m, h) if m < 4 else KR[:, h * H:(h + 1) * H], pairs[:8] + krow)
            for h in range(2):
                rstd("x2", h)
            dve.wait_ge(rstd_done, RSTD("x2", 1))
            r1 = R1[:, :, :].rearrange("p a b -> p (a b)")
            dve.wait_ge(bank_free, freed(UNIT0["dkv"] + 9))
            link(nc.vector.tensor_tensor(KR, KR, r1, ALU.mult))
            for h in range(2):
                for m in range(KT):
                    lo("mx", h, m, half(X, m, h))
            evacuate("dq", lambda h, m: half(Y, m, h), pairs[:4])
            for h in range(2):
                row("ck", h)
            for h in range(2):
                rstd("ck", h)
            evacuate("dq", lambda h, m: half(Y, m, h), pairs[:8], 4)
            for h in range(2):
                for m in range(4):
                    dve.wait_ge(sc_done, SC("ck", h, m))
                    nc.vector.tensor_scalar(half(CK, m, h), scaled[:, SC("ck", h, m) % 2, :], gain("kv_norm", m), None,
                                            ALU.mult).then_inc(ck_val, 1)
            for h in range(2):
                for m in range(4):
                    dve.wait_ge(b_hi, 4 * h + m + 1)
                    nc.vector.tensor_tensor(half(BL, m, h), half(CK, m, h), half(BH, m, h).bitcast(F32),
                                            ALU.subtract).then_inc(b_lo, 1)
            evacuate("dq", lambda h, m: half(Y, m, h), pairs[:12], 8)
            for h in range(2):
                row("cq", h)
            for h in range(2):
                rstd("cq", h)
            for h in range(2):
                for m in range(6):
                    lo("cq", h, m, scaled[:, SC("cq", h, m) % 2, :])

            def rotate(n, t):
                dve.wait_ge(rot_done, n + 1)
                for b, c0, c1 in ((6, 0, TP), (7, TP, T)):
                    nc.vector.tensor_tensor(flat["prod"][:, c0:c1], bank[b][:, 0:c1 - c0], SIN[:, c0:c1], ALU.mult)\
                        .then_inc(rope_step, 1)
                nc.vector.tensor_tensor(t, t, COS, ALU.mult).then_inc(rope_step, 1)
                dve.wait_ge(rope_step, 4 * n + 3)
                nc.vector.tensor_tensor(t, t, flat["prod"][:, 0:T], ALU.add).then_inc(rope_step, 1)
                dve.wait_ge(rope_step, 4 * n + 4)

            dve.wait_ge(rope_in, 16)
            rotate(0, KR)
            for n, (h, m) in enumerate(pairs + pairs[:8]):
                u = UNIT0["uq"] + n
                dve.wait_ge(unit_done, u + 1)
                dst = half(Y, m, h) if n < 16 else half(QR, m, h)
                nc.vector.tensor_copy(dst, bank[u % BANKS][:, 0:H]).then_inc(bank_free, 1)
            dve.wait_ge(bank_free, freed(UNIT0["uq"] + 23))
            for j in range(4):
                rotate(1 + j, QR[:, j, :])
            for e in range(2):
                for r in range(2):
                    nc.vector.tensor_copy(DUP[:, e, DR * r:DR * r + DR], ident[:, DR * e:DR * e + DR]).then_inc(dup_set, 1)
            dve.wait_ge(uk_mm, 1)
            nc.vector.tensor_copy(ukT, bank[3][:, 0:CL]).then_inc(uk_used, 1)
            dve.wait_ge(qrs_mm, 1)
            nc.vector.tensor_copy(QRS.rearrange("p (s h t) -> p h s t", s=NS, h=NH),
                                  bank[5][:, 0:512].rearrange("p (h s t) -> p h s t", s=NS, h=NH)).then_inc(qrs_c, 1)

            dve.wait_ge(consts, 48)
            dve.wait_ge(kv_out, 32 * 5)
            def head_values(hd):
                dve.wait_ge(v_mm, hd // 2 + 1)
                if hd:
                    dve.wait_ge(pv_mm, hd)
                for q in range(2):
                    nc.vector.tensor_copy(vn[:, 256 * q:256 * q + 256].rearrange("p (k v) -> p k v", k=2),
                                          bank[1 + q][:, 0:512].rearrange("p (k e v) -> p k e v", k=2, e=2)[:, :, hd % 2])\
                        .then_inc(v_used, 1)

            def head_uk(hd):
                dve.wait_ge(uk_mm, hd + 1)
                dve.wait_ge(ql_mm, hd)
                nc.vector.tensor_copy(ukT, bank[3][:, 0:CL]).then_inc(uk_used, 1)

            def head_latent(hd):
                dve.wait_ge(ql_mm, hd + 1)
                nc.vector.tensor_copy(QLAT.rearrange("p c (s h t) -> p c s h t", s=NS, h=NH)[:, :, :, hd, :],
                                      bank[3][:, 0:256].rearrange("p (c s t) -> p c s t", c=4, s=NS))\
                    .then_inc(ql_used, 1)

            def top(hd, qb):
                n, c = 4 * hd + qb, 4 * (qb % 2)
                b = bank[4 + n % 2]
                dve.wait_ge(s_mm, n + 1)
                nc.vector.tensor_tensor(b[:, qb * P:(qb + 1) * P], b[:, qb * P:(qb + 1) * P], cmask, ALU.add)\
                    .then_inc(s_masked, 1)
                dve.wait_ge(s_masked, n + 1)
                nc.vector.tensor_reduce(tiny[:, c:c + 1], b[:, 0:(qb + 1) * P], AX.X, ALU.max).then_inc(s_max, 1)
                dve.wait_ge(s_max, 2 * n + 1)
                nc.vector.tensor_scalar(tiny[:, c + 1:c + 2], tiny[:, c:c + 1], -SCALE, None, ALU.mult)\
                    .then_inc(s_max, 1)

            def norm(hd, qb):
                n, c = 4 * hd + qb, 4 * (qb % 2)
                dve.wait_ge(s_exp, n + 1)
                nc.vector.reciprocal(tiny[:, c + 3:c + 4], tiny[:, c + 2:c + 3]).then_inc(s_rec, 1)
                dve.wait_ge(s_rec, n + 1)
                w = (qb + 1) * P
                nc.vector.tensor_scalar(PB[n % 2][:, 0:w], PB[n % 2][:, 0:w], tiny[:, c + 3:c + 4], None,
                                        ALU.mult).then_inc(p_ready, 1)

            def head_out(hd):
                dve.wait_ge(a_hi, A("o", 0, hd))
                nc.vector.tensor_tensor(AL[:, hd, 0:TP], bank[7][:, 0:TP], AH[:, hd, 0:TP].bitcast(F32), ALU.subtract)\
                    .then_inc(a_lo, 1)

            head_latent(0)
            for hd in range(NH):
                top(hd, 0)
                head_values(hd)
                top(hd, 1)
                norm(hd, 0)
                norm(hd, 1)
                top(hd, 2)
                if hd < NH - 1:
                    head_uk(hd + 1)
                norm(hd, 2)
                if hd:
                    head_out(hd - 1)
                top(hd, 3)
                if hd < NH - 1:
                    head_latent(hd + 1)
                norm(hd, 3)
            head_out(NH - 1)

            dve.wait_ge(cs_done, 1)
            dve.wait_ge(ql_used, NH)

            def gather(i):
                dve.wait_ge(new_nat, i + 1)
                nc.vector.tensor_copy(NK, CS[:, :, bass.ds(TQ * i, TQ)]).then_inc(new_in, 1)
                nc.vector.tensor_copy(NKR, KR[0:DR, bass.ds(TP + TQ * i, TQ)]).then_inc(new_in, 1)
                nc.vector.tensor_copy(QS, QLAT[:, :, bass.ds(64 * i, 64)]).then_inc(new_in, 1)
                for r in range(2):
                    rows = slice(DR * r, DR * r + DR)
                    nc.vector.tensor_copy(QSR[rows, r, :], QRS[rows, bass.ds(64 * i, 64)]).then_inc(new_in, 1)

            def queries(i):
                dve.wait_ge(q_hi, 2 + 2 * i)
                nc.vector.tensor_tensor(AL[:, 0:4, TP:T], QS, AH[:, 0:4, TP:T].bitcast(F32), ALU.subtract)\
                    .then_inc(q_lo, 1)
                nc.vector.tensor_tensor(AL[:, 4:6, TP:T], QSR, AH[:, 4:6, TP:T].bitcast(F32), ALU.subtract)\
                    .then_inc(q_lo, 1)

            def key(c, n):
                dve.wait_ge(key_hi, c + 1 + 5 * n)
                dst, part, src = (BL[:, c, 0:TP], BH[:, c, 0:TP], bank[4 + c][:, 0:TP]) if c < 4 else \
                    (BL[:, :, TP:T], BH[:, :, TP:T], rope_bank)
                nc.vector.tensor_tensor(dst, src, part.bitcast(F32), ALU.subtract).then_inc(key_lo, 1)

            def step(ins):
                ins.then_inc(sm_step, 1)

            def new_top(i):
                dve.wait_ge(new_mm, 1 + i)
                step(nc.vector.tensor_tensor(SN, bank[3][0:64, 256:264], nmask, ALU.add))
                dve.wait_ge(sm_step, SM("mask") + NSM * i)
                step(nc.vector.tensor_reduce(col(TOP, 4), SN, AX.X, ALU.max))

            def keep(i):
                dve.wait_ge(out_mm, 1 + i)
                nc.vector.tensor_copy(QLAT[:, :, bass.ds(64 * i, 64)],
                                      bank[7][:, 0:256].rearrange("p (c q) -> p c q", c=4)).then_inc(lat_out, 1)

            def slab(j, i, first, last):
                if j == 3 and not last:
                    gather(i + 1)
                dve.wait_ge(score_mm, j + 2 + 4 * i)
                step(nc.vector.tensor_reduce(col(TOP, j), bank[0][0:64, :], AX.X, ALU.max))
                dve.wait_ge(sm_step, SM("top", j) + NSM * i)
                if j == 0:
                    step(nc.vector.tensor_scalar(col(NM, 0), col(TOP, 0), col(TOP, 4), -SCALE, ALU.max, ALU.mult))
                else:
                    step(nc.vector.tensor_scalar(col(NM, j), col(TOP, j), -SCALE, col(NM, j - 1), ALU.mult, ALU.min))
                if j == 1 and not first:
                    keep(i - 1)
                if not last:
                    for c in range(5):
                        key(c, j + 1 + 4 * i)
                    if j == 3:
                        queries(i + 1)
                dve.wait_ge(exp_done, 2 * j + 2 + 8 * i)
                if j == 0:
                    step(nc.vector.tensor_tensor(col(SUMQ, 0), col(PSUMS, 0), col(PSUMS, 4), ALU.add))
                else:
                    step(nc.vector.tensor_scalar(col(SUMQ, j), col(SUMQ, j - 1), col(ALPHA, j), col(PSUMS, j),
                                                 ALU.mult, ALU.add))

            def gain_output(j, i):
                dve.wait_ge(pe_read_raw, 5 + j + 4 * i)
                if j == 0:
                    nc.vector.tensor_copy(OUT, bank[2][0:64, :]).then_inc(out_done, 1)
                else:
                    dve.wait_ge(out_done, j + OUTS * i)
                    nc.vector.scalar_tensor_tensor(out=OUT, in0=OUT, scalar=col(ALPHA, j), in1=bank[2][0:64, :],
                                                   op0=ALU.mult, op1=ALU.add).then_inc(out_done, 1)

            def finish(i):
                gain_output(3, i)
                dve.wait_ge(out_done, 4 + OUTS * i)
                nc.vector.reciprocal(col(SUMQ, 4), col(SUMQ, 3)).then_inc(out_done, 1)
                dve.wait_ge(out_done, 5 + OUTS * i)
                nc.vector.tensor_scalar(OUTN, OUT, col(SUMQ, 4), None, ALU.mult).then_inc(out_done, 1)

            def sequence(i, first, last):
                for j in range(4):
                    slab(j, i, first, last and j == 3)
                    if j:
                        gain_output(j - 1, i)
                    elif not first:
                        finish(i - 1)
                if not last:
                    new_top(i + 1)

            nc.vector.memset(QSR, 0.0).then_inc(qsr_zero, 1)
            dve.wait_ge(qsr_zero, 1)
            gather(0)
            queries(0)
            for c in range(5):
                key(c, 0)
            new_top(0)
            sequence(0, True, False)
            with dve.Fori(1, NS - 1) as i:
                sequence(i, False, False)
            sequence(NS - 1, False, True)
            finish(NS - 1)
            keep(NS - 1)
            dve.wait_ge(b_hi, 9)
            nc.vector.tensor_tensor(BL[:, :, 0:TP], QLAT[:, :, :], BH[:, :, 0:TP].bitcast(F32), ALU.subtract)\
                .then_inc(b_lo, 1)
            for hd in range(NH):
                dve.wait_ge(a_hi, A("o", 1, hd))
                nc.vector.tensor_tensor(AL[:, hd, TP:T], bank[hd % 4][:, 0:TS], AH[:, hd, TP:T].bitcast(F32),
                                        ALU.subtract).then_inc(a_lo, 1)
            after_mixer("wo", "y1", "mix_post1", "ff1", "x3")
            mlp(1)
            for b, (t0, n) in enumerate(tokens):
                dve.wait_ge(y_turned, 2 * b + 2)
                if b >= 2:
                    dve.wait_ge(y_out[b % 2], 16 * (b // 2))
                nc.vector.tensor_copy(yflat[0:n, (b % 2) * D + 512:(b % 2) * D + D], bank[5 + 2 * (b % 2)][0:n, 0:512])\
                    .then_inc(y_copied_v, 1)

        @block.tensor
        def _(pe):
            def three(out, wsl, hl, first, last):
                (wh, wl), (xh, xl) = wsl, hl
                nc.tensor.matmul(out, wh, xh, start=first, stop=False)
                nc.tensor.matmul(out, wh, xl, start=False, stop=False)
                return nc.tensor.matmul(out, wl, xh, start=False, stop=last)

            def wslab(d, kt, n, k, c):
                a = k * n + c
                return WH[:, d % WRING, a:a + P], WL[:, d % WRING, a:a + P]

            def rows(src, k, h):
                return half(src[0], k, h), half(src[1], k, h)

            def slab_ready(d, i=None):
                pe.wait_ge(lo_done, d + 1 if i is None else d + 1 + RING * i)

            Asrc, Bsrc = (AH, AL), (BH, BL)

            def total(st, h):
                pe.wait_ge(acc_done, ACC(st, h, NT[st] - 1))
                before = [k for k in SUMS[:SUMS.index((st, h))] if k[1] == h]
                if before:
                    pe.wait_ge(rstd_done, RSTD(*before[-1]))
                nc.tensor.matmul(bank[4 + h][:, 0:H], ones[:, :], gathered(st, h), start=True, stop=True)\
                    .then_inc(sum_done, 1)

            def product(phase, kt, n, tiles, v, src=None, after=(), between=None):
                u = UNIT0[phase]
                for j in range(SLABS[phase]):
                    d = DENSE0[phase] + j
                    slab_ready(d)
                    w = n[j] if isinstance(n, tuple) else n
                    nt = w // P
                    for h in range(2):
                        for t in range(nt):
                            def ready(k, h=h):
                                if v and j == 0 and t == 0:
                                    pe.wait_ge(a_lo, A(v, h, k))
                            b = bank[u % BANKS][:, 0:H]
                            pe.wait_ge(bank_free, u + 1)
                            for k in range(kt):
                                ready(k)
                                ins = three(b, wslab(d, kt, w, k, t * P), rows(src or Asrc, k, h), k == 0,
                                            k == kt - 1)
                            ins.then_inc(unit_done, 1)
                            u += 1
                        if between and h == 0:
                            for g in range(2):
                                total(between, g)
                    if j == 0:
                        for st in after:
                            for h in range(2):
                                total(st, h)

            def total_direct(st, h):
                before = [k for k in SUMS[:SUMS.index((st, h))] if k[1] == h]
                pe.wait_ge(rstd_done, RSTD(*before[-1]))
                for m in range(NT[st]):
                    pe.wait_ge(sq_done, SQ(st, h, m))
                    nc.tensor.matmul(bank[4 + h][:, 0:H], ones[:, :], sq[:, SQ(st, h, m) % 2, :], start=m == 0,
                                     stop=m == NT[st] - 1).then_inc(acc_done, 1)

            def turn_input(e):
                if e >= 4:
                    pe.wait_ge(unturned_v if e % 2 == 0 else unturned_a, e // 2 - 1)
                dst = bank[4 + e % 4]
                if e == 16:
                    ins = nc.tensor.transpose(dst[:, 0:NG], flat["prod"][0:NG, 0:P], ident[0:NG, 0:NG])
                elif e < 16 and e % 2 == 0:
                    m = e // 2
                    for b in range(4):
                        ins = nc.tensor.transpose(dst[:, b * P:(b + 1) * P],
                                                  yflat[:, b * D + m * P:b * D + (m + 1) * P], ident[:, :])
                elif e < 17:
                    m = e // 2
                    ins = nc.tensor.transpose(dst[:, 0:TS], x_stage[0:TS, m * P:(m + 1) * P], ident[0:TS, 0:TS])
                elif e == 17:
                    for m in range(KT):
                        ins = nc.tensor.transpose(dst[:, m * CW:(m + 1) * CW], taps_stage[0:CW, m * P:(m + 1) * P],
                                                  ident[0:CW, 0:CW])
                else:
                    m = e - 18
                    for g in range(2):
                        ins = nc.tensor.transpose(dst[:, g * SG:(g + 1) * SG], state_stage[0:SG, g, m * P:(m + 1) * P],
                                                  ident[0:SG, 0:SG])
                ins.then_inc(turned, 1)

            def pw1_units(m, parity, h):
                pe.wait_ge(lo_done, 1 + m)
                for t in range(2):
                    u = 2 * h + t
                    pe.wait_ge(bank_free, u + 1 + 4 * m)
                    for k in range(KT):
                        if type(m) is int and m == 0 and t == 0:
                            pe.wait_ge(a_lo, A("x0", h, k))
                        ins = three(bank[u][:, 0:H], wslab(parity, KT, 256, k, t * P), rows(Asrc, k, h), k == 0,
                                    k == KT - 1)
                    ins.then_inc(unit_done, 1)

            def turn_state(m):
                pe.wait_ge(state_gathered, m + 1)
                if m >= 2:
                    pe.wait_ge(state_copied, 2 * m - 2)
                dst = bank[6 + m % 2]
                for g in range(2):
                    nc.tensor.transpose(dst[0:SG, g * P:(g + 1) * P], state_in[:, m % 2, g * SG:(g + 1) * SG],
                                        ident[:, :])
                nc.tensor.transpose(dst[0:CW - 1, 2 * P:3 * P], V[:, m, TP:VP], ident[:, :]).then_inc(state_turned, 1)

            def mean(m):
                pe.wait_ge(tile_done, m + 1)
                for h in range(2):
                    nc.tensor.matmul(bank[4 + h][:, 0:H], ones[:, :], half(Y, m, h), start=m == 0,
                                     stop=m == KT - 1).then_inc(mean_done, 1)

            pe.wait_ge(consts, 16)
            pe.wait_ge(x_first, 80)
            for e in range(17):
                if e == 16:
                    pe.wait_ge(vecs, 16 * len(GAINS))
                if e == 8:
                    pe.wait_ge(x_in, 64)
                turn_input(e)
            pe.wait_ge(ones_set, 3)
            for h in range(2):
                pw1_units(0, 0, h)
                total("x0", h)
            pe.wait_ge(root_done, ROOT("x0", 1))
            pe.wait_ge(stage_in, 48)
            for e in range(17, 26):
                turn_input(e)
            with pe.Fori(0, KT // 2 - 1) as i:
                for j in range(2):
                    for h in range(2):
                        pw1_units(2 * i + j + 1, (j + 1) % 2, h)
            for h in range(2):
                pw1_units(KT - 1, (KT - 1) % 2, h)
            pe.wait_ge(unturned_a, 13)
            pe.wait_ge(unturned_v, 13)
            for m in range(4):
                turn_state(m)
            for m in range(KT - 2):
                mean(m)
            for m in range(4, KT):
                turn_state(m)
            for m in range(KT - 2, KT):
                mean(m)
            for h in range(2):
                total_direct("lv", h)
            product("pw2", KT, 256, 2, "sw")
            for h in range(2):
                total("y0", h)

            def mlp(layer):
                phase = f"mlp{layer}"
                d0, u0, b0 = DENSE0[phase], UNIT0[phase], UP * NCH * layer
                with pe.Fori(0, NCH) as i:
                    n = 0
                    for j in range(4):
                        slab_ready(d0 + j, i)
                        for h in range(2):
                            for t in range(2 if j < 2 else 4):
                                pe.wait_ge(bank_free, u0 + n + 1 + CHUNK * i)
                                dst = bank[(u0 + n) % BANKS][:, 0:H]
                                for k in range(KT if j < 2 else FC):
                                    if j == 0 and t == 0:
                                        pe.wait_ge(a_lo, A(f"ff{layer}", h, k))
                                    if j == 2 and t == 0:
                                        pe.wait_ge(u_lo, b0 + up_n(h, k) + 3 + UP * i)
                                    if j < 2:
                                        ins = three(dst, wslab(d0 + j, KT, 256, k, t * P), rows(Asrc, k, h), k == 0,
                                                    k == KT - 1)
                                    else:
                                        ins = three(dst, wslab(d0 + j, FC, 512, k, t * P), rows(Bsrc, k, h), k == 0,
                                                    k == FC - 1)
                                ins.then_inc(unit_done, 1)
                                n += 1
                for h in range(2):
                    total(f"x{2 * layer + 1}", h)
                pe.wait_ge(p_in, 80 * (layer + 1))
                for e in range(4):
                    kt, part = e // 2, e % 2
                    if e >= 2:
                        pe.wait_ge(p_lo, 4 * layer + e - 1)
                    if part == 0:
                        for b in range(4):
                            ins = nc.tensor.transpose(bank[6][:, b * P:(b + 1) * P], p_stage[:, b, kt * P:(kt + 1) * P],
                                                      ident[:, :])
                    else:
                        ins = nc.tensor.transpose(bank[7][:, 0:TS], p_stage[0:TS, 4, kt * P:(kt + 1) * P],
                                                  ident[0:TS, 0:TS])
                    ins.then_inc(p_turned, 1)
                pe.wait_ge(p_lo, 4 * layer + 4)
                product(f"ple{layer}", 2, D, 8, None, src=Bsrc, between=f"m{layer}")
                product(f"gate{layer}", KT, 256, 2, f"g{layer}")

            mlp(0)
            product("dkv", KT, (256, 256, 128), 2, "kv")
            for h in range(2):
                total("x2", h)
            product("dq", KT, 256, 2, "mx", after=("ck",))
            for h in range(2):
                total("cq", h)

            def rot(n, t):
                if n:
                    pe.wait_ge(rope_step, 4 * n)
                nc.tensor.matmul(bank[6][:, 0:TP], ROT, t[:, 0:TP], start=True, stop=True)
                nc.tensor.matmul(bank[7][:, 0:TS], ROT, t[:, TP:T], start=True, stop=True).then_inc(rot_done, 1)

            pe.wait_ge(rope_in, 16)
            pe.wait_ge(dve_step, KR_STEP)
            rot(0, KR)
            u = UNIT0["uq"]
            for j in range(6):
                d = DENSE0["uq"] + j
                slab_ready(d)
                for h in range(2):
                    for t in range(2):
                        pe.wait_ge(bank_free, u + 1)
                        for k in range(6):
                            if j == 0 and t == 0:
                                pe.wait_ge(a_lo, A("cq", h, k))
                            ins = three(bank[u % BANKS][:, 0:H], wslab(d, 6, 256, k, t * P), rows(Asrc, k, h), k == 0,
                                        k == 5)
                        ins.then_inc(unit_done, 1)
                        u += 1
                if j < 5:
                    t0, n = tokens[j]
                    pe.wait_ge(rope_step, 4)
                    pe.wait_ge(rstd_done, RSTD("cq", 1))
                    if j:
                        pe.wait_ge(kv_staged, 2 * j)
                    for c in range(4):
                        nc.tensor.transpose(bank[4][0:n, c * P:(c + 1) * P], CK[:, c, t0:t0 + n], ident[:, :])
                    nc.tensor.transpose(bank[5][0:n, 0:DR], KR[0:DR, t0:t0 + n], ident[0:DR, 0:DR])\
                        .then_inc(kv_turned, 1)
            pe.wait_ge(bank_free, freed(u - 1))
            def head_slab(hd):
                return (DENSE0["kvh"] + hd // 2) % WRING, RAW[:, (RAW0["kvh"] + hd // 2) % RING]

            def head_keys(hd):
                w = head_slab(hd)[0]
                slab_ready(DENSE0["kvh"] + hd // 2)
                if hd:
                    pe.wait_ge(kvt_used, hd)
                for k in range(4):
                    a = k * 256 + hd % 2 * P
                    ins = three(bank[0][:, 0:TP], (WH[:, w, a:a + P], WL[:, w, a:a + P]),
                                (BH[:, k, 0:TP], BL[:, k, 0:TP]), k == 0, k == 3)
                ins.then_inc(kvt_done, 1)

            def pair_values(hd, q):
                w = head_slab(hd)[0]
                if hd and q == 0:
                    pe.wait_ge(v_used, 2 * hd)
                for kb in (2 * q, 2 * q + 1):
                    for k in range(4):
                        a = 1024 + k * 256
                        ins = three(bank[1 + q][:, (kb % 2) * 256:(kb % 2) * 256 + 256],
                                    (BH[:, k, kb * P:(kb + 1) * P], BL[:, k, kb * P:(kb + 1) * P]),
                                    (WH[:, w, a:a + 256], WL[:, w, a:a + 256]), k == 0, k == 3)
                if q == 1:
                    ins.then_inc(v_mm, 1)

            def head_uk(hd):
                raw = head_slab(hd)[1]
                if hd:
                    pe.wait_ge(ql_used, hd)
                for k in range(4):
                    a = k * 256 + hd % 2 * P
                    ins = nc.tensor.transpose(bank[3][:, k * P:(k + 1) * P], raw[:, a:a + P], ident[:, :])
                ins.then_inc(uk_mm, 1)

            def head_latent(hd):
                pe.wait_ge(uk_used, hd + 1)
                if hd % 2:
                    pe.sem_inc(pe_read_raw, 1)
                for c in range(4):
                    ins = nc.tensor.matmul(bank[3][:, c * TS:(c + 1) * TS], ukT[:, c * P:(c + 1) * P], Y[:, hd, TP:T],
                                           start=True, stop=True)
                ins.then_inc(ql_mm, 1)

            def head_scores(hd, qb):
                n, w = 4 * hd + qb, (qb + 1) * P
                if qb == 0:
                    pe.wait_ge(kvt_used, hd + 1)
                if n >= 2:
                    pe.wait_ge(s_exp, n - 1)
                r0 = DR * (hd % 2)
                q = slice(qb * P, (qb + 1) * P)
                dst = bank[4 + n % 2][:, 0:w]
                nc.tensor.matmul(dst, Y[:, hd, q], kT[:, 0:w], start=True, stop=False)
                nc.tensor.matmul(dst, QR[r0:r0 + DR, hd // 2, q], KR[r0:r0 + DR, 0:w], start=False, stop=True)\
                    .then_inc(s_mm, 1)

            def head_turn(hd, qb):
                n = 4 * hd + qb
                pe.wait_ge(p_ready, n + 1)
                if n:
                    pe.wait_ge(pt_used, n)
                for k in range(qb + 1):
                    ins = nc.tensor.transpose(bank[6][:, k * P:(k + 1) * P], PB[n % 2][:, k * P:(k + 1) * P],
                                              ident[:, :])
                ins.then_inc(pt_mm, 1)

            def head_out(hd):
                pe.wait_ge(pt_used, 4 * hd + 4)
                pe.wait_ge(v_used, 2 * hd + 2)
                if hd:
                    pe.wait_ge(a_lo, A("o", 0, hd - 1))
                for k in range(4):
                    ins = nc.tensor.matmul(bank[7][:, k * P:TP], vn[:, k * P:(k + 1) * P], PT[:, k, k * P:TP],
                                           start=k == 0, stop=k == 3)
                ins.then_inc(pv_mm, 1)

            rot(1, QR[:, 0, :])
            head_keys(0)
            rot(2, QR[:, 1, :])
            head_uk(0)
            pair_values(0, 0)
            rot(3, QR[:, 2, :])
            pair_values(0, 1)
            rot(4, QR[:, 3, :])
            pe.wait_ge(rope_step, 20)
            pe.wait_ge(kv_staged, 10)
            pe.wait_ge(dup_set, 4)
            for h in range(NH):
                e = h % 2
                ins = nc.tensor.matmul(bank[5][:, h * TS:(h + 1) * TS], DUP[:, e, :],
                                       QR[:, h // 2, TP:T], start=True, stop=True)
            ins.then_inc(qrs_mm, 1)
            head_latent(0)
            pe.wait_ge(qrs_c, 1)
            for hd in range(NH):
                more, pair = hd < NH - 1, hd % 2 == 1 and hd < NH - 1
                head_scores(hd, 0)
                if hd:
                    head_turn(hd - 1, 3)
                head_scores(hd, 1)
                if hd:
                    head_out(hd - 1)
                if more:
                    head_keys(hd + 1)
                head_turn(hd, 0)
                head_scores(hd, 2)
                if more:
                    head_uk(hd + 1)
                head_turn(hd, 1)
                if pair:
                    pair_values(hd + 1, 0)
                head_scores(hd, 3)
                if more:
                    head_latent(hd + 1)
                if pair:
                    pair_values(hd + 1, 1)
                head_turn(hd, 2)
            head_turn(NH - 1, 3)
            head_out(NH - 1)

            pe.wait_ge(a_lo, A("o", 0, NH - 1))
            pe.wait_ge(ql_used, NH)
            g0 = RAW0["cache"]

            def page_slab(j, c):
                src = RAW[:, (g0 + j) % RING]
                if c < 4:
                    for q in range(4):
                        ins = nc.tensor.transpose(bank[4 + c][:, q * P:(q + 1) * P],
                                                  src[:, q * CL + c * P:q * CL + (c + 1) * P], ident[:, :])
                else:
                    for q in range(2):
                        a = 4 * CL + q * P
                        ins = nc.tensor.transpose(bank[3][:, q * P:(q + 1) * P], src[:, a:a + P], ident[:, :])
                ins.then_inc(page_mm, 1)

            def keys(j, i, cs):
                if 0 in cs:
                    pe.wait_ge(landed[(g0 + j) % RING], LANDED[g0 + j] + 128 * i)
                for c in cs:
                    pe.wait_ge(key_lo, c + 1 + 5 * j + 20 * i)
                    if j == 1 and c == 4:
                        pe.wait_ge(sm_step, SM("mask") + NSM * i)
                    if j == 2 and c == 3:
                        pe.wait_ge(lat_out, 1 + i)
                    if j == 1 and c == 0:
                        pe.wait_ge(new_nat_c, 1 + i)
                    page_slab(j, c)

            def new_keys(i):
                pe.wait_ge(new_in, 5 + 5 * i)
                pe.wait_ge(key_lo, 10 + 20 * i)
                dst = bank[3][0:64, 256:264]
                for c in range(4):
                    nc.tensor.matmul(dst, QS[:, c, :], NK[:, c, :], start=c == 0, stop=False)
                nc.tensor.matmul(dst, QSR[0:DR, 0, :], NKR, start=False, stop=True).then_inc(new_mm, 1)
                for c in range(4):
                    ins = nc.tensor.transpose(bank[4][0:TQ, c * P:(c + 1) * P], NK[:, c, :], ident[:, :])
                ins.then_inc(new_nat, 1)

            def scores(j, i):
                pe.wait_ge(key_lo, 10 + 5 * j + 20 * i)
                if j == 0:
                    pe.wait_ge(q_lo, 2 + 2 * i)
                for c in range(4):
                    three(bank[0][0:64, 0:512], (AH[:, c, TP:T], AL[:, c, TP:T]), (BH[:, c, 0:TP], BL[:, c, 0:TP]),
                          c == 0, False)
                for r in range(2):
                    ins = three(bank[0][0:64, 256 * r:256 * r + 256].rearrange("p (a b) -> p a b", a=4),
                                (AH[:, 4 + r, TP:T], AL[:, 4 + r, TP:T]), (BH[:, :, TP:T], BL[:, :, TP:T]),
                                False, r == 1)
                ins.then_inc(score_mm, 1)

            def turn(j, i):
                pe.wait_ge(exp_done, (2 if j == 0 else 2 * j + 1) + 8 * i)
                pe.sem_inc(seen, 1)
                for k in range(4):
                    ins = nc.tensor.transpose(bank[1][:, k * 64:(k + 1) * 64], SP[:, k * P:(k + 1) * P],
                                              ident[0:64, 0:64])
                if j == 0:
                    ins = nc.tensor.transpose(bank[1][0:TQ, 256:320], PN, ident[0:64, 0:64])
                ins.then_inc(spt_mm, 1)

            def values(j, i):
                pe.wait_ge(spt_c, (j + 2 if j else 2) + 5 * i)
                dst = bank[2][0:64, 0:512]
                if j == 0:
                    pe.wait_ge(new_nat_c, 1 + i)
                    nc.tensor.matmul(dst, NPT, NEWC, start=True, stop=False)
                else:
                    pe.wait_ge(out_done, j + OUTS * i)
                src = RAW[:, (g0 + j) % RING]
                for k in range(4):
                    ins = nc.tensor.matmul(dst, SPT[:, k, :], src[:, k * CL:(k + 1) * CL], start=j > 0 and k == 0,
                                           stop=k == 3)
                ins.then_inc(pe_read_raw, 1)

            def give(i):
                pe.wait_ge(out_done, OUTS + OUTS * i)
                pe.sem_inc(seen, 1)
                for c in range(4):
                    ins = nc.tensor.transpose(bank[7][:, c * 64:(c + 1) * 64], OUTN[:, c * P:(c + 1) * P],
                                              ident[0:64, 0:64])
                ins.then_inc(out_mm, 1)

            def sequence(i, first, last):
                for j in range(4):
                    scores(j, i)
                    if j == 1 and not first:
                        give(i - 1)
                    if not (last and j == 3):
                        keys(*((j + 1, i) if j < 3 else (0, i + 1)), range(5))
                    if j:
                        values(j - 1, i)
                    elif not first:
                        values(3, i - 1)
                    turn(j, i)
                if not last:
                    new_keys(i + 1)

            keys(0, 0, range(5))
            new_keys(0)
            sequence(0, True, False)
            with pe.Fori(1, NS - 1) as i:
                sequence(i, False, False)
            sequence(NS - 1, False, True)
            values(3, NS - 1)
            give(NS - 1)
            pe.wait_ge(b_lo, 9)
            for hd in range(NH):
                d = DENSE0["uv"] + hd // 4
                if hd % 4 == 0:
                    slab_ready(d)
                if hd >= 4:
                    pe.wait_ge(a_lo, A("o", 1, hd - 4))
                for k in range(4):
                    a = k * 512 + (hd % 4) * P
                    rhs = [t[:, k, 0:TP].rearrange("p (s h t) -> p s h t", s=NS, h=NH)[:, :, hd, :] for t in (BH, BL)]
                    ins = three(bank[hd % 4][:, 0:TS].rearrange("p (s t) -> p s t", s=NS),
                                (WH[:, d % WRING, a:a + P], WL[:, d % WRING, a:a + P]), rhs, k == 0, k == 3)
                ins.then_inc(uv_mm, 1)
            pe.wait_ge(a_lo, A("o", 1, NH - 1))
            product("wo", KT, 256, 2, None)
            for h in range(2):
                total("y1", h)
            mlp(1)
            pe.wait_ge(xg_done, 32)
            for b, (t0, n) in enumerate(tokens):
                for q in range(2):
                    if b >= 2:
                        pe.wait_ge(y_copied_v if q else y_copied_a, b - 1)
                    for m in range(4):
                        ins = nc.tensor.transpose(bank[4 + 2 * (b % 2) + q][0:n, m * P:(m + 1) * P],
                                                  X[:, 4 * q + m, t0:t0 + n], ident[:, :])
                    ins.then_inc(y_turned, 1)


_INS = ["x_prompt", "x_sample", "state_conv", "cache_kv_latent", "cache_k_rope", "page_table", "p_prompt", "p_sample",
        "norm_mix_pre", "norm_mix_post", "norm_ff_pre", "norm_ff_post", "conv_pw1", "conv_dw", "conv_dw_bias",
        "conv_ln_g", "conv_ln_b", "conv_pw2", "kv_in_norm", "w_dkv", "kv_norm", "w_uk", "w_uv", "w_dq", "q_norm",
        "w_uq", "w_o", "w_up", "w_down", "ple_proj", "ple_gate"]
_OUTS = [("y_prompt", (1, TP, D)), ("y_sample", (NS, TQ, D)), ("new_conv_prompt", (1, 1, CW - 1, D)),
         ("new_conv_sample", (1, NS, CW - 1, D)), ("new_kv_prompt", (1, TP, CL)), ("new_kr_prompt", (1, TP, DR)),
         ("new_kv_sample", (NS, TQ, CL)), ("new_kr_sample", (NS, TQ, DR))]


def shape_constants():
    c = np.zeros((P, 1600), np.float32)
    c[:, 0:P] = np.eye(P)
    c[:, P:2 * P] = np.where(np.arange(P)[None, :] <= np.arange(P)[:, None], 0.0, NEG)
    new = np.where(np.arange(TQ)[None, :] <= np.arange(TQ)[:, None], 0.0, NEG)
    c[0:64, 256:264] = np.tile(new, (NH, 1))
    hd = DR // 2
    freqs = (np.float32(1.0) / np.float32(10000.0) ** (np.arange(hd, dtype=np.float32) / np.float32(hd)))
    pos = np.concatenate([np.arange(TP), np.tile(PAGES * PAGE + np.arange(TQ), NS)]).astype(np.float32)
    ang = (pos[None, :] * freqs.astype(np.float32)[:, None]).astype(np.float32)
    c[:, 320:320 + T] = np.tile(np.cos(ang), (P // hd, 1))
    c[:, 896:896 + T] = np.tile(np.sin(ang), (P // hd, 1))
    for g in range(2):
        for r in range(hd):
            c[g * DR + hd + r, 1472 + g * DR + r] = -1.0
            c[g * DR + r, 1472 + g * DR + hd + r] = 1.0
    return c


def kernel(**inputs):
    import concourse.bacc as _bacc
    from concourse.bass_utils import run_bass_kernel_spmd as _run

    nc = _bacc.Bacc("TRN2", target_bir_lowering=False, num_devices=1)
    arrays, io = {}, {}
    for name in _INS:
        a = np.ascontiguousarray(inputs[name])
        arrays[f"in_{name}"] = a
        io[name] = nc.dram_tensor(f"in_{name}", a.shape, mybir.dt.from_np(a.dtype), kind="ExternalInput").ap()
    arrays["in_consts"] = shape_constants()
    io["consts"] = nc.dram_tensor("in_consts", (P, 1600), F32, kind="ExternalInput").ap()
    for name, shape in _OUTS:
        io[name] = nc.dram_tensor(f"out_{name}", shape, F32, kind="ExternalOutput").ap()
    decoder_step(nc, io)
    r = _run(nc, [arrays], core_ids=[0])
    return tuple(r.results[0][f"out_{name}"] for name, _ in _OUTS)
```
